# Optimizing a Trainium2 kernel written in Bass

```python
import math
import jax
import jax.numpy as jnp
from jax import lax
import numpy as np

D_MODEL = 2048
BATCH = 1
SEQ = 256
DEPTH = 1
DEC_BATCH = 1
DEC_SEQ = 64
PAST_LEN = 128

CHUNK = 64
Q_BLOCK = 128
D_FF = 5632
SSM_WIDTH = D_MODEL // 2
SSM_GROUP = 16
SSM_GROUPS = SSM_WIDTH // SSM_GROUP
SSM_STATE = 64
MLA_HEADS = 16
QK_NOPE = 128
QK_ROPE = 64
V_DIM = 128
Q_LORA = 768
KV_LORA = 512
ROPE_THETA = 10000.0
MEM_TOKENS = 256
MEM_HEADS = 4
MEM_HEAD_DIM = 128
MEM_WIDTH = MEM_HEADS * MEM_HEAD_DIM
N_BRANCHES = 3
IN_SPLITS = (SSM_WIDTH,
             SSM_WIDTH + Q_LORA,
             SSM_WIDTH + Q_LORA + KV_LORA,
             SSM_WIDTH + Q_LORA + KV_LORA + QK_ROPE,
             SSM_WIDTH + Q_LORA + KV_LORA + QK_ROPE + MEM_WIDTH)
IN_COLS = IN_SPLITS[-1] + N_BRANCHES * D_MODEL
RMS_EPS = 1e-6
NEG_INF = -1e30
MLA_SCALE = (QK_NOPE + QK_ROPE) ** -0.5
MEM_SCALE = MEM_HEAD_DIM ** -0.5

kernel_name = "chunk_causal_s5_mla_memory_hybrid_step"

def _rmsnorm(x, g):
    x32 = x.astype(jnp.float32)
    y = x32 * lax.rsqrt(jnp.mean(x32 * x32, axis=-1, keepdims=True) + RMS_EPS)
    return (y * g.astype(jnp.float32)).astype(x.dtype)

def _swiglu(h, w_gate, w_up, w_down):
    return (jax.nn.silu(h @ w_gate) * (h @ w_up)) @ w_down

def _rope(t, pos):
    half = QK_ROPE // 2
    inv_freq = ROPE_THETA ** (-jnp.arange(half, dtype=jnp.float32) / half)
    ang = pos.astype(jnp.float32)[:, None] * inv_freq[None, :]
    cos = jnp.cos(ang)[:, None, :]
    sin = jnp.sin(ang)[:, None, :]
    t32 = t.astype(jnp.float32)
    t1, t2 = t32[..., :half], t32[..., half:]
    return jnp.concatenate([t1 * cos - t2 * sin, t2 * cos + t1 * sin], axis=-1).astype(t.dtype)

def _mla_attend(q_nope, q_rope, q_pos, k_nope, k_rope, v, k_pos):
    s = (jnp.einsum("bqhd,bkhd->bhqk", q_nope, k_nope)
         + jnp.einsum("bqhr,bkr->bhqk", q_rope, k_rope)).astype(jnp.float32) * MLA_SCALE
    visible = (k_pos[None, :] // CHUNK) <= (q_pos[:, None] // CHUNK)
    s = jnp.where(visible[None, None], s, NEG_INF)
    p = jax.nn.softmax(s, axis=-1).astype(v.dtype)
    return jnp.einsum("bhqk,bkhd->bqhd", p, v)

def _mla_attend_blocked(q_nope, q_rope, q_pos, k_nope, k_rope, v, k_pos):
    bsz, seqlen = q_nope.shape[:2]
    n_blk = seqlen // Q_BLOCK

    def blocks(t):
        return jnp.moveaxis(t.reshape((bsz, n_blk, Q_BLOCK) + t.shape[2:]), 1, 0)

    def one_block(args):
        qn, qr, qp = args
        return _mla_attend(qn, qr, qp, k_nope, k_rope, v, k_pos)

    out = lax.map(one_block, (blocks(q_nope), blocks(q_rope), q_pos.reshape(n_blk, Q_BLOCK)))
    return jnp.moveaxis(out, 0, 1).reshape((bsz, seqlen) + out.shape[3:])

def _s5(u, h0_re, h0_im, a_re, a_im, log_dt, b_re, b_im, c_re, c_im, d):
    f32 = jnp.float32
    u32 = u.astype(f32)
    a_re, a_im = a_re.astype(f32), a_im.astype(f32)
    dt = jnp.exp(log_dt.astype(f32))[:, None]
    mag = jnp.exp(a_re * dt)
    phase = a_im * dt
    lb_re, lb_im = mag * jnp.cos(phase), mag * jnp.sin(phase)
    den = a_re * a_re + a_im * a_im
    nr, ni = lb_re - 1.0, lb_im
    z_re = (nr * a_re + ni * a_im) / den
    z_im = (ni * a_re - nr * a_im) / den
    b_re, b_im = b_re.astype(f32), b_im.astype(f32)
    bb_re = z_re[..., None] * b_re - z_im[..., None] * b_im
    bb_im = z_re[..., None] * b_im + z_im[..., None] * b_re
    bu_re = jnp.einsum("blgh,gph->blgp", u32, bb_re)
    bu_im = jnp.einsum("blgh,gph->blgp", u32, bb_im)
    if h0_re is not None:
        h0_re, h0_im = h0_re.astype(f32), h0_im.astype(f32)
        bu_re = bu_re.at[:, 0].add(lb_re * h0_re - lb_im * h0_im)
        bu_im = bu_im.at[:, 0].add(lb_re * h0_im + lb_im * h0_re)
    seqlen = u.shape[1]
    A_re = jnp.broadcast_to(lb_re, (1, seqlen) + lb_re.shape)
    A_im = jnp.broadcast_to(lb_im, (1, seqlen) + lb_im.shape)

    def combine(e1, e2):
        ar1, ai1, br1, bi1 = e1
        ar2, ai2, br2, bi2 = e2
        return (ar1 * ar2 - ai1 * ai2,
                ar1 * ai2 + ai1 * ar2,
                ar2 * br1 - ai2 * bi1 + br2,
                ar2 * bi1 + ai2 * br1 + bi2)

    _, _, x_re, x_im = lax.associative_scan(combine, (A_re, A_im, bu_re, bu_im), axis=1)
    y = (jnp.einsum("blgp,ghp->blgh", x_re, c_re.astype(f32))
         - jnp.einsum("blgp,ghp->blgh", x_im, c_im.astype(f32))
         + d.astype(f32) * u32)
    return y, x_re[:, -1], x_im[:, -1]

def _mem_kv(mem, g, w_k, w_v):
    bsz, n_mem, _ = mem.shape
    mn = _rmsnorm(mem, g)
    k = (mn @ w_k).reshape(bsz, n_mem, MEM_HEADS, MEM_HEAD_DIM)
    v = (mn @ w_v).reshape(bsz, n_mem, MEM_HEADS, MEM_HEAD_DIM)
    return k, v

def _mem_attend(q, k, v):
    s = jnp.einsum("bqhd,bkhd->bhqk", q, k.astype(q.dtype)).astype(jnp.float32) * MEM_SCALE
    p = jax.nn.softmax(s, axis=-1).astype(q.dtype)
    return jnp.einsum("bhqk,bkhd->bqhd", p, v.astype(q.dtype))

def _layer(x, pos, mem_k, mem_v, lat_past, kr_past, h0_re, h0_im, p, blocked):
    bsz, seqlen, _ = x.shape
    x = x + 0.5 * _swiglu(_rmsnorm(x, p["ffn1_norm"]), p["ffn1_w_gate"], p["ffn1_w_up"], p["ffn1_w_down"])
    h = _rmsnorm(x, p["mix_norm"])
    z = h @ p["w_in"]
    u_ssm, c_q, c_kv, k_r, q_mem, gate_pre = jnp.split(z, IN_SPLITS, axis=-1)

    y_ssm, h_re, h_im = _s5(u_ssm.reshape(bsz, seqlen, SSM_GROUPS, SSM_GROUP), h0_re, h0_im,
                            p["ssm_a_re"], p["ssm_a_im"], p["ssm_log_dt"], p["ssm_b_re"], p["ssm_b_im"],
                            p["ssm_c_re"], p["ssm_c_im"], p["ssm_d"])
    y_ssm = jax.nn.gelu(y_ssm.reshape(bsz, seqlen, SSM_WIDTH).astype(x.dtype))
    y_ssm = y_ssm * jax.nn.sigmoid(y_ssm @ p["ssm_w_glu"] + p["ssm_b_glu"])

    q = (_rmsnorm(c_q, p["q_norm"]) @ p["w_uq"]).reshape(bsz, seqlen, MLA_HEADS, QK_NOPE + QK_ROPE)
    q_nope = q[..., :QK_NOPE]
    q_rope = _rope(q[..., QK_NOPE:], pos)
    lat_new = _rmsnorm(c_kv, p["kv_norm"])
    kr_new = _rope(k_r[:, :, None, :], pos)[:, :, 0, :]
    if lat_past is None:
        lat, kr = lat_new, kr_new
    else:
        lat = jnp.concatenate([lat_past.astype(lat_new.dtype), lat_new], axis=1)
        kr = jnp.concatenate([kr_past.astype(kr_new.dtype), kr_new], axis=1)
    n_keys = lat.shape[1]
    k_pos = jnp.arange(n_keys)
    k_nope = (lat @ p["w_uk"]).reshape(bsz, n_keys, MLA_HEADS, QK_NOPE)
    v = (lat @ p["w_uv"]).reshape(bsz, n_keys, MLA_HEADS, V_DIM)
    attend = _mla_attend_blocked if blocked else _mla_attend
    y_mla = attend(q_nope, q_rope, pos, k_nope, kr, v, k_pos).reshape(bsz, seqlen, MLA_HEADS * V_DIM)

    y_mem = _mem_attend(q_mem.reshape(bsz, seqlen, MEM_HEADS, MEM_HEAD_DIM), mem_k, mem_v)
    y_mem = y_mem.reshape(bsz, seqlen, MEM_WIDTH)

    g_ssm, g_mla, g_mem = jnp.split(jax.nn.sigmoid(gate_pre), N_BRANCHES, axis=-1)
    merged = (g_ssm * (y_ssm @ p["w_br_ssm"])
              + g_mla * (y_mla @ p["w_br_mla"])
              + g_mem * (y_mem @ p["w_br_mem"]))
    x = x + merged @ p["w_out"]
    x = x + 0.5 * _swiglu(_rmsnorm(x, p["ffn2_norm"]), p["ffn2_w_gate"], p["ffn2_w_up"], p["ffn2_w_down"])
    return x, lat_new, kr_new, h_re, h_im

def setup_inputs(seed: int = 0) -> dict:
    key = jax.random.key(seed)
    keys = jax.random.split(key, 64)
    ks = (keys[i] for i in range(64))
    f32 = jnp.float32
    L = DEPTH

    def nrm(shape, scale):
        return jax.random.normal(next(ks), shape, f32) * scale

    def gain(shape):
        return 1.0 + 0.01 * jax.random.normal(next(ks), shape, f32)

    G, P, Hc = SSM_GROUPS, SSM_STATE, SSM_GROUP
    return {
        "x_prompt": nrm((BATCH, SEQ, D_MODEL), 1.0),
        "x_sample": nrm((DEC_BATCH, DEC_SEQ, D_MODEL), 1.0),
        "cache_kv_latent": nrm((L, DEC_BATCH, PAST_LEN, KV_LORA), 1.0),
        "cache_k_rope": nrm((L, DEC_BATCH, PAST_LEN, QK_ROPE), 1.0),
        "cache_mem_k": nrm((L, DEC_BATCH, MEM_TOKENS, MEM_HEADS, MEM_HEAD_DIM), 1.0),
        "cache_mem_v": nrm((L, DEC_BATCH, MEM_TOKENS, MEM_HEADS, MEM_HEAD_DIM), 1.0),
        "state_ssm_re": nrm((L, DEC_BATCH, G, P), 0.1),
        "state_ssm_im": nrm((L, DEC_BATCH, G, P), 0.1),
        "mem_prompt": nrm((BATCH, MEM_TOKENS, D_MODEL), 1.0),
        "ffn1_norm": gain((L, D_MODEL)),
        "ffn1_w_gate": nrm((L, D_MODEL, D_FF), D_MODEL ** -0.5),
        "ffn1_w_up": nrm((L, D_MODEL, D_FF), D_MODEL ** -0.5),
        "ffn1_w_down": nrm((L, D_FF, D_MODEL), D_FF ** -0.5),
        "mix_norm": gain((L, D_MODEL)),
        "w_in": nrm((L, D_MODEL, IN_COLS), D_MODEL ** -0.5),
        "q_norm": gain((L, Q_LORA)),
        "w_uq": nrm((L, Q_LORA, MLA_HEADS * (QK_NOPE + QK_ROPE)), Q_LORA ** -0.5),
        "kv_norm": gain((L, KV_LORA)),
        "w_uk": nrm((L, KV_LORA, MLA_HEADS * QK_NOPE), KV_LORA ** -0.5),
        "w_uv": nrm((L, KV_LORA, MLA_HEADS * V_DIM), KV_LORA ** -0.5),
        "ssm_a_re": -0.5 * (1.0 + 0.05 * nrm((L, G, P), 1.0)),
        "ssm_a_im": jnp.tile(math.pi * jnp.arange(P, dtype=f32), (L, G, 1)),
        "ssm_log_dt": jax.random.uniform(next(ks), (L, G), f32, math.log(1e-3), math.log(1e-1)),
        "ssm_b_re": nrm((L, G, P, Hc), (2.0 * Hc) ** -0.5),
        "ssm_b_im": nrm((L, G, P, Hc), (2.0 * Hc) ** -0.5),
        "ssm_c_re": nrm((L, G, Hc, P), 0.5),
        "ssm_c_im": nrm((L, G, Hc, P), 0.5),
        "ssm_d": nrm((L, G, Hc), 1.0),
        "ssm_w_glu": nrm((L, SSM_WIDTH, SSM_WIDTH), SSM_WIDTH ** -0.5),
        "ssm_b_glu": nrm((L, SSM_WIDTH), 0.01),
        "mem_norm": gain((L, D_MODEL)),
        "w_mem_k": nrm((L, D_MODEL, MEM_WIDTH), D_MODEL ** -0.5),
        "w_mem_v": nrm((L, D_MODEL, MEM_WIDTH), D_MODEL ** -0.5),
        "w_br_ssm": nrm((L, SSM_WIDTH, D_MODEL), SSM_WIDTH ** -0.5),
        "w_br_mla": nrm((L, MLA_HEADS * V_DIM, D_MODEL), (MLA_HEADS * V_DIM) ** -0.5),
        "w_br_mem": nrm((L, MEM_WIDTH, D_MODEL), MEM_WIDTH ** -0.5),
        "w_out": nrm((L, D_MODEL, D_MODEL), D_MODEL ** -0.5),
        "ffn2_norm": gain((L, D_MODEL)),
        "ffn2_w_gate": nrm((L, D_MODEL, D_FF), D_MODEL ** -0.5),
        "ffn2_w_up": nrm((L, D_MODEL, D_FF), D_MODEL ** -0.5),
        "ffn2_w_down": nrm((L, D_FF, D_MODEL), D_FF ** -0.5),
        "final_norm": gain((D_MODEL,)),
    }

def reference(x_prompt, x_sample, cache_kv_latent, cache_k_rope, cache_mem_k, cache_mem_v,
              state_ssm_re, state_ssm_im, mem_prompt,
              ffn1_norm, ffn1_w_gate, ffn1_w_up, ffn1_w_down, mix_norm, w_in,
              q_norm, w_uq, kv_norm, w_uk, w_uv,
              ssm_a_re, ssm_a_im, ssm_log_dt, ssm_b_re, ssm_b_im, ssm_c_re, ssm_c_im, ssm_d,
              ssm_w_glu, ssm_b_glu, mem_norm, w_mem_k, w_mem_v,
              w_br_ssm, w_br_mla, w_br_mem, w_out,
              ffn2_norm, ffn2_w_gate, ffn2_w_up, ffn2_w_down, final_norm):
    xp, xs = x_prompt, x_sample
    past = cache_kv_latent.shape[2]
    pos_p = jnp.arange(xp.shape[1])
    pos_s = past + jnp.arange(xs.shape[1])
    lat_p_l, kr_p_l, mk_p_l, mv_p_l, sre_p_l, sim_p_l = [], [], [], [], [], []
    lat_s_l, kr_s_l, sre_s_l, sim_s_l = [], [], [], []
    for l in range(DEPTH):
        p = {
            "ffn1_norm": ffn1_norm[l], "ffn1_w_gate": ffn1_w_gate[l], "ffn1_w_up": ffn1_w_up[l],
            "ffn1_w_down": ffn1_w_down[l], "mix_norm": mix_norm[l], "w_in": w_in[l],
            "q_norm": q_norm[l], "w_uq": w_uq[l], "kv_norm": kv_norm[l], "w_uk": w_uk[l], "w_uv": w_uv[l],
            "ssm_a_re": ssm_a_re[l], "ssm_a_im": ssm_a_im[l], "ssm_log_dt": ssm_log_dt[l],
            "ssm_b_re": ssm_b_re[l], "ssm_b_im": ssm_b_im[l], "ssm_c_re": ssm_c_re[l],
            "ssm_c_im": ssm_c_im[l], "ssm_d": ssm_d[l], "ssm_w_glu": ssm_w_glu[l], "ssm_b_glu": ssm_b_glu[l],
            "w_br_ssm": w_br_ssm[l], "w_br_mla": w_br_mla[l], "w_br_mem": w_br_mem[l], "w_out": w_out[l],
            "ffn2_norm": ffn2_norm[l], "ffn2_w_gate": ffn2_w_gate[l], "ffn2_w_up": ffn2_w_up[l],
            "ffn2_w_down": ffn2_w_down[l],
        }
        mk_p, mv_p = _mem_kv(mem_prompt, mem_norm[l], w_mem_k[l], w_mem_v[l])
        xp, lat_p, kr_p, sre_p, sim_p = _layer(xp, pos_p, mk_p, mv_p, None, None, None, None, p, True)
        xs, lat_s, kr_s, sre_s, sim_s = _layer(xs, pos_s, cache_mem_k[l], cache_mem_v[l],
                                               cache_kv_latent[l], cache_k_rope[l],
                                               state_ssm_re[l], state_ssm_im[l], p, False)
        lat_p_l.append(lat_p); kr_p_l.append(kr_p); mk_p_l.append(mk_p); mv_p_l.append(mv_p)
        sre_p_l.append(sre_p); sim_p_l.append(sim_p)
        lat_s_l.append(lat_s); kr_s_l.append(kr_s); sre_s_l.append(sre_s); sim_s_l.append(sim_s)
    y_prompt = _rmsnorm(xp, final_norm)
    y_sample = _rmsnorm(xs, final_norm)
    return (y_prompt, y_sample,
            jnp.stack(lat_p_l), jnp.stack(kr_p_l), jnp.stack(mk_p_l), jnp.stack(mv_p_l),
            jnp.stack(sre_p_l), jnp.stack(sim_p_l),
            jnp.stack(lat_s_l), jnp.stack(kr_s_l), jnp.stack(sre_s_l), jnp.stack(sim_s_l))


_drawn_inputs = setup_inputs


def setup_inputs(seed=0):
    import zlib

    import numpy as np

    out = dict(_drawn_inputs(seed))
    spreads = {}
    factors = {'ffn1_norm': 8.0,
     'mix_norm': 15.015,
     'q_norm': 35.297,
     'kv_norm': 31.362,
     'ssm_b_glu': 200.0,
     'mem_norm': 29.986,
     'ffn2_norm': 181.77,
     'final_norm': 158.864}
    for name, (base, spread) in spreads.items():
        noise = np.random.default_rng([zlib.crc32(name.encode()), seed]).standard_normal(out[name].shape)
        drawn = base * np.exp(spread * noise) if base else spread * noise
        out[name] = jnp.asarray(drawn.astype(out[name].dtype))
    for name, factor in factors.items():
        out[name] = (out[name] * factor).astype(out[name].dtype)
    return out
```

```python
from contextlib import ExitStack, contextmanager

import numpy as np
import concourse.bass as bass
from concourse import mybir

F32 = mybir.dt.float32
F32R = mybir.dt.float32r
ACT = mybir.ActivationFunctionType
ALU = mybir.AluOpType
AX_X = mybir.AxisListType.X

P = 128
D = 2048
KD = D // P
N_P, N_S = 256, 64
N = N_P + N_S
PAST = 128
KEYS = N_P + PAST + N_S
D_FF = 5632
WIN = 512
FFN_BLOCKS = D_FF // WIN
SSM_W, Q_LORA, KV_LORA, ROPE, MEM_W = 1024, 768, 512, 64, 512
NOPE, HEADS, MEM_HEADS, HD = 128, 16, 4, 128
COL_Q = SSM_W
COL_KV = COL_Q + Q_LORA
COL_KR = COL_KV + KV_LORA
COL_QM = COL_KR + ROPE
COL_GATE = COL_QM + MEM_W
EPS = 1e-6
MLA_SCALE = (NOPE + ROPE) ** -0.5
MEM_SCALE = HD ** -0.5
S_TILES = 32
S_IT = 4
RAW, SPL = 3, 4

G_FFN1, G_MIX, G_FFN2, G_FIN, G_MEM, G_Q, G_KV, G_BGLU, G_D = 0, 16, 32, 48, 64, 80, 86, 90, 98
G_COLS = 106
C_ID, C_PERM, C_COS, C_SIN, C_HALF, C_MASK = 0, 128, 256, 576, 896, 1024
C_COLS = 1280
S_ARE, S_AIM, S_LDT, S_H0RE, S_H0IM = range(5)
(V_C1, V_S1, V_R, V_ZRE, V_ZIM, V_L0R, V_L0I, V_DT, V_AR, V_PH, V_PS, V_PC, V_K, V_LRE, V_LIM, V_INV, V_T,
 V_NR) = range(18)

FFN_CH = 24 * FFN_BLOCKS
CH_MEM = 0
CH_FFN1 = CH_MEM + 16
CH_Z = CH_FFN1 + FFN_CH
CH_MLA = CH_Z + 56
CH_GLU = CH_MLA + 4 * 12
CH_MERGE = CH_GLU + 8
CH_FFN2 = CH_MERGE + 4 * 48
CH_END = CH_FFN2 + FFN_CH
GR_MEM = (0, 0)
GR_FFN1 = (1, 1)
GR_Z = (1 + 33, 1 + 33)
GR_MLA = (GR_Z[0] + 4, GR_Z[1] + 3)
GR_GLU = (GR_MLA[0] + 8, GR_MLA[1] + 8)
GR_MERGE = (GR_GLU[0] + 1, GR_GLU[1] + 1)
GR_FFN2 = (GR_MERGE[0] + 20, GR_MERGE[1] + 20)
GR_END = (GR_FFN2[0] + 33, GR_FFN2[1] + 33)
SQ = {"mem": 0, "ffn1": 8, "mix": 16, "q": 24, "kv": 27, "ffn2": 29, "fin": 37}
AP = {"mem": 0, "ffn1": 8, "mix": 16, "q": 24, "kv": 27, "mix2": 29, "ffn2": 37, "fin": 45}
NORM = {"mem": 0, "ffn1": 1, "mix": 2, "q": 3, "kv": 4, "ffn2": 5, "fin": 6}
MLA_LINKS, S5_LINKS, MERGE_LINKS = 12, 29, 3
AT_MEM, AT_MLA = 0, MEM_HEADS

MLA_ATT = dict(
    tiles=[(0, 128, 0, 128, 0, 0), (128, 128, 0, 256, 0, 128), (256, 64, 256, 192, 1, 0)],
    pcols=[0, 128, 384],
    turns=[(0, 0, 128, 2, 0), (1, 0, 128, 2, 128), (1, 128, 128, 2, 256), (2, 0, 128, 3, 0), (2, 128, 64, 3, 64)],
    pv=[(0, 128, 0, 256, 0, True, False), (1, 128, 256, 128, 128, False, True),
        (2, 128, 384, 64, 256, True, False), (3, 64, 448, 64, 256, False, True)],
    split=384, total=512, scale=MLA_SCALE, last_rows=64)
MEM_ATT = dict(
    tiles=[(0, 128, 0, 256, 0, 0), (128, 128, 0, 256, 0, 256), (256, 64, 256, 256, 1, 0)],
    pcols=[0, 256, 512],
    turns=[(0, 0, 128, 2, 0), (1, 0, 128, 2, 128), (0, 128, 128, 2, 256), (1, 128, 128, 2, 384),
           (2, 0, 128, 3, 0), (2, 128, 128, 3, 64)],
    pv=[(0, 128, 0, 256, 0, True, False), (1, 128, 256, 256, 0, False, True),
        (2, 128, 512, 64, 256, True, False), (3, 128, 576, 64, 256, False, True)],
    split=512, total=640, scale=MEM_SCALE, last_rows=128)


def build(nc, t_in, t_out):
    with ExitStack() as ctx:
        def psum(name, shape):
            return ctx.enter_context(nc.psum_tensor(name, shape, F32))

        def sem(name):
            return ctx.enter_context(nc.semaphore(name))

        BASE = 16512
        END = nc.sbuf_usable_end

        class Region:

            def __init__(self, at):
                self.at = at

            def take(self, name, cols, dt=F32):
                shape = [P] + (list(cols) if isinstance(cols, (list, tuple)) else [cols])
                size = 4
                for c in shape[1:]:
                    size *= c
                t = nc.alloc_sbuf_tensor_at(name, shape, dt, offset=self.at)
                self.at += (size + 31) // 32 * 32
                assert self.at <= END, (name, self.at, END)
                return t

        R = Region(BASE)
        const = R.take("const", C_COLS)
        ones = R.take("ones", P)
        gains = R.take("gains", G_COLS)
        s5p = R.take("s5p", [5, S_TILES])
        s5v = R.take("s5v", [18, S_TILES])
        states = R.take("states", [4, S_TILES])
        stats = R.take("stats", [4, 4])
        rstd = R.take("rstd", N)
        rstd_mix = R.take("rstd_mix", N)
        mean = R.take("mean", N)
        x = R.take("x", [KD, N])
        raw = R.take("raw", [RAW, 2 * WIN])
        whi = R.take("whi", [SPL, 2 * WIN], F32R)
        wlo = R.take("wlo", [SPL, 2 * WIN], F32R)
        n0 = R.at
        sq = R.take("sq", [2, 2, N])
        hf = R.take("hf", [2, 2, N])
        M = Region(n0)
        gate = M.take("gate", [4, N])
        merged = M.take("merged", [4, N])
        assert M.at <= R.at
        h0 = R.at
        hhi = R.take("hhi", [KD, N], F32R)
        hlo = R.take("hlo", [KD, N], F32R)
        v0 = R.at

        V = Region(v0)
        mkT = V.take("mkT", [MEM_HEADS, 512])
        mv = V.take("mv", [4, MEM_W])
        v16 = V.at
        memT = Region(v16).take("memT", [KD, 256])
        B = Region(v16)
        silu_g = B.take("silu_g", [4, N])
        prod = B.take("prod", [4, N])
        phi = B.take("phi", [4, N], F32R)
        plo = B.take("plo", [4, N], F32R)
        Z = Region(v16)
        cqT = Z.take("cqT", [6, N])
        ckvT = Z.take("ckvT", [4, N])
        krraw = Z.take("krraw", N)
        qmT = Z.take("qmT", [MEM_HEADS, N])
        mem_p = [Z.take(f"mem_p{b}", 768) for b in range(2)]
        mem_pT = Z.take("mem_pT", 640)
        ymf = Z.take("ymf", [4, N])
        assert Z.at <= v0 + 61440
        T = Region(v0 + 61440)
        ymhi = T.take("ymhi", [4, N], F32R)
        ymlo = T.take("ymlo", [4, N], F32R)
        u = T.take("u", [8, N])
        T = Region(v0 + 71680)
        mhi = T.take("mhi", [4, N], F32R)
        mlo = T.take("mlo", [4, N], F32R)
        L = Region(h0)
        cqhi = L.take("cqhi", [6, N], F32R)
        cqlo = L.take("cqlo", [6, N], F32R)
        lathi = L.take("lathi", [4, 512], F32R)
        latlo = L.take("latlo", [4, 512], F32R)
        kr = L.take("kr", [2, KEYS])
        krot = L.take("krot", N)
        assert L.at <= v0
        K1 = Region(v0)
        qn = K1.take("qn", [4, N])
        qraw = K1.take("qraw", [2, N])
        qrope = K1.take("qrope", [2, N])
        kn = K1.take("kn", [4, KEYS])
        mla_p0 = K1.take("mla_p0", 576)
        assert K1.at <= v0 + 20480
        ymla = Region(v0 + 20480).take("ymla", [HEADS, N])
        K2 = Region(v0 + 40960)
        vv = K2.take("vv", [4, WIN])
        mla_pT = K2.take("mla_pT", 512)
        mla_p = [mla_p0, K2.take("mla_p1", 576)]
        past = K2.take("past", [4, PAST])
        latf = K2.take("latf", [4, N])
        assert K2.at <= v0 + 61440
        S = Region(h0)
        ec = S.take("ec", [S_IT, N])
        es = S.take("es", [S_IT, N])
        dec = S.take("dec", [S_IT, N])
        s_t = S.take("s_t", [S_IT, N])
        w_re = S.take("w_re", [S_IT, N])
        w_im = S.take("w_im", [S_IT, N])
        v_re = S.take("v_re", [S_IT, N])
        v_im = S.take("v_im", [S_IT, N])
        assert S.at <= v0
        S = Region(v0)
        brw = S.take("brw", [2, S_IT, P])
        cpd = S.take("cpd", [2, S_IT, P])
        bb = S.take("bb", [2, S_IT, P])
        bT = S.take("bT", [2, S_IT, P])
        ucur = S.take("ucur", N)
        ycur = S.take("ycur", N)
        cur = S.take("cur", [7, S_IT])
        pw = S.take("pw", [5, S_IT])
        assert S.at <= v0 + 20480
        U = Region(v0)
        yshi = U.take("yshi", [8, N], F32R)
        yslo = U.take("yslo", [8, N], F32R)
        U = Region(h0)
        gyhi = U.take("gyhi", [8, N], F32R)
        gylo = U.take("gylo", [8, N], F32R)
        sgl = Region(v0 + 40960).take("sgl", [4, N])
        yalo = Region(v0 + 20480).take("yalo", [HEADS, N], F32R)
        yahi = Region(v0 + 40960).take("yahi", [HEADS, N], F32R)

        banks = psum("banks", [P, 8, 512])

        const_in = sem("const_in")
        x_in = sem("x_in")
        mem_in = sem("mem_in")
        memkv_in = sem("memkv_in")
        past_in = sem("past_in")
        s5_in = sem("s5_in")
        raw_in = [sem(f"raw_in{i}") for i in range(RAW)]
        w_hi = sem("w_hi")
        w_lo = sem("w_lo")
        w_used = sem("w_used")
        half_free = [sem("half0_free"), sem("half1_free")]
        ones_set = sem("ones_set")
        sq_ready = sem("sq_ready")
        sq_used = sem("sq_used")
        mean_ready = sem("mean_ready")
        rstd_ready = sem("rstd_ready")
        hf_ready = sem("hf_ready")
        hf_hi = sem("hf_hi")
        hf_lo = sem("hf_lo")
        prod_hi = sem("prod_hi")
        prod_lo = sem("prod_lo")
        past_hi = sem("past_hi")
        past_lo = sem("past_lo")
        lat_out = sem("lat_out")
        y_out = [sem("y_out0"), sem("y_out1")]
        kr_turned = sem("kr_turned")
        kr_rotated = sem("kr_rotated")
        q_turned = sem("q_turned")
        q_rotated = sem("q_rotated")
        scores = sem("scores")
        max_ready = sem("max_ready")
        exp_ready = sem("exp_ready")
        p_ready = sem("p_ready")
        p_turned = sem("p_turned")
        pT_ready = sem("pT_ready")
        pv_done = sem("pv_done")
        pv_out = sem("pv_out")
        ym_split = sem("ym_split")
        dve_link = sem("dve_link")
        s5_exp = sem("s5_exp")
        s5_arg = sem("s5_arg")
        s5_sin = sem("s5_sin")
        bb_ready = sem("bb_ready")
        bb_turned = sem("bb_turned")
        bT_ready = sem("bT_ready")
        bu_ready = sem("bu_ready")
        s5_x = sem("s5_x")
        s5_y = sem("s5_y")
        ycur_ready = sem("ycur_ready")
        gelu_ready = sem("gelu_ready")
        gy_split = sem("gy_split")
        ys_half = sem("ys_half")
        ys_split = sem("ys_split")
        ya_split = sem("ya_split")
        m_split = sem("m_split")
        stored = sem("stored")

        def wait(e, s, base, i=None, per=0):
            e.wait_ge(s, base if i is None else i * per + base)

        def rows(w, r0, n, c0, width):
            return w[bass.ds(r0, n * P), bass.ds(c0, width)].rearrange("(t p) c -> p t c", p=P)


        def load(e, c, src, n, width, i=None, per=0):
            slot = c % RAW
            if c >= RAW:
                wait(e, w_lo, c - RAW + 1, i, per)
            e.dma_start(raw[:, slot, 0:n * width].rearrange("p (t c) -> p t c", t=n), src).then_inc(raw_in[slot], 16)

        def round_w(e, c, size, i=None, per=0):
            slot = c % RAW
            wait(e, raw_in[slot], 16 * (c // RAW + 1), i, 16 * per // RAW)
            if c >= SPL:
                wait(e, w_used, c - SPL + 1, i, per)
            e.activation(whi[:, c % SPL, 0:size], raw[:, slot, 0:size], ACT.Copy).then_inc(w_hi, 1)

        def split_w(e, c, size, i=None, per=0):
            wait(e, w_hi, c + 1, i, per)
            e.tensor_tensor(wlo[:, c % SPL, 0:size], raw[:, c % RAW, 0:size],
                            whi[:, c % SPL, 0:size].bitcast(F32), ALU.subtract).then_inc(w_lo, 1)

        def three(e, out, hi_s, lo_s, hi_m, lo_m, start, stop):
            e.matmul(out, hi_s, hi_m, start=start, stop=False)
            e.matmul(out, hi_s, lo_m, start=False, stop=False)
            return e.matmul(out, lo_s, hi_m, start=False, stop=stop)

        def products(e, c, half, n, width, tiles, ahi, alo, k, first, last, cols=N, i=None, per=0):
            wait(e, w_lo, c + 1, i, per)
            s = c % SPL
            wh = whi[:, s, 0:n * width].rearrange("p (t c) -> p t c", t=n)
            wl = wlo[:, s, 0:n * width].rearrange("p (t c) -> p t c", t=n)
            for q in range(n):
                for m in range(tiles):
                    a, b = wh[:, q, m * P:(m + 1) * P], wl[:, q, m * P:(m + 1) * P]
                    ins = three(e, banks[:, 4 * half + m, 0:cols], a, b, ahi[:, k + q, 0:cols], alo[:, k + q, 0:cols],
                                first and q == 0, last and q == n - 1)
            ins.then_inc(w_used, 1)

        def token_products(e, c, half, n, tiles, ahi, alo, k, first, last, i=None, per=0):
            wait(e, w_lo, c + 1, i, per)
            s = c % SPL
            wh = whi[:, s, :].rearrange("p (t c) -> p t c", t=n)
            wl = wlo[:, s, :].rearrange("p (t c) -> p t c", t=n)
            for q in range(n):
                for m in range(tiles):
                    o = banks[:, 4 * half + m, :]
                    sl = slice(m * P, (m + 1) * P)
                    e.matmul(o, ahi[:, k + q, sl], wh[:, q, :], start=first and q == 0, stop=False)
                    e.matmul(o, alo[:, k + q, sl], wh[:, q, :], start=False, stop=False)
                    ins = e.matmul(o, ahi[:, k + q, sl], wl[:, q, :], start=False, stop=last and q == n - 1)
            ins.then_inc(w_used, 1)

        def ffn_order(first, last):
            g = [("gate", k) for k in range(8)]
            d = [("down", k) for k in range(8)]
            up = [("up", k) for k in range(8)]
            return g + up if first else d if last else g + d + up

        def ffn_stream(e, c0, visit):
            for j, (kind, k) in enumerate(ffn_order(True, False)):
                visit(c0 + j, kind, k, 0, None, 0, "head")
            with e.Fori(0, FFN_BLOCKS - 1) as i:
                for j, (kind, k) in enumerate(ffn_order(False, False)):
                    visit(c0 + 16 + j, kind, k, i, i, 24, "body")
            ce = c0 + 16 + 24 * (FFN_BLOCKS - 1)
            for j, (kind, k) in enumerate(ffn_order(False, True)):
                visit(ce + j, kind, k, FFN_BLOCKS - 1, None, 0, "tail")

        BR = [("ssm", 4, 2, D), ("mla", 8, 2, D + SSM_W), ("mem", 4, 1, D + SSM_W + HEADS * HD)]

        def merge_order():
            out = []
            for b, (name, nch, n, row) in enumerate(BR):
                out += [("gate", b, k) for k in range(8)]
                out += [("branch", b, k) for k in range(nch)]
            out += [("out", 0, k) for k in range(8)]
            assert len(out) == 48
            return out

        Z_WIN = [(0, 512, 0), (512, 512, 1), (COL_Q, 512, 0), (COL_Q + 512, 256, 1), (COL_KV, 512, 0),
                 (COL_KR, 128, 1), (COL_QM, 512, 0)]
        MLA_ORDER = ([("uq", un, k, n) for un in range(2) for k, n in ((0, 2), (2, 2), (4, 1), (5, 1))]
                     + [("uk", 0, 0, 2), ("uk", 0, 2, 2), ("uv", 0, 0, 2), ("uv", 0, 2, 2)])
        QW = 2 * (NOPE + ROPE)

        def size_of_mla(kind, n):
            return n * (QW if kind == "uq" else WIN)

        with nc.Block() as block:
            @block.sync
            def _(e):
                e.dma_start(const[:], t_in["const"]).then_inc(const_in, 16)
                e.dma_start(gains[:], t_in["gains"]).then_inc(const_in, 16)
                e.dma_start(s5p[:], t_in["s5p"]).then_inc(const_in, 16)
                e.dma_start(memT[:], t_in["memT"].rearrange("(t p) n -> p t n", p=P)).then_inc(mem_in, 16)
                e.dma_start(x[:], t_in["xT"].rearrange("(t p) n -> p t n", p=P)).then_inc(x_in, 16)
                e.dma_start(mkT[:, :, 256:512], t_in["cmkT"].rearrange("(h p) n -> p h n", p=P)).then_inc(memkv_in, 16)
                e.dma_start(mv[:, 2:4, :], t_in["cmv"].rearrange("(t p) n -> p t n", p=P)).then_inc(memkv_in, 16)
                for w, name in enumerate(("w_mem_k", "w_mem_v")):
                    for k in range(8):
                        load(e, CH_MEM + 8 * w + k, rows(t_in[name], 256 * k, 2, 0, WIN), 2, WIN)

                def ffn_loads(c0, name):
                    def visit(c, kind, k, b, i, per, step):
                        w = t_in[f"{name}_w_{kind}"]
                        if kind == "down":
                            r0 = b * WIN + (k % 2) * 256
                            c_at = (k // 2) * WIN
                        else:
                            r0 = k * 256
                            c_at = 0 if step == "head" else b * WIN + WIN
                        if step == "body":
                            if kind == "down":
                                r0 = e.snap(r0)
                            else:
                                c_at = e.snap(c_at)
                        load(e, c, rows(w, r0, 2, c_at, WIN), 2, WIN, i, per)
                    ffn_stream(e, c0, visit)

                ffn_loads(CH_FFN1, "ffn1")
                e.wait_ge(half_free[0], 1)
                e.wait_ge(half_free[1], 1)
                e.dma_start(t_out["mkT"].rearrange("(h p) n -> p h n", p=P), mkT[:, :, 0:256]).then_inc(stored, 16)
                e.dma_start(t_out["mv"].rearrange("(t p) n -> p t n", p=P), mv[:, 0:2, :]).then_inc(stored, 16)
                c = CH_Z
                for c_at, width, half in Z_WIN:
                    for k in range(8):
                        w, at = (t_in["w_kr2"], 0) if width == 128 else (t_in["w_in"], c_at)
                        load(e, c, rows(w, 256 * k, 2, at, width), 2, width)
                        c += 1
                e.wait_ge(pv_out, MEM_HEADS)
                e.dma_start(past[:], t_in["platT"].rearrange("(t p) n -> p t n", p=P)).then_inc(past_in, 16)
                e.dma_start(kr[0:64, 0, N_P:N_P + PAST], t_in["pkrT"]).then_inc(past_in, 16)
                e.dma_start(kr[64:128, 1, N_P:N_P + PAST], t_in["pkrT"]).then_inc(past_in, 16)
                e.wait_ge(hf_ready, AP["kv"] + 2)
                e.dma_start(t_out["latT"].rearrange("(t p) n -> p t n", p=P), latf[:]).then_inc(lat_out, 16)
                e.wait_ge(kr_rotated, 1)
                e.dma_start(t_out["krT"], krot[0:64, :]).then_inc(lat_out, 16)
                with e.Fori(0, 4) as i:
                    for j, (kind, un, k, n) in enumerate(MLA_ORDER):
                        width = QW if kind == "uq" else WIN
                        c_at = e.snap(i * 2 * QW + un * QW) if kind == "uq" else e.snap(i * WIN)
                        load(e, CH_MLA + j, rows(t_in["w_" + kind], k * P, n, c_at, width), n, width, i, 12)
                def s5_loads(at):
                    for z, name in enumerate(("bp_re", "bp_im")):
                        e.dma_start(brw[:, z], t_in[name][:, bass.ds(at, S_IT), :]).then_inc(s5_in, 16)
                    for z, name in enumerate(("cp_re", "cp_im")):
                        e.dma_start(cpd[:, z], t_in[name][:, bass.ds(at, S_IT), :]).then_inc(s5_in, 16)

                e.wait_ge(pv_out, AT_MLA + 16)
                s5_loads(0)
                with e.Fori(0, 7) as i:
                    at = e.snap(i * S_IT + S_IT)
                    e.wait_ge(s5_y, i + 1)
                    s5_loads(at)
                for w in range(2):
                    for k in range(4):
                        load(e, CH_GLU + 4 * w + k, rows(t_in["ssm_w_glu"], 256 * k, 2, w * WIN, WIN), 2, WIN)
                e.wait_ge(ys_split, 1)
                e.dma_start(t_out["states"], states[:]).then_inc(stored, 16)
                with e.Fori(0, 4) as i:
                    for j, (kind, b, k) in enumerate(merge_order()):
                        if kind == "gate":
                            c_at = e.snap(i * WIN + (COL_GATE + b * D))
                            load(e, CH_MERGE + j, rows(t_in["w_in"], 256 * k, 2, c_at, WIN), 2, WIN, i, 48)
                        elif kind == "branch":
                            n = BR[b][2]
                            c_at = e.snap(i * WIN)
                            load(e, CH_MERGE + j, rows(t_in["w_post"], BR[b][3] + n * P * k, n, c_at, WIN), n, WIN, i, 48)
                        else:
                            r_at = e.snap(i * WIN + (k % 2) * 256)
                            load(e, CH_MERGE + j, rows(t_in["w_post"], r_at, 2, (k // 2) * WIN, WIN), 2, WIN, i, 48)
                ffn_loads(CH_FFN2, "ffn2")
                out = t_out["yT"].rearrange("(t p) n -> p t n", p=P)
                for p in range(8):
                    e.wait_ge(hf_ready, AP["fin"] + p + 1)
                    e.dma_start(out[:, 2 * p:2 * p + 2, :], hf[:, p % 2]).then_inc(y_out[p % 2], 16)
                e.wait_ge(y_out[0], 64)
                e.wait_ge(y_out[1], 64)
                e.wait_ge(stored, 48)
                e.wait_ge(lat_out, 32)

            @block.scalar
            def _(e):
                def squares(name, src, pairs, cols=N):
                    for p in range(pairs):
                        if SQ[name] + p >= 2:
                            e.wait_ge(sq_used, SQ[name] + p - 1)
                        e.activation(sq[:, p % 2, :, 0:cols], src[:, 2 * p:2 * p + 2, :], ACT.Square).then_inc(sq_ready, 1)

                def root(name, out, cols=N):
                    e.wait_ge(mean_ready, 2 * NORM[name] + 2)
                    e.activation(out[:, 0:cols], mean[:, 0:cols], ACT.Sqrt).then_inc(rstd_ready, 1)

                def round_h(name, out, pairs, cols=N):
                    for p in range(pairs):
                        e.wait_ge(hf_ready, AP[name] + p + 1)
                        e.activation(out[:, 2 * p:2 * p + 2, 0:cols], hf[:, p % 2, :, 0:cols], ACT.Copy).then_inc(hf_hi, 1)

                e.wait_ge(const_in, 48)
                e.activation(s5v[:, V_DT], s5p[:, S_LDT], ACT.Exp).then_inc(s5_exp, 1)
                e.wait_ge(s5_arg, 1)
                e.activation(s5v[:, V_R], s5v[:, V_AR], ACT.Exp).then_inc(s5_exp, 1)
                e.wait_ge(s5_arg, 2)
                e.activation(s5v[:, V_S1], s5v[:, V_PS], ACT.Sin).then_inc(s5_sin, 1)
                e.activation(s5v[:, V_C1], s5v[:, V_PC], ACT.Sin).then_inc(s5_sin, 1)
                e.wait_ge(mem_in, 16)
                squares("mem", memT, 8, 256)
                root("mem", rstd, 256)
                round_h("mem", hhi, 8, 256)
                for c in range(16):
                    round_w(e, CH_MEM + c, 2 * WIN)

                def ffn(name, c0, gr):
                    if name == "ffn1":
                        e.wait_ge(x_in, 16)
                    else:
                        e.wait_ge(half_free[0], gr[0])
                        e.wait_ge(half_free[1], gr[1])
                    squares(name, x, 8)
                    root(name, rstd)
                    if name == "ffn1":
                        e.wait_ge(w_used, CH_FFN1)
                    round_h(name, hhi, 8)

                    def silu(c_last, i, per, body):
                        wait(e, w_used, c_last + 1, i, per)
                        if body:
                            wait(e, half_free[1], gr[1] + 1, i, 3)
                        for m in range(4):
                            ins = e.activation(silu_g[:, m], banks[:, m, 0:N], ACT.Silu)
                        ins.then_inc(half_free[0], 1)

                    def visit(c, kind, k, b, i, per, step):
                        round_w(e, c, 2 * WIN, i, per)
                        if step == "head" and kind == "up" and k == 2:
                            silu(c - 3, i, per, False)
                        if step == "body" and kind == "down" and k == 2:
                            silu(c - 3, i, per, True)
                    ffn_stream(e, c0, visit)

                ffn("ffn1", CH_FFN1, GR_FFN1)
                e.wait_ge(half_free[0], GR_Z[0])
                e.wait_ge(half_free[1], GR_Z[1])
                squares("mix", x, 8)
                root("mix", rstd_mix)
                round_h("mix", hhi, 8)
                c = CH_Z
                for c_at, width, half in Z_WIN:
                    for k in range(8):
                        round_w(e, c, 2 * width)
                        c += 1

                def softmax(att, p_sb, h, i=None):
                    wait(e, max_ready, h + 1, i, 4)
                    for t, (q0, nq, k0, nk, bank, col) in enumerate(att["tiles"]):
                        ins = e.activation(p_sb[0:nq, att["pcols"][t]:att["pcols"][t] + nk],
                                           banks[0:nq, bank, col:col + nk], ACT.Exp, scale=att["scale"],
                                           bias=stats[0:nq, 1, t:t + 1], accum_out=stats[0:nq, 2, t:t + 1])
                    ins.then_inc(exp_ready, 1)

                for h in range(MEM_HEADS):
                    softmax(MEM_ATT, mem_p[h % 2], AT_MEM + h)
                squares("q", cqT, 3)
                root("q", rstd)
                round_h("q", cqhi, 3)
                e.wait_ge(w_used, CH_MLA)
                squares("kv", ckvT, 2)
                root("kv", rstd)
                for p in range(2):
                    e.wait_ge(hf_ready, AP["kv"] + p + 1)
                    for q in range(2):
                        ins = e.activation(lathi[:, 2 * p + q, 0:N_P], latf[:, 2 * p + q, 0:N_P], ACT.Copy)
                        ins = e.activation(lathi[:, 2 * p + q, N_P + PAST:KEYS], latf[:, 2 * p + q, N_P:N], ACT.Copy)
                    ins.then_inc(hf_hi, 1)
                e.wait_ge(past_in, 48)
                e.activation(lathi[:, :, N_P:N_P + PAST], past[:], ACT.Copy).then_inc(past_hi, 1)
                with e.Fori(0, 4) as i:
                    for j, (kind, un, k, n) in enumerate(MLA_ORDER):
                        round_w(e, CH_MLA + j, size_of_mla(kind, n), i, 12)
                    for h in range(4):
                        softmax(MLA_ATT, mla_p[h % 2], AT_MLA + h, i)
                with e.Fori(0, 8) as i:
                    e.wait_ge(ycur_ready, i + 1)
                    e.activation(u[:, bass.ds(i, 1), :], ycur[:].rearrange("p (o n) -> p o n", o=1),
                                 ACT.Gelu_apprx_tanh).then_inc(gelu_ready, 1)
                for w in range(2):
                    for k in range(4):
                        round_w(e, CH_GLU + 4 * w + k, 2 * WIN)
                for w in range(2):
                    e.wait_ge(w_used, CH_GLU + 4 * w + 4)
                    if w == 1:
                        e.wait_ge(ys_half, 1)
                    for m in range(4):
                        ins = e.activation(sgl[:, m], banks[:, 4 * w + m, 0:N], ACT.Sigmoid,
                                           bias=gains[:, G_BGLU + 4 * w + m:G_BGLU + 4 * w + m + 1])
                    ins.then_inc(half_free[w], 1)
                round_h("mix2", hhi, 8)
                with e.Fori(0, 4) as i:
                    gates = 0
                    for j, (kind, b, k) in enumerate(merge_order()):
                        n = BR[b][2] if kind == "branch" else 2
                        round_w(e, CH_MERGE + j, n * WIN, i, 48)
                        if kind == "branch" and k == 2:
                            wait(e, w_used, CH_MERGE + j - 2, i, 48)
                            wait(e, half_free[1], GR_MERGE[1] + gates, i, 5)
                            for m in range(4):
                                ins = e.activation(gate[:, m], banks[:, m, 0:N], ACT.Sigmoid)
                            ins.then_inc(half_free[0], 1)
                            gates += 1
                ffn("ffn2", CH_FFN2, GR_FFN2)
                e.wait_ge(half_free[0], GR_END[0])
                e.wait_ge(half_free[1], GR_END[1])
                squares("fin", x, 8)
                root("fin", rstd)

            @block.gpsimd
            def _(e):
                e.memset(ones[:], 1.0).then_inc(ones_set, 1)

                def split_h(name, out, hi, pairs, cols=N):
                    for p in range(pairs):
                        e.wait_ge(hf_hi, AP[name] + p + 1)
                        e.tensor_tensor(out[:, 2 * p:2 * p + 2, 0:cols], hf[:, p % 2, :, 0:cols],
                                        hi[:, 2 * p:2 * p + 2, 0:cols].bitcast(F32), ALU.subtract).then_inc(hf_lo, 1)

                split_h("mem", hlo, hhi, 8, 256)
                for c in range(16):
                    split_w(e, CH_MEM + c, 2 * WIN)
                split_h("ffn1", hlo, hhi, 8)
                ffn_stream(e, CH_FFN1, lambda c, kind, k, b, i, per, step: split_w(e, c, 2 * WIN, i, per))
                split_h("mix", hlo, hhi, 8)
                c = CH_Z
                for c_at, width, half in Z_WIN:
                    for k in range(8):
                        split_w(e, c, 2 * width)
                        c += 1
                split_h("q", cqlo, cqhi, 3)
                for p in range(2):
                    e.wait_ge(hf_hi, AP["kv"] + p + 1)
                    for q in range(2):
                        ins = e.tensor_tensor(latlo[:, 2 * p + q, 0:N_P], latf[:, 2 * p + q, 0:N_P],
                                              lathi[:, 2 * p + q, 0:N_P].bitcast(F32), ALU.subtract)
                        ins = e.tensor_tensor(latlo[:, 2 * p + q, N_P + PAST:KEYS], latf[:, 2 * p + q, N_P:N],
                                              lathi[:, 2 * p + q, N_P + PAST:KEYS].bitcast(F32), ALU.subtract)
                    ins.then_inc(hf_lo, 1)
                e.wait_ge(past_hi, 1)
                e.tensor_tensor(latlo[:, :, N_P:N_P + PAST], past[:], lathi[:, :, N_P:N_P + PAST].bitcast(F32),
                                ALU.subtract).then_inc(past_lo, 1)
                e.memset(lathi[:, :, KEYS:512].bitcast(F32), 0.0)
                e.memset(latlo[:, :, KEYS:512].bitcast(F32), 0.0).then_inc(past_lo, 1)
                with e.Fori(0, 4) as i:
                    for j, (kind, un, k, n) in enumerate(MLA_ORDER):
                        split_w(e, CH_MLA + j, size_of_mla(kind, n), i, 12)
                for c in range(8):
                    split_w(e, CH_GLU + c, 2 * WIN)
                split_h("mix2", hlo, hhi, 8)
                with e.Fori(0, 4) as i:
                    for j, (kind, b, k) in enumerate(merge_order()):
                        n = BR[b][2] if kind == "branch" else 2
                        split_w(e, CH_MERGE + j, n * WIN, i, 48)
                split_h("ffn2", hlo, hhi, 8)
                ffn_stream(e, CH_FFN2, lambda c, kind, k, b, i, per, step: split_w(e, c, 2 * WIN, i, per))

            @block.tensor
            def _(e):
                def sums(name, pairs, cols=N):
                    for p in range(pairs):
                        e.wait_ge(sq_ready, SQ[name] + p + 1)
                        for q in range(2):
                            ins = e.matmul(banks[:, 0, 0:cols], ones[:], sq[:, p % 2, q, 0:cols],
                                           start=p == 0 and q == 0, stop=p == pairs - 1 and q == 1)
                        ins.then_inc(sq_used, 1)

                def window(half, c0, name, ahi, alo, tiles, width, kpairs, group, base=CH_MEM, cols=N, norm=None):
                    for k in range(kpairs):
                        if k == 0 and group:
                            e.wait_ge(half_free[half], group)
                        if norm is not None:
                            e.wait_ge(hf_lo, AP[norm] + k + 1)
                        products(e, c0 + k, half, 2, width, tiles, ahi, alo, 2 * k, k == 0, k == kpairs - 1, cols)

                e.wait_ge(ones_set, 1)
                sums("mem", 8, 256)
                e.wait_ge(mean_ready, 1)
                window(0, CH_MEM, "w_mem_k", hhi, hlo, 4, WIN, 8, 0, cols=256, norm="mem")
                for k in range(8):
                    token_products(e, CH_MEM + 8 + k, 1, 2, 2, hhi, hlo, 2 * k, k == 0, k == 7)

                def ffn(name, c0, gr):
                    e.wait_ge(half_free[0], gr[0])
                    e.wait_ge(half_free[1], gr[1])
                    sums(name, 8)
                    e.wait_ge(mean_ready, 2 * NORM[name] + 1)
                    sbase = 0 if name == "ffn1" else FFN_BLOCKS

                    def visit(c, kind, k, b, i, per, step):
                        if kind in ("gate", "up"):
                            half = 0 if kind == "gate" else 1
                            if step == "head" and kind == "gate":
                                e.wait_ge(hf_lo, AP[name] + k + 1)
                            if k == 0 and step == "body":
                                wait(e, half_free[half], gr[half] + (1 if kind == "gate" else 3), i, 3)
                            products(e, c, half, 2, WIN, 4, hhi, hlo, 2 * k, k == 0, k == 7, N, i, per)
                        else:
                            w = k // 2
                            half = (1, 0, 1, 0)[w] if step == "body" else (0, 1, 0, 1)[w]
                            if k % 2 == 0:
                                if w == 0:
                                    if step == "body":
                                        wait(e, prod_lo, sbase + 1, i, 1)
                                    else:
                                        e.wait_ge(prod_lo, sbase + FFN_BLOCKS)
                                if step == "body":
                                    wait(e, half_free[half], gr[half] + (1, 2, 2, 3)[w], i, 3)
                                else:
                                    e.wait_ge(half_free[half], gr[half] + 3 * (FFN_BLOCKS - 1) + 1 + w // 2)
                            products(e, c, half, 2, WIN, 4, phi, plo, 2 * (k % 2), k % 2 == 0, k % 2 == 1, N, i, per)
                    ffn_stream(e, c0, visit)

                ffn("ffn1", CH_FFN1, GR_FFN1)
                e.wait_ge(half_free[0], GR_Z[0])
                e.wait_ge(half_free[1], GR_Z[1])
                sums("mix", 8)
                e.wait_ge(mean_ready, 2 * NORM["mix"] + 1)
                seen = list(GR_Z)
                for w, (c_at, width, half) in enumerate(Z_WIN):
                    window(half, CH_Z + 8 * w, "w_in", hhi, hlo, width // P, width, 8, seen[half],
                           norm="mix" if w == 0 else None)
                    seen[half] += 1

                def heads(att, h0_, keys, queries, values, p_sb, pT, extra, i=None):
                    def score(h):
                        if h0_ + h >= 1:
                            wait(e, exp_ready, h0_ + h, i, 4)
                        for t, (q0, nq, k0, nk, bank, col) in enumerate(att["tiles"]):
                            ops = [(queries[:, h, q0:q0 + nq], keys[:, h, k0:k0 + nk])] + extra(h, t, q0, nq, k0, nk)
                            for n_, (a, b) in enumerate(ops):
                                ins = e.matmul(banks[0:nq, bank, col:col + nk], a, b, start=n_ == 0,
                                               stop=n_ == len(ops) - 1)
                        ins.then_inc(scores, 1)

                    score(0)
                    for h in range(4):
                        if h < 3:
                            score(h + 1)
                        wait(e, p_ready, h0_ + h + 1, i, 4)
                        for t, kk, nk, bank, col in att["turns"]:
                            nq = att["tiles"][t][1]
                            at = att["pcols"][t] + kk
                            ins = e.transpose(banks[0:nk, bank, col:col + nq], p_sb[h % 2][0:nq, at:at + nk],
                                              const[0:nq, C_ID:C_ID + nq])
                        ins.then_inc(p_turned, 1)
                        wait(e, pT_ready, h0_ + h + 1, i, 4)
                        if h0_ + h >= 1:
                            wait(e, pv_out, h0_ + h, i, 4)
                        for vt, nr, pc, nq, oc, st, sp_ in att["pv"]:
                            ins = e.matmul(banks[:, 4, oc:oc + nq], values[0:nr, vt, h * HD:(h + 1) * HD],
                                           pT[0:nr, pc:pc + nq], start=st, stop=sp_, skip_group_check=True)
                        ins.then_inc(pv_done, 1)

                e.wait_ge(half_free[0], GR_MLA[0])
                e.wait_ge(half_free[1], GR_MLA[1])
                e.wait_ge(memkv_in, 32)
                heads(MEM_ATT, AT_MEM, mkT, qmT, mv, mem_p, mem_pT, lambda h, t, q0, nq, k0, nk: [])
                e.wait_ge(pv_out, MEM_HEADS)
                e.matmul(banks[:, 5, 0:N], const[:, C_PERM:C_PERM + P], krraw[:], start=True, stop=True).then_inc(kr_turned, 1)
                sums("q", 3)
                e.wait_ge(mean_ready, 2 * NORM["q"] + 1)
                sums("kv", 2)
                e.wait_ge(mean_ready, 2 * NORM["kv"] + 1)

                e.wait_ge(hf_lo, AP["kv"] + 2)
                e.wait_ge(past_lo, 2)
                e.wait_ge(kr_rotated, 2)
                e.wait_ge(past_in, 48)

                with e.Fori(0, 4) as i:
                    for j, (kind, un, k, n) in enumerate(MLA_ORDER):
                        half = un if kind == "uq" else 0 if kind == "uk" else 1
                        prior = {"uq": 0, "uk": 1, "uv": 1}[kind]
                        if k == 0:
                            wait(e, half_free[half], GR_MLA[half] + prior, i, 2)
                        if kind == "uq":
                            products(e, CH_MLA + j, half, n, QW, 3, cqhi, cqlo, k, k == 0, k == 5, N, i, 12)
                        elif kind == "uk":
                            products(e, CH_MLA + j, half, n, WIN, 4, lathi, latlo, k, k == 0, k == 2, KEYS, i, 12)
                        else:
                            token_products(e, CH_MLA + j, half, n, 4, lathi, latlo, k, k == 0, k == 2, i, 12)
                    wait(e, half_free[0], GR_MLA[0] + 2, i, 2)
                    wait(e, half_free[1], GR_MLA[1] + 2, i, 2)
                    for un in range(2):
                        e.matmul(banks[:, 5 + un, 0:N], const[:, C_PERM:C_PERM + P], qraw[:, un], start=True,
                                 stop=True).then_inc(q_turned, 1)
                    wait(e, q_rotated, 2, i, 2)

                    def extra(h, t, q0, nq, k0, nk):
                        ops = [(qrope[:, h // 2, q0:q0 + nq], kr[:, h % 2, k0:k0 + nk])]
                        if t < 2:
                            m0 = C_MASK + (128 if t == 0 else 0)
                            ops.append((const[0:1, C_HALF:C_HALF + nq], const[0:1, m0:m0 + nk]))
                        return ops

                    heads(MLA_ATT, AT_MLA, kn, qn, vv, mla_p, mla_pT, extra, i)
                    wait(e, pv_out, AT_MLA + 4, i, 4)

                with e.Fori(0, 8) as i:
                    e.wait_ge(bb_ready, i + 1)
                    for z in range(2):
                        for j in range(S_IT):
                            ins = e.transpose(banks[:, z, j * P:(j + 1) * P], bb[:, z, j], const[:, C_ID:C_ID + P])
                    ins.then_inc(bb_turned, 1)
                    e.wait_ge(bT_ready, i + 1)
                    for z in range(2):
                        for j in range(S_IT):
                            ins = e.matmul(banks[:, 4 * z + j, 0:N], bT[:, z, j], ucur[:], start=True, stop=True)
                    ins.then_inc(bu_ready, 1)
                    e.wait_ge(s5_x, i + 1)
                    for z, xs in enumerate((w_re, w_im)):
                        for j in range(S_IT):
                            ins = e.matmul(banks[:, 0, 0:N], cpd[:, z, j], xs[:, j, :], start=z == 0 and j == 0,
                                           stop=z == 1 and j == S_IT - 1)
                    ins.then_inc(s5_y, 1)
                e.wait_ge(gy_split, 2)
                for w in range(2):
                    for k in range(4):
                        products(e, CH_GLU + 4 * w + k, w, 2, WIN, 4, gyhi, gylo, 2 * k, k == 0, k == 3)
                e.wait_ge(ya_split, 2)
                e.wait_ge(ys_split, 1)
                e.wait_ge(half_free[0], GR_MERGE[0])
                e.wait_ge(half_free[1], GR_MERGE[1])
                e.wait_ge(hf_lo, AP["mix2"] + 8)
                acts = {"ssm": (yshi, yslo), "mla": (yahi, yalo), "mem": (ymhi, ymlo)}
                with e.Fori(0, 4) as i:
                    seen = [0, 0]
                    for j, (kind, b, k) in enumerate(merge_order()):
                        if kind == "gate":
                            if k == 0:
                                wait(e, half_free[0], GR_MERGE[0] + seen[0], i, 5)
                                seen[0] += 1
                            products(e, CH_MERGE + j, 0, 2, WIN, 4, hhi, hlo, 2 * k, k == 0, k == 7, N, i, 48)
                        elif kind == "branch":
                            name, nch, n, _ = BR[b]
                            if k == 0:
                                wait(e, half_free[1], GR_MERGE[1] + seen[1], i, 5)
                                seen[1] += 1
                            products(e, CH_MERGE + j, 1, n, WIN, 4, *acts[name], n * k, k == 0, k == nch - 1, N, i, 48)
                        else:
                            half = (k // 2) % 2
                            if k == 0:
                                wait(e, m_split, 1, i, 1)
                            if k % 2 == 0:
                                wait(e, half_free[half], GR_MERGE[half] + seen[half], i, 5)
                                seen[half] += 1
                            products(e, CH_MERGE + j, half, 2, WIN, 4, mhi, mlo, 2 * (k % 2), k % 2 == 0, k % 2 == 1,
                                     N, i, 48)
                ffn("ffn2", CH_FFN2, GR_FFN2)
                e.wait_ge(half_free[0], GR_END[0])
                e.wait_ge(half_free[1], GR_END[1])
                sums("fin", 8)

            @block.vector
            def _(e):
                links = [0, None, 0]

                def link(ins):
                    links[0] += 1
                    ins.then_inc(dve_link, 1)
                    wait(e, dve_link, links[0], links[1], links[2])

                @contextmanager
                def loop(trips, links_a_pass):
                    start = links[0]
                    with e.Fori(0, trips) as i:
                        links[1:] = [i, links_a_pass]
                        yield i
                    assert links[0] - start == links_a_pass, (links[0] - start, links_a_pass)
                    links[0] = start + trips * links_a_pass
                    links[1:] = [None, 0]

                def mean_inv(name, pairs, dim, cols=N):
                    e.wait_ge(sq_used, SQ[name] + pairs)
                    e.tensor_scalar(mean[:, 0:cols], banks[:, 0, 0:cols], 1.0 / dim, EPS, ALU.mult,
                                    ALU.add).then_inc(mean_ready, 1)
                    e.wait_ge(mean_ready, 2 * NORM[name] + 1)
                    e.reciprocal(mean[:, 0:cols], mean[:, 0:cols]).then_inc(mean_ready, 1)

                def apply(name, src, rs, g, pairs, cols=N):
                    for p in range(pairs):
                        if AP[name] + p >= 2:
                            e.wait_ge(hf_lo, AP[name] + p - 1 if name != "fin" else AP[name])
                        if name == "fin" and p >= 2:
                            e.wait_ge(y_out[p % 2], 16 * (p // 2))
                        for q in range(2):
                            t = 2 * p + q
                            ins = e.scalar_tensor_tensor(out=hf[:, p % 2, q, 0:cols], in0=src[:, t, 0:cols],
                                                         scalar=gains[:, g + t:g + t + 1], in1=rs[:, 0:cols],
                                                         op0=ALU.mult, op1=ALU.mult)
                        ins.then_inc(hf_ready, 1)

                def tt(out, a, b, op):
                    link(e.tensor_tensor(out, a, b, op))

                def ts(out, a, s1, op0, s2=None, op1=ALU.bypass):
                    link(e.tensor_scalar(out, a, s1, s2, op0, op1))

                link(e.memset(stats[:], 1.0))
                e.wait_ge(const_in, 48)
                v = [s5v[:, r] for r in range(18)]
                are, aim = s5p[:, S_ARE], s5p[:, S_AIM]
                e.wait_ge(s5_exp, 1)
                e.tensor_tensor(v[V_AR], are, v[V_DT], ALU.mult).then_inc(s5_arg, 1)
                tt(v[V_PH], aim, v[V_DT], ALU.mult)
                two_pi = 2 * np.pi
                c1 = 6.28125
                c2 = float(np.round((two_pi - c1) * 2 ** 20) / 2 ** 20)
                c3 = two_pi - c1 - c2
                for quarter, out in ((0.0, v[V_PS]), (0.25, v[V_PC])):
                    ts(v[V_K], v[V_PH], 1 / two_pi, ALU.mult, quarter, ALU.add)
                    ts(v[V_K], v[V_K], 12582912.0, ALU.add)
                    ts(v[V_K], v[V_K], 12582912.0, ALU.subtract)
                    src = v[V_PH]
                    for c in (c1, c2, c3):
                        link(e.scalar_tensor_tensor(out=out, in0=v[V_K], scalar=-c, in1=src, op0=ALU.mult, op1=ALU.add))
                        src = out
                    ts(out, out, two_pi * quarter, ALU.add)
                    ins = e.tensor_scalar(out, out, 3.1415925, -3.1415925, ALU.min, ALU.max)
                    if quarter:
                        ins.then_inc(s5_arg, 1)
                    else:
                        link(ins)
                e.wait_ge(s5_sin, 2)
                tt(v[V_LRE], v[V_R], v[V_C1], ALU.mult)
                tt(v[V_LIM], v[V_R], v[V_S1], ALU.mult)
                tt(v[V_INV], are, are, ALU.mult)
                tt(v[V_T], aim, aim, ALU.mult)
                tt(v[V_INV], v[V_INV], v[V_T], ALU.add)
                link(e.reciprocal(v[V_INV], v[V_INV]))
                ts(v[V_NR], v[V_LRE], 1.0, ALU.subtract)
                for out, a, b, op in ((V_ZRE, (v[V_NR], are), (v[V_LIM], aim), ALU.add),
                                      (V_ZIM, (v[V_LIM], are), (v[V_NR], aim), ALU.subtract)):
                    tt(v[out], a[0], a[1], ALU.mult)
                    tt(v[V_T], b[0], b[1], ALU.mult)
                    tt(v[out], v[out], v[V_T], op)
                    tt(v[out], v[out], v[V_INV], ALU.mult)
                for out, h_a, h_b, op in ((V_L0R, S_H0RE, S_H0IM, ALU.subtract), (V_L0I, S_H0IM, S_H0RE, ALU.add)):
                    tt(v[out], v[V_LRE], s5p[:, h_a], ALU.mult)
                    tt(v[V_T], v[V_LIM], s5p[:, h_b], ALU.mult)
                    tt(v[out], v[out], v[V_T], op)

                e.wait_ge(mem_in, 16)
                mean_inv("mem", 8, D, 256)
                e.wait_ge(rstd_ready, 1)
                apply("mem", memT, rstd, G_MEM, 8, 256)
                e.wait_ge(w_used, CH_MEM + 8)
                e.tensor_copy(mkT[:, :, 0:256], banks[:, 0:4, 0:256]).then_inc(half_free[0], 1)
                e.wait_ge(w_used, CH_MEM + 16)
                e.tensor_copy(mv[:, 0:2, :], banks[:, 4:6, :]).then_inc(half_free[1], 1)

                def add_down(half, w, scale, i=None, per=0):
                    for m in range(4):
                        ins = e.scalar_tensor_tensor(out=x[:, 4 * w + m], in0=banks[:, 4 * half + m, 0:N], scalar=scale,
                                                     in1=x[:, 4 * w + m], op0=ALU.mult, op1=ALU.add)
                    ins.then_inc(half_free[half], 1)

                def ffn(name, c0, gr, g):
                    if name == "ffn1":
                        e.wait_ge(x_in, 16)
                    else:
                        e.wait_ge(half_free[0], gr[0])
                        e.wait_ge(half_free[1], gr[1])
                    mean_inv(name, 8, D)
                    e.wait_ge(rstd_ready, NORM[name] + 1)
                    apply(name, x, rstd, g, 8)
                    base = 0 if name == "ffn1" else FFN_BLOCKS

                    def visit(c, kind, k, b, i, per, step):
                        body = step == "body"
                        if kind == "up" and k == 7:
                            wait(e, half_free[0], gr[0] + (2 if body else 1), i, 3)
                            wait(e, w_used, c + 1, i, per)
                            for m in range(4):
                                ins = e.tensor_tensor(prod[:, m], banks[:, 4 + m, 0:N], silu_g[:, m], ALU.mult)
                            ins.then_inc(half_free[1], 1)
                            wait(e, half_free[1], gr[1] + (4 if body else 1), i, 3)
                            e.tensor_copy(phi[:], prod[:]).then_inc(prod_hi, 1)
                            wait(e, prod_hi, base + (2 if body else 1), i, 1)
                            e.tensor_tensor(plo[:], prod[:], phi[:].bitcast(F32), ALU.subtract).then_inc(prod_lo, 1)
                        if kind == "down" and k % 2 == 1:
                            w = k // 2
                            half = (1, 0, 1, 0)[w] if body else (0, 1, 0, 1)[w]
                            wait(e, w_used, c + 1, i, per)
                            add_down(half, w, 0.5)
                    ffn_stream(e, c0, visit)

                ffn("ffn1", CH_FFN1, GR_FFN1, G_FFN1)
                e.wait_ge(half_free[0], GR_Z[0])
                e.wait_ge(half_free[1], GR_Z[1])
                mean_inv("mix", 8, D)
                e.wait_ge(rstd_ready, NORM["mix"] + 1)
                apply("mix", x, rstd_mix, G_MIX, 8)
                z_out = [u[:, 0:4], u[:, 4:8], cqT[:, 0:4], cqT[:, 4:6], ckvT[:], krraw[:], qmT[:]]
                for w, (c_at, width, half) in enumerate(Z_WIN):
                    e.wait_ge(w_used, CH_Z + 8 * (w + 1))
                    n = width // P
                    src = banks[:, 4 * half:4 * half + n, 0:N] if n > 1 else banks[:, 4 * half, 0:N]
                    e.tensor_copy(z_out[w], src).then_inc(half_free[half], 1)

                def heads(att, h0_, p_sb, pT, out, i=None):
                    nt = 3

                    def biggest(h):
                        wait(e, scores, h0_ + h + 1, i, 4)
                        for t, (q0, nq, k0, nk, bank, col) in enumerate(att["tiles"]):
                            ins = e.reduce_max(stats[0:nq, 0, t:t + 1], banks[0:nq, bank, col:col + nk], AX_X)
                        link(ins)
                        e.tensor_scalar(stats[:, 1, 0:nt], stats[:, 0, 0:nt], -att["scale"], None,
                                        ALU.mult).then_inc(max_ready, 1)

                    biggest(0)
                    for h in range(4):
                        wait(e, exp_ready, h0_ + h + 1, i, 4)
                        link(e.reciprocal(stats[:, 3, 0:nt], stats[:, 2, 0:nt]))
                        for t, (q0, nq, k0, nk, bank, col) in enumerate(att["tiles"]):
                            a = p_sb[h % 2][0:nq, att["pcols"][t]:att["pcols"][t] + nk]
                            ins = e.tensor_scalar(a, a, stats[0:nq, 3, t:t + 1], None, ALU.mult)
                        ins.then_inc(p_ready, 1)
                        if h < 3:
                            biggest(h + 1)
                        wait(e, p_turned, h0_ + h + 1, i, 4)
                        sp_, last = att["split"], att["last_rows"]
                        e.tensor_copy(pT[:, 0:sp_], banks[:, 2, 0:sp_])
                        e.tensor_copy(pT[:, sp_:sp_ + 64], banks[:, 3, 0:64])
                        e.tensor_copy(pT[0:last, sp_ + 64:sp_ + 128], banks[0:last, 3, 64:128]).then_inc(pT_ready, 1)
                        wait(e, pv_done, h0_ + h + 1, i, 4)
                        o = out(h)
                        src = banks[:, 4, 0:N]
                        if len(o.shape) == 3:
                            src = src.rearrange("p (o n) -> p o n", o=1)
                        e.tensor_copy(o, src).then_inc(pv_out, 1)

                heads(MEM_ATT, AT_MEM, mem_p, mem_pT, lambda h: ymf[:, h, :])
                e.wait_ge(pv_out, MEM_HEADS)
                e.tensor_copy(ymhi[:], ymf[:]).then_inc(ym_split, 1)
                e.wait_ge(ym_split, 1)
                e.tensor_tensor(ymlo[:], ymf[:], ymhi[:].bitcast(F32), ALU.subtract).then_inc(ym_split, 1)
                cos, sin = const[:, C_COS:C_COS + N], const[:, C_SIN:C_SIN + N]
                tt(krot[:], krraw[:], cos, ALU.mult)
                e.wait_ge(kr_turned, 1)
                tt(mean[:], banks[:, 5, 0:N], sin, ALU.mult)
                e.tensor_tensor(krot[:], krot[:], mean[:], ALU.add).then_inc(kr_rotated, 1)
                e.wait_ge(kr_rotated, 1)
                e.memset(kr[64:128, 0, :], 0.0)
                e.memset(kr[0:64, 1, :], 0.0)
                for z in range(2):
                    r = slice(64 * z, 64 * z + 64)
                    e.tensor_copy(kr[r, z, 0:N_P], krot[r, 0:N_P])
                    ins = e.tensor_copy(kr[r, z, N_P + PAST:KEYS], krot[r, N_P:N])
                ins.then_inc(kr_rotated, 1)
                mean_inv("q", 3, Q_LORA)
                e.wait_ge(rstd_ready, NORM["q"] + 1)
                apply("q", cqT, rstd, G_Q, 3)
                mean_inv("kv", 2, KV_LORA)
                e.wait_ge(rstd_ready, NORM["kv"] + 1)
                for p in range(2):
                    for q in range(2):
                        t = 2 * p + q
                        ins = e.scalar_tensor_tensor(out=latf[:, t], in0=ckvT[:, t], scalar=gains[:, G_KV + t:G_KV + t + 1],
                                                     in1=rstd[:], op0=ALU.mult, op1=ALU.mult)
                    ins.then_inc(hf_ready, 1)
                with loop(4, MLA_LINKS) as i:
                    for un in range(2):
                        wait(e, w_used, CH_MLA + 4 * un + 4, i, 12)
                        e.tensor_copy(qn[:, 2 * un:2 * un + 2, :], banks[:, 4 * un:4 * un + 2, 0:N])
                        e.tensor_copy(qraw[:, un], banks[:, 4 * un + 2, 0:N]).then_inc(half_free[un], 1)
                    wait(e, w_used, CH_MLA + 10, i, 12)
                    e.tensor_copy(kn[:], banks[:, 0:4, 0:KEYS]).then_inc(half_free[0], 1)
                    wait(e, w_used, CH_MLA + 12, i, 12)
                    e.tensor_copy(vv[:], banks[:, 4:8, :]).then_inc(half_free[1], 1)
                    for un in range(2):
                        tt(qrope[:, un], qraw[:, un], cos, ALU.mult)
                        wait(e, q_turned, un + 1, i, 2)
                        tt(mean[:], banks[:, 5 + un, 0:N], sin, ALU.mult)
                        e.tensor_tensor(qrope[:, un], qrope[:, un], mean[:], ALU.add).then_inc(q_rotated, 1)
                    at = e.snap(i * 4)
                    heads(MLA_ATT, AT_MLA, mla_p, mla_pT, lambda h: ymla[:, bass.ds(at + h, 1), :], i)
                e.wait_ge(pv_out, AT_MLA + 16)
                with loop(8, S5_LINKS) as i:
                    at = e.snap(i * S_IT)
                    one = e.snap(i * 1)
                    link(e.tensor_copy(cur[:], s5v[:, V_C1:V_L0I + 1, bass.ds(at, S_IT)]))
                    e.tensor_copy(ucur[:].rearrange("p (o n) -> p o n", o=1), u[:, bass.ds(one, 1), :])
                    wait(e, s5_in, 64, i, 64)
                    for j in range(S_IT):
                        zr, zi = cur[:, V_ZRE, j:j + 1], cur[:, V_ZIM, j:j + 1]
                        e.tensor_scalar(bb[:, 0, j], brw[:, 1, j], zi, None, ALU.mult)
                        ins = e.tensor_scalar(bb[:, 1, j], brw[:, 0, j], zi, None, ALU.mult)
                    link(ins)
                    for j in range(S_IT):
                        zr = cur[:, V_ZRE, j:j + 1]
                        e.scalar_tensor_tensor(out=bb[:, 0, j], in0=brw[:, 0, j], scalar=zr, in1=bb[:, 0, j],
                                               op0=ALU.mult, op1=ALU.subtract)
                        ins = e.scalar_tensor_tensor(out=bb[:, 1, j], in0=brw[:, 1, j], scalar=zr, in1=bb[:, 1, j],
                                                     op0=ALU.mult, op1=ALU.add)
                    ins.then_inc(bb_ready, 1)
                    col = lambda t, k: t[:, :, k:k + 1]
                    grow = lambda a, n: a.rearrange("p (j o) -> p j o", o=1).broadcast_to([P, S_IT, n])
                    e.memset(ec[:, :, 0:1], 1.0)
                    e.memset(es[:, :, 0:1], 0.0)
                    link(e.tensor_copy(pw[:, 0:2, :], cur[:, V_C1:V_S1 + 1, :]))
                    for k in range(8):
                        n = 1 << k
                        a_c, a_s, b_c, b_s = ec[:, :, 0:n], es[:, :, 0:n], ec[:, :, n:2 * n], es[:, :, n:2 * n]
                        pc, ps = grow(pw[:, 0], n), grow(pw[:, 1], n)
                        e.tensor_tensor(b_c, a_c, pc, ALU.mult)
                        e.tensor_tensor(b_s, a_c, ps, ALU.mult)
                        e.tensor_tensor(s_t[:, :, 0:n], a_s, ps, ALU.mult)
                        e.tensor_tensor(v_re[:, :, 0:n], a_s, pc, ALU.mult)
                        if k < 7:
                            e.tensor_tensor(pw[:, 2], pw[:, 0], pw[:, 0], ALU.mult)
                            e.tensor_tensor(pw[:, 3], pw[:, 1], pw[:, 1], ALU.mult)
                            link(e.tensor_tensor(pw[:, 4], pw[:, 0], pw[:, 1], ALU.mult))
                            e.tensor_tensor(pw[:, 0], pw[:, 2], pw[:, 3], ALU.subtract)
                            e.tensor_scalar(pw[:, 1], pw[:, 4], 2.0, None, ALU.mult)
                        else:
                            link(e.memset(dec[:, :, 0:1], 0.0))
                        e.tensor_tensor(b_c, b_c, s_t[:, :, 0:n], ALU.subtract)
                        link(e.tensor_tensor(b_s, b_s, v_re[:, :, 0:n], ALU.add))
                    e.tensor_copy(ec[:, :, N_P:N], ec[:, :, 0:N_S])
                    e.tensor_copy(es[:, :, N_P:N], es[:, :, 0:N_S])
                    link(e.tensor_copy(dec[:], grow(cur[:, V_R], N)))
                    e.memset(dec[:, :, 0:1], 0.0)
                    link(e.memset(dec[:, :, N_P:N_P + 1], 0.0))
                    wait(e, bb_turned, 1, i, 1)
                    e.tensor_copy(bT[:, 0], banks[:, 0, :].rearrange("p (j c) -> p j c", j=S_IT))
                    e.tensor_copy(bT[:, 1], banks[:, 1, :].rearrange("p (j c) -> p j c", j=S_IT)).then_inc(bT_ready, 1)
                    b_re, b_im = banks[:, 0:4, 0:N], banks[:, 4:8, 0:N]
                    wait(e, bu_ready, 1, i, 1)
                    e.tensor_tensor(s_t[:], b_re, ec[:], ALU.mult)
                    e.tensor_tensor(w_re[:], b_im, es[:], ALU.mult)
                    e.tensor_tensor(w_im[:], b_im, ec[:], ALU.mult)
                    link(e.tensor_tensor(v_re[:], b_re, es[:], ALU.mult))
                    e.tensor_tensor(w_re[:], s_t[:], w_re[:], ALU.add)
                    link(e.tensor_tensor(w_im[:], w_im[:], v_re[:], ALU.subtract))
                    g1 = lambda a: a.rearrange("p (j o) -> p j o", o=1)
                    e.tensor_tensor(w_re[:, :, N_P:N_P + 1], w_re[:, :, N_P:N_P + 1], g1(cur[:, V_L0R]), ALU.add)
                    link(e.tensor_tensor(w_im[:, :, N_P:N_P + 1], w_im[:, :, N_P:N_P + 1], g1(cur[:, V_L0I]), ALU.add))
                    flat = lambda t: t[:].rearrange("p j n -> p (j n)")
                    e.tensor_tensor_scan(flat(v_re), flat(dec), flat(w_re), 0.0, ALU.mult, ALU.add)
                    link(e.tensor_tensor_scan(flat(v_im), flat(dec), flat(w_im), 0.0, ALU.mult, ALU.add))
                    e.tensor_tensor(s_t[:], v_re[:], ec[:], ALU.mult)
                    link(e.tensor_tensor(w_re[:], v_im[:], es[:], ALU.mult))
                    link(e.tensor_tensor(w_re[:], s_t[:], w_re[:], ALU.subtract))
                    e.tensor_tensor(s_t[:], v_re[:], es[:], ALU.mult)
                    link(e.tensor_tensor(w_im[:], v_im[:], ec[:], ALU.mult))
                    e.scalar_tensor_tensor(out=w_im[:], in0=s_t[:], scalar=-1.0, in1=w_im[:], op0=ALU.mult,
                                           op1=ALU.subtract).then_inc(s5_x, 1)
                    wait(e, s5_x, 1, i, 1)
                    for z, xs in enumerate((w_re, w_im)):
                        for s, last in enumerate((N_P - 1, N - 1)):
                            e.tensor_scalar(g1(states[:, 2 * s + z, bass.ds(at, S_IT)]), xs[:, :, last:last + 1],
                                            1.0 - 2 * z, None, ALU.mult)
                    wait(e, s5_y, 1, i, 1)
                    link(e.tensor_scalar(s_t[:, 0], ucur[:], gains[:, bass.ds(one + G_D, 1)], None, ALU.mult))
                    e.tensor_tensor(ycur[:], banks[:, 0, 0:N], s_t[:, 0], ALU.add).then_inc(ycur_ready, 1)
                    wait(e, gelu_ready, 1, i, 1)
                e.wait_ge(gelu_ready, 8)
                e.tensor_copy(gyhi[:], u[:]).then_inc(gy_split, 1)
                e.wait_ge(gy_split, 1)
                e.tensor_tensor(gylo[:], u[:], gyhi[:].bitcast(F32), ALU.subtract).then_inc(gy_split, 1)
                for w in range(2):
                    e.wait_ge(half_free[w], GR_GLU[w] + 1)
                    e.tensor_tensor(u[:, 4 * w:4 * w + 4], u[:, 4 * w:4 * w + 4], sgl[:], ALU.mult).then_inc(ys_half, 1)
                e.wait_ge(ys_half, 2)
                link(e.tensor_copy(yshi[:], u[:]))
                e.tensor_tensor(yslo[:], u[:], yshi[:].bitcast(F32), ALU.subtract).then_inc(ys_split, 1)
                apply("mix2", x, rstd_mix, G_MIX, 8)
                e.tensor_copy(yahi[:], ymla[:]).then_inc(ya_split, 1)
                e.wait_ge(ya_split, 1)
                e.tensor_tensor(yalo[:], ymla[:], yahi[:].bitcast(F32), ALU.subtract).then_inc(ya_split, 1)
                with loop(4, MERGE_LINKS) as i:
                    branch = -1
                    for j, (kind, b, k) in enumerate(merge_order()):
                        if kind == "branch" and k == BR[b][1] - 1:
                            wait(e, half_free[0], GR_MERGE[0] + b + 1, i, 5)
                            wait(e, w_used, CH_MERGE + j + 1, i, 48)
                            dst = merged if b == 0 else gate
                            for m in range(4):
                                ins = e.tensor_tensor(dst[:, m], banks[:, 4 + m, 0:N], gate[:, m], ALU.mult)
                            if b:
                                link(ins)
                                ins = e.tensor_tensor(merged[:], merged[:], gate[:], ALU.add)
                            ins.then_inc(half_free[1], 1)
                            wait(e, half_free[1], GR_MERGE[1] + b + 1, i, 5)
                            if b == 2:
                                link(e.tensor_copy(mhi[:], merged[:]))
                                e.tensor_tensor(mlo[:], merged[:], mhi[:].bitcast(F32), ALU.subtract).then_inc(m_split, 1)
                        if kind == "out" and k % 2 == 1:
                            wait(e, w_used, CH_MERGE + j + 1, i, 48)
                            add_down((k // 2) % 2, k // 2, 1.0)
                ffn("ffn2", CH_FFN2, GR_FFN2, G_FFN2)
                e.wait_ge(half_free[0], GR_END[0])
                e.wait_ge(half_free[1], GR_END[1])
                mean_inv("fin", 8, D)
                e.wait_ge(rstd_ready, NORM["fin"] + 1)
                apply("fin", x, rstd, G_FIN, 8)


_OUT = {"yT": (D, N), "latT": (KV_LORA, N), "krT": (ROPE, N), "mkT": (MEM_W, 256), "mv": (256, MEM_W),
        "states": (P, 4, S_TILES)}


def _constants():
    c = np.zeros((P, C_COLS), np.float32)
    c[:, C_ID:C_ID + P] = np.eye(P, dtype=np.float32)
    for b in (0, 64):
        for r in range(32):
            c[b + 32 + r, C_PERM + b + r] = -1.0
            c[b + r, C_PERM + b + 32 + r] = 1.0
    half = ROPE // 2
    inv = np.float32(10000.0) ** (-np.arange(half, dtype=np.float32) / np.float32(half))
    pos = np.concatenate([np.arange(N_P), PAST + np.arange(N_S)]).astype(np.float32)
    ang = (inv[:, None] * pos[None, :]).astype(np.float32)
    c[:, C_COS:C_COS + N] = np.tile(np.cos(ang), (4, 1))
    c[:, C_SIN:C_SIN + N] = np.tile(np.sin(ang), (4, 1))
    c[0, C_HALF:C_HALF + 64] = 1.0
    c[0, C_MASK + 192:C_MASK + 256] = -1e30
    return c


def kernel(**inp):
    import concourse.bacc as bacc
    from concourse.bass_utils import run_bass_kernel_spmd as run
    a = {k: np.asarray(v) for k, v in inp.items()}
    col = lambda v: v.reshape(-1, P)
    gains = np.concatenate([col(a["ffn1_norm"]), col(a["mix_norm"]), col(a["ffn2_norm"]), col(a["final_norm"]),
                            col(a["mem_norm"]), col(a["q_norm"]), col(a["kv_norm"]), col(a["ssm_b_glu"]),
                            col(a["ssm_d"])]).T
    modes = lambda v: v.reshape(S_TILES, P).T
    ldt = np.repeat(a["ssm_log_dt"][0], 64)
    s5p = np.stack([modes(a["ssm_a_re"]), modes(a["ssm_a_im"]), modes(ldt), modes(a["state_ssm_re"]),
                    modes(a["state_ssm_im"])], axis=1)

    def blocks(v):
        out = np.zeros((2, 64, S_TILES, 4, 2, 16), np.float32)
        w = v.reshape(S_TILES, 2, 64, 16)
        for t in range(S_TILES):
            for g in range(2):
                out[g, :, t, t % 4, g, :] = w[t, g]
        return out.reshape(P, S_TILES, P)

    w_in = a["w_in"][0]
    arrays = {
        "const": _constants(), "gains": gains, "s5p": s5p,
        "xT": np.concatenate([a["x_prompt"][0], a["x_sample"][0]]).T,
        "memT": a["mem_prompt"][0].T,
        "cmkT": a["cache_mem_k"].reshape(256, MEM_W).T, "cmv": a["cache_mem_v"].reshape(256, MEM_W),
        "platT": a["cache_kv_latent"][0, 0].T, "pkrT": a["cache_k_rope"][0, 0].T,
        "bp_re": blocks(a["ssm_b_re"][0]), "bp_im": blocks(a["ssm_b_im"][0]),
        "cp_re": blocks(a["ssm_c_re"][0].transpose(0, 2, 1)), "cp_im": blocks(a["ssm_c_im"][0].transpose(0, 2, 1)),
        "w_in": w_in, "w_kr2": np.concatenate([w_in[:, COL_KR:COL_QM]] * 2, axis=1),
    }
    arrays["w_post"] = np.concatenate([a[n][0] for n in ("w_out", "w_br_ssm", "w_br_mla", "w_br_mem")])
    uq = a["w_uq"][0].reshape(Q_LORA, HEADS // 2, 2, NOPE + ROPE)
    arrays["w_uq"] = np.concatenate([uq[..., :NOPE].reshape(Q_LORA, HEADS // 2, 2 * NOPE),
                                     uq[..., NOPE:].reshape(Q_LORA, HEADS // 2, 2 * ROPE)], axis=2).reshape(Q_LORA, -1)
    for name in ("w_mem_k", "w_mem_v", "ffn1_w_gate", "ffn1_w_up", "ffn1_w_down", "w_uk", "w_uv", "ssm_w_glu",
                 "ffn2_w_gate", "ffn2_w_up", "ffn2_w_down"):
        arrays[name] = a[name][0]
    nc = bacc.Bacc("TRN2", target_bir_lowering=False, num_devices=1)
    t_in, feed = {}, {}
    for name, v in arrays.items():
        feed["i_" + name] = np.ascontiguousarray(v)
        t_in[name] = nc.dram_tensor("i_" + name, v.shape, F32, kind="ExternalInput").ap()
    t_out = {n: nc.dram_tensor("o_" + n, s, F32, kind="ExternalOutput").ap() for n, s in _OUT.items()}
    build(nc, t_in, t_out)
    r = run(nc, [feed], core_ids=[0]).results[0]
    y, lat, kr = (np.asarray(r["o_" + n]).T for n in ("yT", "latT", "krT"))
    st = np.asarray(r["o_states"]).transpose(1, 2, 0).reshape(4, 1, 1, 64, 64)
    cut = lambda v: (v[None, :N_P], v[None, N_P:])
    (y_p, y_s), (l_p, l_s), (k_p, k_s) = cut(y), cut(lat), cut(kr)
    mk = np.asarray(r["o_mkT"]).T.reshape(1, 1, 256, MEM_HEADS, HD)
    mv = np.asarray(r["o_mv"]).reshape(1, 1, 256, MEM_HEADS, HD)
    return tuple(np.ascontiguousarray(v) for v in (
        y_p, y_s, l_p[None], k_p[None], mk, mv, st[0], st[1], l_s[None], k_s[None], st[2], st[3]))
```

```python
from contextlib import ExitStack, contextmanager

import numpy as np
import concourse.bass as bass
from concourse import mybir

F32 = mybir.dt.float32
F32R = mybir.dt.float32r
ACT = mybir.ActivationFunctionType
ALU = mybir.AluOpType
AX_X = mybir.AxisListType.X

P = 128
D = 2048
KD = D // P
N_P, N_S = 256, 64
N = N_P + N_S
PAST = 128
KEYS = N_P + PAST + N_S
D_FF = 5632
WIN = 512
FFN_BLOCKS = D_FF // WIN
SSM_W, Q_LORA, KV_LORA, ROPE, MEM_W = 1024, 768, 512, 64, 512
NOPE, HEADS, MEM_HEADS, HD = 128, 16, 4, 128
COL_Q = SSM_W
COL_KV = COL_Q + Q_LORA
COL_KR = COL_KV + KV_LORA
COL_QM = COL_KR + ROPE
COL_GATE = COL_QM + MEM_W
EPS = 1e-6
MLA_SCALE = (NOPE + ROPE) ** -0.5
MEM_SCALE = HD ** -0.5
S_TILES = 32
S_IT = 4
S_STEPS = S_TILES // S_IT
T_BLK = 4
B_P, B_S = N_P // T_BLK, N_S // T_BLK
BLKS = B_P + 1 + B_S
RAW, SPL = 3, 4

G_FFN1, G_MIX, G_FFN2, G_FIN, G_MEM, G_Q, G_KV, G_BGLU, G_D = 0, 16, 32, 48, 64, 80, 86, 90, 98
G_COLS = 98 + S_TILES
C_ID, C_PERM, C_COS, C_SIN, C_HALF, C_MASK = 0, 128, 256, 576, 896, 1024
C_COLS = 1280
S_ARE, S_AIM, S_LDT, S_H0RE, S_H0IM = range(5)
(V_ZRE, V_LRE, V_ZIM, V_LIM, V_NZRE, V_NLRE, V_L2RE, V_L2IM, V_R4, V_C1, V_S1, V_R, V_DT, V_AR, V_PH, V_PS, V_PC,
 V_K, V_INV, V_T, V_NR, V_T2) = range(22)

FFN_CH = 24 * FFN_BLOCKS
CH_MEM = 0
CH_FFN1 = CH_MEM + 16
CH_Z = CH_FFN1 + FFN_CH
CH_MLA = CH_Z + 56
CH_GLU = CH_MLA + 4 * 12
CH_MERGE = CH_GLU + 8
CH_FFN2 = CH_MERGE + 4 * 48
CH_END = CH_FFN2 + FFN_CH
GR_MEM = (0, 0)
GR_FFN1 = (1, 1)
GR_Z = (1 + 33, 1 + 33)
GR_MLA = (GR_Z[0] + 6, GR_Z[1] + 1)
GR_GLU = (GR_MLA[0] + 8, GR_MLA[1] + 8)
GR_MERGE = (GR_GLU[0] + 1, GR_GLU[1] + 1)
GR_FFN2 = (GR_MERGE[0] + 20, GR_MERGE[1] + 20)
GR_END = (GR_FFN2[0] + 33, GR_FFN2[1] + 33)
SQ = {"mem": 0, "ffn1": 8, "mix": 16, "q": 24, "kv": 27, "ffn2": 29, "fin": 37}
AP = {"mem": 0, "ffn1": 8, "mix": 16, "q": 24, "kv": 27, "mix2": 29, "ffn2": 37, "fin": 45}
NORM = {"mem": 0, "ffn1": 1, "mix": 2, "q": 3, "kv": 4, "ffn2": 5, "fin": 6}
MLA_LINKS, MERGE_LINKS = 12, 3
AT_MEM, AT_MLA = 0, MEM_HEADS

MLA_ATT = dict(
    tiles=[(0, 128, 0, 128, 0, 0), (128, 128, 0, 256, 0, 128), (256, 64, 256, 192, 1, 0)],
    pcols=[0, 128, 384],
    turns=[(0, 0, 128, 2, 0), (1, 0, 128, 2, 128), (1, 128, 128, 2, 256), (2, 0, 128, 3, 0), (2, 128, 64, 3, 64)],
    pv=[(0, 128, 0, 256, 0, True, False), (1, 128, 256, 128, 128, False, True),
        (2, 128, 384, 64, 256, True, False), (3, 64, 448, 64, 256, False, True)],
    split=384, total=512, scale=MLA_SCALE, last_rows=64)
MEM_ATT = dict(
    tiles=[(0, 128, 0, 256, 0, 0), (128, 128, 0, 256, 0, 256), (256, 64, 256, 256, 1, 0)],
    pcols=[0, 256, 512],
    turns=[(0, 0, 128, 2, 0), (1, 0, 128, 2, 128), (0, 128, 128, 2, 256), (1, 128, 128, 2, 384),
           (2, 0, 128, 3, 0), (2, 128, 128, 3, 64)],
    pv=[(0, 128, 0, 256, 0, True, False), (1, 128, 256, 256, 0, False, True),
        (2, 128, 512, 64, 256, True, False), (3, 128, 576, 64, 256, False, True)],
    split=512, total=640, scale=MEM_SCALE, last_rows=128)


def build(nc, t_in, t_out):
    with ExitStack() as ctx:
        def psum(name, shape):
            return ctx.enter_context(nc.psum_tensor(name, shape, F32))

        def sem(name):
            return ctx.enter_context(nc.semaphore(name))

        BASE = 16512
        END = nc.sbuf_usable_end

        class Region:

            def __init__(self, at):
                self.at = at

            def take(self, name, cols, dt=F32):
                shape = [P] + (list(cols) if isinstance(cols, (list, tuple)) else [cols])
                size = 4
                for c in shape[1:]:
                    size *= c
                t = nc.alloc_sbuf_tensor_at(name, shape, dt, offset=self.at)
                self.at += (size + 31) // 32 * 32
                assert self.at <= END, (name, self.at, END)
                return t

        R = Region(BASE)
        const = R.take("const", C_COLS)
        ones = R.take("ones", P)
        gains = R.take("gains", G_COLS)
        s5p = R.take("s5p", [5, S_TILES])
        s5v = R.take("s5v", [22, S_TILES])
        states = R.take("states", [4, S_TILES])
        stats = R.take("stats", [4, 4])
        rstd = R.take("rstd", N)
        rstd_mix = R.take("rstd_mix", N)
        mean = R.take("mean", N)
        x = R.take("x", [KD, N])
        raw = R.take("raw", [RAW, 2 * WIN])
        whi = R.take("whi", [SPL, 2 * WIN], F32R)
        wlo = R.take("wlo", [SPL, 2 * WIN], F32R)
        n0 = R.at
        sq = R.take("sq", [2, 2, N])
        hf = R.take("hf", [2, 2, N])
        M = Region(n0)
        gate = M.take("gate", [4, N])
        merged = M.take("merged", [4, N])
        assert M.at <= R.at
        u = Region(n0).take("u", [8, N])
        M = Region(n0)
        s_t = M.take("s_t", [S_IT, BLKS])
        s_t2 = M.take("s_t2", [S_IT, BLKS])
        v_re = M.take("v_re", [S_IT, BLKS])
        v_im = M.take("v_im", [S_IT, BLKS])
        dec = M.take("dec", [S_IT, BLKS])
        ycur = M.take("ycur", [S_IT, BLKS])
        assert M.at <= R.at
        h0 = R.at
        hhi = R.take("hhi", [KD, N], F32R)
        hlo = R.take("hlo", [KD, N], F32R)
        v0 = R.at

        V = Region(v0)
        mkT = V.take("mkT", [MEM_HEADS, 512])
        mv = V.take("mv", [4, MEM_W])
        v16 = V.at
        memT = Region(v16).take("memT", [KD, 256])
        B = Region(v16)
        silu_g = B.take("silu_g", [4, N])
        prod = B.take("prod", [4, N])
        phi = B.take("phi", [4, N], F32R)
        plo = B.take("plo", [4, N], F32R)
        Z = Region(v16)
        cqT = Z.take("cqT", [6, N])
        ckvT = Z.take("ckvT", [4, N])
        krraw = Z.take("krraw", N)
        qmT = Z.take("qmT", [MEM_HEADS, N])
        S = Region(Z.at)
        mem_p = [Z.take(f"mem_p{b}", 768) for b in range(2)]
        mem_pT = Z.take("mem_pT", 640)
        ymf = Z.take("ymf", [4, N])
        assert Z.at <= v0 + 61440
        T = Region(v0 + 61440)
        ymhi = T.take("ymhi", [4, N], F32R)
        ymlo = T.take("ymlo", [4, N], F32R)
        T = Region(v0 + 71680)
        u4 = T.take("u4", [S_TILES, BLKS])
        pq = [S.take(f"pq{b}", [2, T_BLK, 2, S_IT, 16]) for b in range(2)]
        sw = [S.take(f"sw{b}", [8, S_IT, 16]) for b in range(2)]
        elh = S.take("elh", [2, 2, S_TILES, 8])
        bp = S.take("bp", [2, S_IT, T_BLK, 32])
        qp = S.take("qp", [2, S_IT, T_BLK, 32])
        pT = S.take("pT", [2, S_IT, P])
        tz = S.take("tz", [S_IT, P])
        ee = S.take("ee", [2, S_IT, BLKS])
        xs = S.take("xs", [2, S_IT, BLKS + 1])
        assert S.at <= v0 + 71680
        S = Region(v0 + 39680)
        uph = S.take("uph", [6, 2, S_TILES])
        e_t = S.take("e_t", [2, S_TILES, 4])
        assert S.at <= v0 + 43776
        T = Region(v0 + 71680)
        mhi = T.take("mhi", [4, N], F32R)
        mlo = T.take("mlo", [4, N], F32R)
        L = Region(h0)
        cqhi = L.take("cqhi", [6, N], F32R)
        cqlo = L.take("cqlo", [6, N], F32R)
        lathi = L.take("lathi", [4, 512], F32R)
        latlo = L.take("latlo", [4, 512], F32R)
        kr = L.take("kr", [2, KEYS])
        krot = L.take("krot", N)
        assert L.at <= v0
        K1 = Region(v0)
        qn = K1.take("qn", [4, N])
        qraw = K1.take("qraw", [2, N])
        qrope = K1.take("qrope", [2, N])
        kn = K1.take("kn", [4, KEYS])
        mla_p0 = K1.take("mla_p0", 576)
        assert K1.at <= v0 + 20480
        ymla = Region(v0 + 20480).take("ymla", [HEADS, N])
        K2 = Region(v0 + 40960)
        vv = K2.take("vv", [4, WIN])
        mla_pT = K2.take("mla_pT", 512)
        mla_p = [mla_p0, K2.take("mla_p1", 576)]
        past = K2.take("past", [4, PAST])
        latf = K2.take("latf", [4, N])
        assert K2.at <= v0 + 61440
        U = Region(v0)
        yshi = U.take("yshi", [8, N], F32R)
        yslo = U.take("yslo", [8, N], F32R)
        U = Region(h0)
        gyhi = U.take("gyhi", [8, N], F32R)
        gylo = U.take("gylo", [8, N], F32R)
        sgl = Region(v0 + 40960).take("sgl", [4, N])
        yalo = Region(v0 + 20480).take("yalo", [HEADS, N], F32R)
        yahi = Region(v0 + 40960).take("yahi", [HEADS, N], F32R)

        banks = psum("banks", [P, 8, 512])

        const_in = sem("const_in")
        x_in = sem("x_in")
        mem_in = sem("mem_in")
        memkv_in = sem("memkv_in")
        past_in = sem("past_in")
        s5_in = [sem("s5_in0"), sem("s5_in1")]
        raw_in = [sem(f"raw_in{i}") for i in range(RAW)]
        w_hi = sem("w_hi")
        w_lo = sem("w_lo")
        w_used = sem("w_used")
        half_free = [sem("half0_free"), sem("half1_free")]
        ones_set = sem("ones_set")
        sq_ready = sem("sq_ready")
        sq_used = sem("sq_used")
        mean_ready = sem("mean_ready")
        rstd_ready = sem("rstd_ready")
        hf_ready = sem("hf_ready")
        hf_hi = sem("hf_hi")
        hf_lo = sem("hf_lo")
        prod_hi = sem("prod_hi")
        prod_lo = sem("prod_lo")
        past_hi = sem("past_hi")
        past_lo = sem("past_lo")
        lat_out = sem("lat_out")
        y_out = [sem("y_out0"), sem("y_out1")]
        kr_turned = sem("kr_turned")
        kr_rotated = sem("kr_rotated")
        q_turned = sem("q_turned")
        q_rotated = sem("q_rotated")
        scores = sem("scores")
        max_ready = sem("max_ready")
        exp_ready = sem("exp_ready")
        p_ready = sem("p_ready")
        p_turned = sem("p_turned")
        pT_ready = sem("pT_ready")
        pv_done = sem("pv_done")
        pv_out = sem("pv_out")
        ym_split = sem("ym_split")
        dve_link = sem("dve_link")
        s5_exp = sem("s5_exp")
        s5_arg = sem("s5_arg")
        s5_sin = sem("s5_sin")
        pads_set = sem("pads_set")
        pq_ready = sem("pq_ready")
        b_padded = sem("b_padded")
        q_padded = sem("q_padded")
        s5_turned = sem("s5_turned")
        own_ready = sem("own_ready")
        pT_set = sem("pT_set")
        tz_set = sem("tz_set")
        bu_ready = sem("bu_ready")
        bu_read = sem("bu_read")
        s5_x = sem("s5_x")
        s5_y = sem("s5_y")
        ycur_ready = sem("ycur_ready")
        gelu_ready = sem("gelu_ready")
        gy_split = sem("gy_split")
        ys_half = sem("ys_half")
        ys_split = sem("ys_split")
        ya_split = sem("ya_split")
        m_split = sem("m_split")
        stored = sem("stored")

        def wait(e, s, base, i=None, per=0):
            e.wait_ge(s, base if i is None else i * per + base)

        def rows(w, r0, n, c0, width):
            return w[bass.ds(r0, n * P), bass.ds(c0, width)].rearrange("(t p) c -> p t c", p=P)


        def load(e, c, src, n, width, i=None, per=0):
            slot = c % RAW
            if c >= RAW:
                wait(e, w_lo, c - RAW + 1, i, per)
            e.dma_start(raw[:, slot, 0:n * width].rearrange("p (t c) -> p t c", t=n), src).then_inc(raw_in[slot], 16)

        def round_w(e, c, size, i=None, per=0):
            slot = c % RAW
            wait(e, raw_in[slot], 16 * (c // RAW + 1), i, 16 * per // RAW)
            if c >= SPL:
                wait(e, w_used, c - SPL + 1, i, per)
            e.activation(whi[:, c % SPL, 0:size], raw[:, slot, 0:size], ACT.Copy).then_inc(w_hi, 1)

        def split_w(e, c, size, i=None, per=0):
            wait(e, w_hi, c + 1, i, per)
            e.tensor_tensor(wlo[:, c % SPL, 0:size], raw[:, c % RAW, 0:size],
                            whi[:, c % SPL, 0:size].bitcast(F32), ALU.subtract).then_inc(w_lo, 1)

        def three(e, out, hi_s, lo_s, hi_m, lo_m, start, stop):
            e.matmul(out, hi_s, hi_m, start=start, stop=False)
            e.matmul(out, hi_s, lo_m, start=False, stop=False)
            return e.matmul(out, lo_s, hi_m, start=False, stop=stop)

        def products(e, c, half, n, width, tiles, ahi, alo, k, first, last, cols=N, i=None, per=0):
            wait(e, w_lo, c + 1, i, per)
            s = c % SPL
            wh = whi[:, s, 0:n * width].rearrange("p (t c) -> p t c", t=n)
            wl = wlo[:, s, 0:n * width].rearrange("p (t c) -> p t c", t=n)
            for q in range(n):
                for m in range(tiles):
                    a, b = wh[:, q, m * P:(m + 1) * P], wl[:, q, m * P:(m + 1) * P]
                    ins = three(e, banks[:, 4 * half + m, 0:cols], a, b, ahi[:, k + q, 0:cols], alo[:, k + q, 0:cols],
                                first and q == 0, last and q == n - 1)
            ins.then_inc(w_used, 1)

        def token_products(e, c, half, n, tiles, ahi, alo, k, first, last, i=None, per=0):
            wait(e, w_lo, c + 1, i, per)
            s = c % SPL
            wh = whi[:, s, :].rearrange("p (t c) -> p t c", t=n)
            wl = wlo[:, s, :].rearrange("p (t c) -> p t c", t=n)
            for q in range(n):
                for m in range(tiles):
                    o = banks[:, 4 * half + m, :]
                    sl = slice(m * P, (m + 1) * P)
                    e.matmul(o, ahi[:, k + q, sl], wh[:, q, :], start=first and q == 0, stop=False)
                    e.matmul(o, alo[:, k + q, sl], wh[:, q, :], start=False, stop=False)
                    ins = e.matmul(o, ahi[:, k + q, sl], wl[:, q, :], start=False, stop=last and q == n - 1)
            ins.then_inc(w_used, 1)

        def ffn_order(first, last):
            g = [("gate", k) for k in range(8)]
            d = [("down", k) for k in range(8)]
            up = [("up", k) for k in range(8)]
            return g + up if first else d if last else g + d + up

        def ffn_stream(e, c0, visit):
            for j, (kind, k) in enumerate(ffn_order(True, False)):
                visit(c0 + j, kind, k, 0, None, 0, "head")
            with e.Fori(0, FFN_BLOCKS - 1) as i:
                for j, (kind, k) in enumerate(ffn_order(False, False)):
                    visit(c0 + 16 + j, kind, k, i, i, 24, "body")
            ce = c0 + 16 + 24 * (FFN_BLOCKS - 1)
            for j, (kind, k) in enumerate(ffn_order(False, True)):
                visit(ce + j, kind, k, FFN_BLOCKS - 1, None, 0, "tail")

        BR = [("ssm", 4, 2, D), ("mla", 8, 2, D + SSM_W), ("mem", 4, 1, D + SSM_W + HEADS * HD)]

        def merge_order():
            out = []
            for b, (name, nch, n, row) in enumerate(BR):
                out += [("gate", b, k) for k in range(8)]
                out += [("branch", b, k) for k in range(nch)]
            out += [("out", 0, k) for k in range(8)]
            assert len(out) == 48
            return out

        Z_WIN = [(0, 512, 0), (512, 512, 1), (COL_Q, 512, 0), (COL_Q + 512, 256, 0), (COL_KV, 512, 0),
                 (COL_KR, 128, 0), (COL_QM, 512, 0)]

        S5_AT = 16 + 2

        def s5_slots(parts):
            at = {}
            for s in range(S_STEPS):
                for part, after in parts:
                    at.setdefault(min(S5_AT + 5 * s + after, 56), []).append((part, s))
            return at

        MLA_ORDER = ([("uq", un, k, n) for un in range(2) for k, n in ((0, 2), (2, 2), (4, 1), (5, 1))]
                     + [("uk", 0, 0, 2), ("uk", 0, 2, 2), ("uv", 0, 0, 2), ("uv", 0, 2, 2)])
        QW = 2 * (NOPE + ROPE)

        def size_of_mla(kind, n):
            return n * (QW if kind == "uq" else WIN)

        with nc.Block() as block:
            @block.sync
            def _(e):
                e.dma_start(const[:], t_in["const"]).then_inc(const_in, 16)
                e.dma_start(gains[:], t_in["gains"]).then_inc(const_in, 16)
                e.dma_start(s5p[:], t_in["s5p"]).then_inc(const_in, 16)
                e.dma_start(memT[:], t_in["memT"].rearrange("(t p) n -> p t n", p=P)).then_inc(mem_in, 16)
                e.dma_start(x[:], t_in["xT"].rearrange("(t p) n -> p t n", p=P)).then_inc(x_in, 16)
                e.dma_start(mkT[:, :, 256:512], t_in["cmkT"].rearrange("(h p) n -> p h n", p=P)).then_inc(memkv_in, 16)
                e.dma_start(mv[:, 2:4, :], t_in["cmv"].rearrange("(t p) n -> p t n", p=P)).then_inc(memkv_in, 16)
                for w, name in enumerate(("w_mem_k", "w_mem_v")):
                    for k in range(8):
                        load(e, CH_MEM + 8 * w + k, rows(t_in[name], 256 * k, 2, 0, WIN), 2, WIN)

                def ffn_loads(c0, name):
                    def visit(c, kind, k, b, i, per, step):
                        w = t_in[f"{name}_w_{kind}"]
                        if kind == "down":
                            r0 = b * WIN + (k % 2) * 256
                            c_at = (k // 2) * WIN
                        else:
                            r0 = k * 256
                            c_at = 0 if step == "head" else b * WIN + WIN
                        if step == "body":
                            if kind == "down":
                                r0 = e.snap(r0)
                            else:
                                c_at = e.snap(c_at)
                        load(e, c, rows(w, r0, 2, c_at, WIN), 2, WIN, i, per)
                    ffn_stream(e, c0, visit)

                ffn_loads(CH_FFN1, "ffn1")
                e.wait_ge(half_free[0], 1)
                e.wait_ge(half_free[1], 1)
                e.dma_start(t_out["mkT"].rearrange("(h p) n -> p h n", p=P), mkT[:, :, 0:256]).then_inc(stored, 16)
                e.dma_start(t_out["mv"].rearrange("(t p) n -> p t n", p=P), mv[:, 0:2, :]).then_inc(stored, 16)
                def s5_load(s):
                    if s >= 2:
                        e.wait_ge(own_ready, s - 1)
                    e.dma_start(sw[s % 2][:], t_in["s5w"][:, s]).then_inc(s5_in[s % 2], 16)

                s5_load(0)
                s5_load(1)
                c = CH_Z
                for c_at, width, half in Z_WIN:
                    for k in range(8):
                        n = c - CH_Z
                        if n >= S5_AT + 10 - 3 and (n - S5_AT + 3) % 5 == 0 and (n - S5_AT + 3) // 5 < S_STEPS:
                            s5_load((n - S5_AT + 3) // 5)
                        w, at = (t_in["w_kr2"], 0) if width == 128 else (t_in["w_in"], c_at)
                        load(e, c, rows(w, 256 * k, 2, at, width), 2, width)
                        c += 1
                e.wait_ge(pv_out, MEM_HEADS)
                e.dma_start(past[:], t_in["platT"].rearrange("(t p) n -> p t n", p=P)).then_inc(past_in, 16)
                e.dma_start(kr[0:64, 0, N_P:N_P + PAST], t_in["pkrT"]).then_inc(past_in, 16)
                e.dma_start(kr[64:128, 1, N_P:N_P + PAST], t_in["pkrT"]).then_inc(past_in, 16)
                e.wait_ge(hf_ready, AP["kv"] + 2)
                e.dma_start(t_out["latT"].rearrange("(t p) n -> p t n", p=P), latf[:]).then_inc(lat_out, 16)
                e.wait_ge(kr_rotated, 1)
                e.dma_start(t_out["krT"], krot[0:64, :]).then_inc(lat_out, 16)
                with e.Fori(0, 4) as i:
                    for j, (kind, un, k, n) in enumerate(MLA_ORDER):
                        width = QW if kind == "uq" else WIN
                        c_at = e.snap(i * 2 * QW + un * QW) if kind == "uq" else e.snap(i * WIN)
                        load(e, CH_MLA + j, rows(t_in["w_" + kind], k * P, n, c_at, width), n, width, i, 12)
                for w in range(2):
                    for k in range(4):
                        load(e, CH_GLU + 4 * w + k, rows(t_in["ssm_w_glu"], 256 * k, 2, w * WIN, WIN), 2, WIN)
                e.wait_ge(ys_split, 1)
                e.dma_start(t_out["states"], states[:]).then_inc(stored, 16)
                with e.Fori(0, 4) as i:
                    for j, (kind, b, k) in enumerate(merge_order()):
                        if kind == "gate":
                            c_at = e.snap(i * WIN + (COL_GATE + b * D))
                            load(e, CH_MERGE + j, rows(t_in["w_in"], 256 * k, 2, c_at, WIN), 2, WIN, i, 48)
                        elif kind == "branch":
                            n = BR[b][2]
                            c_at = e.snap(i * WIN)
                            load(e, CH_MERGE + j, rows(t_in["w_post"], BR[b][3] + n * P * k, n, c_at, WIN), n, WIN, i, 48)
                        else:
                            r_at = e.snap(i * WIN + (k % 2) * 256)
                            load(e, CH_MERGE + j, rows(t_in["w_post"], r_at, 2, (k // 2) * WIN, WIN), 2, WIN, i, 48)
                ffn_loads(CH_FFN2, "ffn2")
                out = t_out["yT"].rearrange("(t p) n -> p t n", p=P)
                for p in range(8):
                    e.wait_ge(hf_ready, AP["fin"] + p + 1)
                    e.dma_start(out[:, 2 * p:2 * p + 2, :], hf[:, p % 2]).then_inc(y_out[p % 2], 16)
                e.wait_ge(y_out[0], 64)
                e.wait_ge(y_out[1], 64)
                e.wait_ge(stored, 48)
                e.wait_ge(lat_out, 32)

            @block.scalar
            def _(e):
                def squares(name, src, pairs, cols=N):
                    for p in range(pairs):
                        if SQ[name] + p >= 2:
                            e.wait_ge(sq_used, SQ[name] + p - 1)
                        e.activation(sq[:, p % 2, :, 0:cols], src[:, 2 * p:2 * p + 2, :], ACT.Square).then_inc(sq_ready, 1)

                def root(name, out, cols=N):
                    e.wait_ge(mean_ready, 2 * NORM[name] + 2)
                    e.activation(out[:, 0:cols], mean[:, 0:cols], ACT.Sqrt).then_inc(rstd_ready, 1)

                def round_h(name, out, pairs, cols=N):
                    for p in range(pairs):
                        e.wait_ge(hf_ready, AP[name] + p + 1)
                        e.activation(out[:, 2 * p:2 * p + 2, 0:cols], hf[:, p % 2, :, 0:cols], ACT.Copy).then_inc(hf_hi, 1)

                e.wait_ge(const_in, 48)
                e.activation(s5v[:, V_DT], s5p[:, S_LDT], ACT.Exp).then_inc(s5_exp, 1)
                e.wait_ge(s5_arg, 1)
                e.activation(s5v[:, V_R], s5v[:, V_AR], ACT.Exp).then_inc(s5_exp, 1)
                e.wait_ge(s5_arg, 2)
                e.activation(s5v[:, V_S1], s5v[:, V_PS], ACT.Sin).then_inc(s5_sin, 1)
                e.activation(s5v[:, V_C1], s5v[:, V_PC], ACT.Sin).then_inc(s5_sin, 1)
                e.wait_ge(mem_in, 16)
                squares("mem", memT, 8, 256)
                root("mem", rstd, 256)
                round_h("mem", hhi, 8, 256)
                for c in range(16):
                    round_w(e, CH_MEM + c, 2 * WIN)

                def ffn(name, c0, gr):
                    if name == "ffn1":
                        e.wait_ge(x_in, 16)
                    else:
                        e.wait_ge(half_free[0], gr[0])
                        e.wait_ge(half_free[1], gr[1])
                    squares(name, x, 8)
                    root(name, rstd)
                    if name == "ffn1":
                        e.wait_ge(w_used, CH_FFN1)
                    round_h(name, hhi, 8)

                    def silu(c_last, i, per, body):
                        wait(e, w_used, c_last + 1, i, per)
                        if body:
                            wait(e, half_free[1], gr[1] + 1, i, 3)
                        for m in range(4):
                            ins = e.activation(silu_g[:, m], banks[:, m, 0:N], ACT.Silu)
                        ins.then_inc(half_free[0], 1)

                    def visit(c, kind, k, b, i, per, step):
                        round_w(e, c, 2 * WIN, i, per)
                        if step == "head" and kind == "up" and k == 2:
                            silu(c - 3, i, per, False)
                        if step == "body" and kind == "down" and k == 2:
                            silu(c - 3, i, per, True)
                    ffn_stream(e, c0, visit)

                ffn("ffn1", CH_FFN1, GR_FFN1)
                e.wait_ge(half_free[0], GR_Z[0])
                e.wait_ge(half_free[1], GR_Z[1])
                squares("mix", x, 8)
                root("mix", rstd_mix)
                round_h("mix", hhi, 8)
                def s5_act(part, s):
                    b = s % 2
                    if part == "pad_b":
                        e.wait_ge(pq_ready, s + 1)
                        if s == 0:
                            e.wait_ge(pads_set, 3)
                        else:
                            e.wait_ge(own_ready, s)
                        for g in range(2):
                            r = slice(64 * g, 64 * g + 64)
                            for k in range(T_BLK):
                                ins = e.activation(bp[r, :, :, k, 16 * g:16 * g + 16], pq[b][r, :, T_BLK - 1 - k, 0],
                                                   ACT.Copy)
                        ins.then_inc(b_padded, 1)
                    elif part == "pad_q":
                        if s >= 1:
                            e.wait_ge(s5_y, s)
                        for g in range(2):
                            r = slice(64 * g, 64 * g + 64)
                            for z in range(2):
                                ins = e.activation(qp[r, z, :, :, 16 * g:16 * g + 16].rearrange("p i j h -> p j i h"),
                                                   pq[b][r, z, :, 1], ACT.Copy)
                        ins.then_inc(q_padded, 1)
                    elif part == "turned":
                        e.wait_ge(s5_turned, s + 1)
                        if s >= 1:
                            e.wait_ge(bu_ready, s)
                        for z in range(2):
                            ins = e.activation(pT[:, z], banks[:, 4 + z, :].rearrange("p (i m) -> p i m", i=S_IT),
                                               ACT.Copy)
                        ins.then_inc(pT_set, 1)
                    elif part == "own":
                        e.wait_ge(own_ready, s + 1)
                        if s >= 1:
                            e.wait_ge(s5_y, s)
                        own = banks[:, 6, 384:512].rearrange("p (i h) -> p i h", i=S_IT)
                        for k in range(T_BLK):
                            for j in range(k, T_BLK):
                                r = 32 * (T_BLK - 1 - (j - k))
                                ins = e.activation(tz[32 * k:32 * k + 32, :, 32 * j:32 * j + 32], own[r:r + 32],
                                                   ACT.Copy)
                        ins.then_inc(tz_set, 1)
                    else:
                        e.wait_ge(ycur_ready, s + 1)
                        e.activation(u4[:, S_IT * s:S_IT * s + S_IT, :], ycur[:],
                                     ACT.Gelu_apprx_tanh).then_inc(gelu_ready, 1)

                s5_at = s5_slots([("gelu", 12), ("pad_b", 2), ("turned", 3), ("own", 4), ("pad_q", 5)])

                def drain(w):
                    e.wait_ge(w_used, CH_Z + 8 * (w + 1))
                    n = Z_WIN[w][1] // P
                    src = banks[:, 0:n, 0:N] if n > 1 else banks[:, 0, 0:N]
                    e.activation(z_out[w - 2], src, ACT.Copy).then_inc(half_free[0], 1)

                z_out = [cqT[:, 0:4], cqT[:, 4:6], ckvT[:], krraw[:], qmT[:]]
                for n in range(56):
                    w = n // 8 - 1
                    if n % 8 == 3 and w >= 2:
                        drain(w)
                    for part, s in s5_at.get(n, []):
                        s5_act(part, s)
                    round_w(e, CH_Z + n, 2 * Z_WIN[n // 8][1])
                after = dict(gelu=12, pad_b=2, turned=3, own=4, pad_q=5)
                rest = sorted(s5_at[56], key=lambda a: 5 * a[1] + after[a[0]])
                for part, s in rest:
                    if part == "gelu" and s == S_STEPS - 2:
                        drain(6)
                    s5_act(part, s)

                def softmax(att, p_sb, h, i=None):
                    wait(e, max_ready, h + 1, i, 4)
                    for t, (q0, nq, k0, nk, bank, col) in enumerate(att["tiles"]):
                        ins = e.activation(p_sb[0:nq, att["pcols"][t]:att["pcols"][t] + nk],
                                           banks[0:nq, bank, col:col + nk], ACT.Exp, scale=att["scale"],
                                           bias=stats[0:nq, 1, t:t + 1], accum_out=stats[0:nq, 2, t:t + 1])
                    ins.then_inc(exp_ready, 1)

                for h in range(MEM_HEADS):
                    softmax(MEM_ATT, mem_p[h % 2], AT_MEM + h)
                squares("q", cqT, 3)
                root("q", rstd)
                round_h("q", cqhi, 3)
                e.wait_ge(w_used, CH_MLA)
                squares("kv", ckvT, 2)
                root("kv", rstd)
                for p in range(2):
                    e.wait_ge(hf_ready, AP["kv"] + p + 1)
                    for q in range(2):
                        ins = e.activation(lathi[:, 2 * p + q, 0:N_P], latf[:, 2 * p + q, 0:N_P], ACT.Copy)
                        ins = e.activation(lathi[:, 2 * p + q, N_P + PAST:KEYS], latf[:, 2 * p + q, N_P:N], ACT.Copy)
                    ins.then_inc(hf_hi, 1)
                e.wait_ge(past_in, 48)
                e.activation(lathi[:, :, N_P:N_P + PAST], past[:], ACT.Copy).then_inc(past_hi, 1)
                with e.Fori(0, 4) as i:
                    for j, (kind, un, k, n) in enumerate(MLA_ORDER):
                        round_w(e, CH_MLA + j, size_of_mla(kind, n), i, 12)
                    for h in range(4):
                        softmax(MLA_ATT, mla_p[h % 2], AT_MLA + h, i)
                for w in range(2):
                    for k in range(4):
                        round_w(e, CH_GLU + 4 * w + k, 2 * WIN)
                for w in range(2):
                    e.wait_ge(w_used, CH_GLU + 4 * w + 4)
                    if w == 1:
                        e.wait_ge(ys_half, 1)
                    for m in range(4):
                        ins = e.activation(sgl[:, m], banks[:, 4 * w + m, 0:N], ACT.Sigmoid,
                                           bias=gains[:, G_BGLU + 4 * w + m:G_BGLU + 4 * w + m + 1])
                    ins.then_inc(half_free[w], 1)
                round_h("mix2", hhi, 8)
                with e.Fori(0, 4) as i:
                    gates = 0
                    for j, (kind, b, k) in enumerate(merge_order()):
                        n = BR[b][2] if kind == "branch" else 2
                        round_w(e, CH_MERGE + j, n * WIN, i, 48)
                        if kind == "branch" and k == 2:
                            wait(e, w_used, CH_MERGE + j - 2, i, 48)
                            wait(e, half_free[1], GR_MERGE[1] + gates, i, 5)
                            for m in range(4):
                                ins = e.activation(gate[:, m], banks[:, m, 0:N], ACT.Sigmoid)
                            ins.then_inc(half_free[0], 1)
                            gates += 1
                ffn("ffn2", CH_FFN2, GR_FFN2)
                e.wait_ge(half_free[0], GR_END[0])
                e.wait_ge(half_free[1], GR_END[1])
                squares("fin", x, 8)
                root("fin", rstd)

            @block.gpsimd
            def _(e):
                e.memset(ones[:], 1.0).then_inc(ones_set, 1)
                e.memset(bp[:], 0.0).then_inc(pads_set, 1)
                e.memset(qp[:], 0.0).then_inc(pads_set, 1)
                e.memset(tz[:], 0.0).then_inc(pads_set, 1)

                def split_h(name, out, hi, pairs, cols=N):
                    for p in range(pairs):
                        e.wait_ge(hf_hi, AP[name] + p + 1)
                        e.tensor_tensor(out[:, 2 * p:2 * p + 2, 0:cols], hf[:, p % 2, :, 0:cols],
                                        hi[:, 2 * p:2 * p + 2, 0:cols].bitcast(F32), ALU.subtract).then_inc(hf_lo, 1)

                split_h("mem", hlo, hhi, 8, 256)
                for c in range(16):
                    split_w(e, CH_MEM + c, 2 * WIN)
                split_h("ffn1", hlo, hhi, 8)
                ffn_stream(e, CH_FFN1, lambda c, kind, k, b, i, per, step: split_w(e, c, 2 * WIN, i, per))
                split_h("mix", hlo, hhi, 8)
                c = CH_Z
                for c_at, width, half in Z_WIN:
                    for k in range(8):
                        split_w(e, c, 2 * width)
                        c += 1
                split_h("q", cqlo, cqhi, 3)
                for p in range(2):
                    e.wait_ge(hf_hi, AP["kv"] + p + 1)
                    for q in range(2):
                        ins = e.tensor_tensor(latlo[:, 2 * p + q, 0:N_P], latf[:, 2 * p + q, 0:N_P],
                                              lathi[:, 2 * p + q, 0:N_P].bitcast(F32), ALU.subtract)
                        ins = e.tensor_tensor(latlo[:, 2 * p + q, N_P + PAST:KEYS], latf[:, 2 * p + q, N_P:N],
                                              lathi[:, 2 * p + q, N_P + PAST:KEYS].bitcast(F32), ALU.subtract)
                    ins.then_inc(hf_lo, 1)
                e.wait_ge(past_hi, 1)
                e.tensor_tensor(latlo[:, :, N_P:N_P + PAST], past[:], lathi[:, :, N_P:N_P + PAST].bitcast(F32),
                                ALU.subtract).then_inc(past_lo, 1)
                e.memset(lathi[:, :, KEYS:512].bitcast(F32), 0.0)
                e.memset(latlo[:, :, KEYS:512].bitcast(F32), 0.0).then_inc(past_lo, 1)
                with e.Fori(0, 4) as i:
                    for j, (kind, un, k, n) in enumerate(MLA_ORDER):
                        split_w(e, CH_MLA + j, size_of_mla(kind, n), i, 12)
                for c in range(8):
                    split_w(e, CH_GLU + c, 2 * WIN)
                split_h("mix2", hlo, hhi, 8)
                with e.Fori(0, 4) as i:
                    for j, (kind, b, k) in enumerate(merge_order()):
                        n = BR[b][2] if kind == "branch" else 2
                        split_w(e, CH_MERGE + j, n * WIN, i, 48)
                split_h("ffn2", hlo, hhi, 8)
                ffn_stream(e, CH_FFN2, lambda c, kind, k, b, i, per, step: split_w(e, c, 2 * WIN, i, per))

            @block.tensor
            def _(e):
                def sums(name, pairs, cols=N):
                    for p in range(pairs):
                        e.wait_ge(sq_ready, SQ[name] + p + 1)
                        for q in range(2):
                            ins = e.matmul(banks[:, 0, 0:cols], ones[:], sq[:, p % 2, q, 0:cols],
                                           start=p == 0 and q == 0, stop=p == pairs - 1 and q == 1)
                        ins.then_inc(sq_used, 1)

                def window(half, c0, name, ahi, alo, tiles, width, kpairs, group, base=CH_MEM, cols=N, norm=None):
                    for k in range(kpairs):
                        if k == 0 and group:
                            e.wait_ge(half_free[half], group)
                        if norm is not None:
                            e.wait_ge(hf_lo, AP[norm] + k + 1)
                        products(e, c0 + k, half, 2, width, tiles, ahi, alo, 2 * k, k == 0, k == kpairs - 1, cols)

                e.wait_ge(ones_set, 1)
                sums("mem", 8, 256)
                e.wait_ge(mean_ready, 1)
                window(0, CH_MEM, "w_mem_k", hhi, hlo, 4, WIN, 8, 0, cols=256, norm="mem")
                for k in range(8):
                    token_products(e, CH_MEM + 8 + k, 1, 2, 2, hhi, hlo, 2 * k, k == 0, k == 7)

                def ffn(name, c0, gr):
                    e.wait_ge(half_free[0], gr[0])
                    e.wait_ge(half_free[1], gr[1])
                    sums(name, 8)
                    e.wait_ge(mean_ready, 2 * NORM[name] + 1)
                    sbase = 0 if name == "ffn1" else FFN_BLOCKS

                    def visit(c, kind, k, b, i, per, step):
                        if kind in ("gate", "up"):
                            half = 0 if kind == "gate" else 1
                            if step == "head" and kind == "gate":
                                e.wait_ge(hf_lo, AP[name] + k + 1)
                            if k == 0 and step == "body":
                                wait(e, half_free[half], gr[half] + (1 if kind == "gate" else 3), i, 3)
                            products(e, c, half, 2, WIN, 4, hhi, hlo, 2 * k, k == 0, k == 7, N, i, per)
                        else:
                            w = k // 2
                            half = (1, 0, 1, 0)[w] if step == "body" else (0, 1, 0, 1)[w]
                            if k % 2 == 0:
                                if w == 0:
                                    if step == "body":
                                        wait(e, prod_lo, sbase + 1, i, 1)
                                    else:
                                        e.wait_ge(prod_lo, sbase + FFN_BLOCKS)
                                if step == "body":
                                    wait(e, half_free[half], gr[half] + (1, 2, 2, 3)[w], i, 3)
                                else:
                                    e.wait_ge(half_free[half], gr[half] + 3 * (FFN_BLOCKS - 1) + 1 + w // 2)
                            products(e, c, half, 2, WIN, 4, phi, plo, 2 * (k % 2), k % 2 == 0, k % 2 == 1, N, i, per)
                    ffn_stream(e, c0, visit)

                ffn("ffn1", CH_FFN1, GR_FFN1)
                e.wait_ge(half_free[0], GR_Z[0])
                e.wait_ge(half_free[1], GR_Z[1])
                sums("mix", 8)
                e.wait_ge(mean_ready, 2 * NORM["mix"] + 1)
                seen = list(GR_Z)

                def s5_pe(part, s):
                    ident = const[:, C_ID:C_ID + P]
                    if part == "A":
                        e.wait_ge(b_padded, s + 1)
                        if s == 0:
                            e.wait_ge(half_free[1], GR_Z[1] + 1)
                        else:
                            e.wait_ge(pT_set, s)
                        if s >= 2:
                            e.wait_ge(ycur_ready, s - 1)
                        for z in range(2):
                            for i in range(S_IT):
                                ins = e.transpose(banks[:, 4 + z, i * P:(i + 1) * P],
                                                  bp[:, z, i].rearrange("p k h -> p (k h)"), ident)
                        ins.then_inc(s5_turned, 1)
                        if s >= 1:
                            e.wait_ge(bu_read, s)
                            e.wait_ge(tz_set, s)
                        for i in range(S_IT):
                            for z in range(2):
                                ins = e.matmul(banks[:, 6, 384 + 32 * i:384 + 32 * i + 32],
                                               bp[:, z, i].rearrange("p k h -> p (k h)"),
                                               sw[s % 2][:, 4 + 2 * z:6 + 2 * z].rearrange("p a i h -> p (a i h)")
                                               [:, 32 * i:32 * i + 32], start=z == 0, stop=z == 1)
                        ins.then_inc(own_ready, 1)
                    elif part == "B":
                        if s == 0:
                            e.wait_ge(half_free[0], GR_Z[0] + 1)
                        e.wait_ge(pT_set, s + 1)
                        e.wait_ge(tz_set, s + 1)
                        for z in range(2):
                            for i in range(S_IT):
                                ins = e.matmul(banks[:, 6 + z, BLKS * i:BLKS * i + BLKS], pT[:, z, i],
                                               u4[:, S_IT * s + i, :], start=True, stop=True)
                        ins.then_inc(bu_ready, 1)
                    else:
                        e.wait_ge(s5_x, s + 1)
                        e.wait_ge(q_padded, s + 1)
                        if s + 1 < S_STEPS:
                            e.wait_ge(pT_set, s + 2)
                        for i in range(S_IT):
                            o = banks[:, 4, BLKS * i:BLKS * i + BLKS]
                            for z in range(2):
                                e.matmul(o, qp[:, z, i].rearrange("p k h -> p (k h)"), xs[:, z, i, 0:BLKS],
                                         start=z == 0, stop=False)
                            ins = e.matmul(o, tz[:, i], u4[:, S_IT * s + i, :], start=False, stop=True)
                        ins.then_inc(s5_y, 1)

                s5_at = s5_slots([("C", 6), ("A", 0), ("B", 3)])
                for w, (c_at, width, half) in enumerate(Z_WIN):
                    for k in range(8):
                        for part, s in s5_at.get(8 * w + k, []):
                            s5_pe(part, s)
                        if k == 0:
                            e.wait_ge(half_free[half], seen[half])
                            seen[half] += 1
                        if w == 0:
                            e.wait_ge(hf_lo, AP["mix"] + k + 1)
                        products(e, CH_Z + 8 * w + k, half, 2, width, width // P, hhi, hlo, 2 * k, k == 0, k == 7)
                for part, s in sorted(s5_at[56], key=lambda a: 5 * a[1] + dict(A=0, B=3, C=6)[a[0]]):
                    s5_pe(part, s)

                def heads(att, h0_, keys, queries, values, p_sb, pT, extra, i=None):
                    def score(h):
                        if h0_ + h >= 1:
                            wait(e, exp_ready, h0_ + h, i, 4)
                        for t, (q0, nq, k0, nk, bank, col) in enumerate(att["tiles"]):
                            ops = [(queries[:, h, q0:q0 + nq], keys[:, h, k0:k0 + nk])] + extra(h, t, q0, nq, k0, nk)
                            for n_, (a, b) in enumerate(ops):
                                ins = e.matmul(banks[0:nq, bank, col:col + nk], a, b, start=n_ == 0,
                                               stop=n_ == len(ops) - 1)
                        ins.then_inc(scores, 1)

                    score(0)
                    for h in range(4):
                        if h < 3:
                            score(h + 1)
                        wait(e, p_ready, h0_ + h + 1, i, 4)
                        for t, kk, nk, bank, col in att["turns"]:
                            nq = att["tiles"][t][1]
                            at = att["pcols"][t] + kk
                            ins = e.transpose(banks[0:nk, bank, col:col + nq], p_sb[h % 2][0:nq, at:at + nk],
                                              const[0:nq, C_ID:C_ID + nq])
                        ins.then_inc(p_turned, 1)
                        wait(e, pT_ready, h0_ + h + 1, i, 4)
                        if h0_ + h >= 1:
                            wait(e, pv_out, h0_ + h, i, 4)
                        for vt, nr, pc, nq, oc, st, sp_ in att["pv"]:
                            ins = e.matmul(banks[:, 4, oc:oc + nq], values[0:nr, vt, h * HD:(h + 1) * HD],
                                           pT[0:nr, pc:pc + nq], start=st, stop=sp_, skip_group_check=True)
                        ins.then_inc(pv_done, 1)

                e.wait_ge(half_free[0], GR_MLA[0])
                e.wait_ge(half_free[1], GR_MLA[1])
                e.wait_ge(ycur_ready, S_STEPS)
                e.wait_ge(memkv_in, 32)
                heads(MEM_ATT, AT_MEM, mkT, qmT, mv, mem_p, mem_pT, lambda h, t, q0, nq, k0, nk: [])
                e.wait_ge(pv_out, MEM_HEADS)
                e.matmul(banks[:, 5, 0:N], const[:, C_PERM:C_PERM + P], krraw[:], start=True, stop=True).then_inc(kr_turned, 1)
                sums("q", 3)
                e.wait_ge(mean_ready, 2 * NORM["q"] + 1)
                sums("kv", 2)
                e.wait_ge(mean_ready, 2 * NORM["kv"] + 1)

                e.wait_ge(hf_lo, AP["kv"] + 2)
                e.wait_ge(past_lo, 2)
                e.wait_ge(kr_rotated, 2)
                e.wait_ge(past_in, 48)

                with e.Fori(0, 4) as i:
                    for j, (kind, un, k, n) in enumerate(MLA_ORDER):
                        half = un if kind == "uq" else 0 if kind == "uk" else 1
                        prior = {"uq": 0, "uk": 1, "uv": 1}[kind]
                        if k == 0:
                            wait(e, half_free[half], GR_MLA[half] + prior, i, 2)
                        if kind == "uq":
                            products(e, CH_MLA + j, half, n, QW, 3, cqhi, cqlo, k, k == 0, k == 5, N, i, 12)
                        elif kind == "uk":
                            products(e, CH_MLA + j, half, n, WIN, 4, lathi, latlo, k, k == 0, k == 2, KEYS, i, 12)
                        else:
                            token_products(e, CH_MLA + j, half, n, 4, lathi, latlo, k, k == 0, k == 2, i, 12)
                    wait(e, half_free[0], GR_MLA[0] + 2, i, 2)
                    wait(e, half_free[1], GR_MLA[1] + 2, i, 2)
                    for un in range(2):
                        e.matmul(banks[:, 5 + un, 0:N], const[:, C_PERM:C_PERM + P], qraw[:, un], start=True,
                                 stop=True).then_inc(q_turned, 1)
                    wait(e, q_rotated, 2, i, 2)

                    def extra(h, t, q0, nq, k0, nk):
                        ops = [(qrope[:, h // 2, q0:q0 + nq], kr[:, h % 2, k0:k0 + nk])]
                        if t < 2:
                            m0 = C_MASK + (128 if t == 0 else 0)
                            ops.append((const[0:1, C_HALF:C_HALF + nq], const[0:1, m0:m0 + nk]))
                        return ops

                    heads(MLA_ATT, AT_MLA, kn, qn, vv, mla_p, mla_pT, extra, i)
                    wait(e, pv_out, AT_MLA + 4, i, 4)

                e.wait_ge(gy_split, 2)
                for w in range(2):
                    for k in range(4):
                        products(e, CH_GLU + 4 * w + k, w, 2, WIN, 4, gyhi, gylo, 2 * k, k == 0, k == 3)
                e.wait_ge(ya_split, 2)
                e.wait_ge(ys_split, 1)
                e.wait_ge(half_free[0], GR_MERGE[0])
                e.wait_ge(half_free[1], GR_MERGE[1])
                e.wait_ge(hf_lo, AP["mix2"] + 8)
                acts = {"ssm": (yshi, yslo), "mla": (yahi, yalo), "mem": (ymhi, ymlo)}
                with e.Fori(0, 4) as i:
                    seen = [0, 0]
                    for j, (kind, b, k) in enumerate(merge_order()):
                        if kind == "gate":
                            if k == 0:
                                wait(e, half_free[0], GR_MERGE[0] + seen[0], i, 5)
                                seen[0] += 1
                            products(e, CH_MERGE + j, 0, 2, WIN, 4, hhi, hlo, 2 * k, k == 0, k == 7, N, i, 48)
                        elif kind == "branch":
                            name, nch, n, _ = BR[b]
                            if k == 0:
                                wait(e, half_free[1], GR_MERGE[1] + seen[1], i, 5)
                                seen[1] += 1
                            products(e, CH_MERGE + j, 1, n, WIN, 4, *acts[name], n * k, k == 0, k == nch - 1, N, i, 48)
                        else:
                            half = (k // 2) % 2
                            if k == 0:
                                wait(e, m_split, 1, i, 1)
                            if k % 2 == 0:
                                wait(e, half_free[half], GR_MERGE[half] + seen[half], i, 5)
                                seen[half] += 1
                            products(e, CH_MERGE + j, half, 2, WIN, 4, mhi, mlo, 2 * (k % 2), k % 2 == 0, k % 2 == 1,
                                     N, i, 48)
                ffn("ffn2", CH_FFN2, GR_FFN2)
                e.wait_ge(half_free[0], GR_END[0])
                e.wait_ge(half_free[1], GR_END[1])
                sums("fin", 8)

            @block.vector
            def _(e):
                links = [0, None, 0]

                def link(ins):
                    links[0] += 1
                    ins.then_inc(dve_link, 1)
                    wait(e, dve_link, links[0], links[1], links[2])

                @contextmanager
                def loop(trips, links_a_pass):
                    start = links[0]
                    with e.Fori(0, trips) as i:
                        links[1:] = [i, links_a_pass]
                        yield i
                    assert links[0] - start == links_a_pass, (links[0] - start, links_a_pass)
                    links[0] = start + trips * links_a_pass
                    links[1:] = [None, 0]

                def mean_inv(name, pairs, dim, cols=N):
                    e.wait_ge(sq_used, SQ[name] + pairs)
                    e.tensor_scalar(mean[:, 0:cols], banks[:, 0, 0:cols], 1.0 / dim, EPS, ALU.mult,
                                    ALU.add).then_inc(mean_ready, 1)
                    e.wait_ge(mean_ready, 2 * NORM[name] + 1)
                    e.reciprocal(mean[:, 0:cols], mean[:, 0:cols]).then_inc(mean_ready, 1)

                def apply(name, src, rs, g, pairs, cols=N):
                    for p in range(pairs):
                        if AP[name] + p >= 2:
                            e.wait_ge(hf_lo, AP[name] + p - 1 if name != "fin" else AP[name])
                        if name == "fin" and p >= 2:
                            e.wait_ge(y_out[p % 2], 16 * (p // 2))
                        for q in range(2):
                            t = 2 * p + q
                            ins = e.scalar_tensor_tensor(out=hf[:, p % 2, q, 0:cols], in0=src[:, t, 0:cols],
                                                         scalar=gains[:, g + t:g + t + 1], in1=rs[:, 0:cols],
                                                         op0=ALU.mult, op1=ALU.mult)
                        ins.then_inc(hf_ready, 1)

                def tt(out, a, b, op):
                    link(e.tensor_tensor(out, a, b, op))

                def ts(out, a, s1, op0, s2=None, op1=ALU.bypass):
                    link(e.tensor_scalar(out, a, s1, s2, op0, op1))

                link(e.memset(stats[:], 1.0))
                e.memset(u4[:, :, B_P:B_P + 1], 0.0)
                e.wait_ge(const_in, 48)
                v = [s5v[:, r] for r in range(22)]
                are, aim = s5p[:, S_ARE], s5p[:, S_AIM]
                e.wait_ge(s5_exp, 1)
                e.tensor_tensor(v[V_AR], are, v[V_DT], ALU.mult).then_inc(s5_arg, 1)
                tt(v[V_PH], aim, v[V_DT], ALU.mult)
                two_pi = 2 * np.pi
                c1 = 6.28125
                c2 = float(np.round((two_pi - c1) * 2 ** 20) / 2 ** 20)
                c3 = two_pi - c1 - c2
                for quarter, out in ((0.0, v[V_PS]), (0.25, v[V_PC])):
                    ts(v[V_K], v[V_PH], 1 / two_pi, ALU.mult, quarter, ALU.add)
                    ts(v[V_K], v[V_K], 12582912.0, ALU.add)
                    ts(v[V_K], v[V_K], 12582912.0, ALU.subtract)
                    src = v[V_PH]
                    for c in (c1, c2, c3):
                        link(e.scalar_tensor_tensor(out=out, in0=v[V_K], scalar=-c, in1=src, op0=ALU.mult, op1=ALU.add))
                        src = out
                    ts(out, out, two_pi * quarter, ALU.add)
                    ins = e.tensor_scalar(out, out, 3.1415925, -3.1415925, ALU.min, ALU.max)
                    if quarter:
                        ins.then_inc(s5_arg, 1)
                    else:
                        link(ins)
                e.wait_ge(s5_sin, 2)
                tt(v[V_LRE], v[V_R], v[V_C1], ALU.mult)
                tt(v[V_LIM], v[V_R], v[V_S1], ALU.mult)
                tt(v[V_INV], are, are, ALU.mult)
                tt(v[V_T], aim, aim, ALU.mult)
                tt(v[V_INV], v[V_INV], v[V_T], ALU.add)
                link(e.reciprocal(v[V_INV], v[V_INV]))
                ts(v[V_NR], v[V_LRE], 1.0, ALU.subtract)
                for out, a, b, op in ((V_ZRE, (v[V_NR], are), (v[V_LIM], aim), ALU.add),
                                      (V_ZIM, (v[V_LIM], are), (v[V_NR], aim), ALU.subtract)):
                    tt(v[out], a[0], a[1], ALU.mult)
                    tt(v[V_T], b[0], b[1], ALU.mult)
                    tt(v[out], v[out], v[V_T], op)
                    tt(v[out], v[out], v[V_INV], ALU.mult)
                ts(v[V_NZRE], v[V_ZRE], -1.0, ALU.mult)
                ts(v[V_NLRE], v[V_LRE], -1.0, ALU.mult)
                ts(s5p[:, S_H0IM], s5p[:, S_H0IM], -1.0, ALU.mult)

                def square(c2, s2, c, s, t):
                    tt(c2, c, c, ALU.mult)
                    tt(t, s, s, ALU.mult)
                    tt(s2, c, s, ALU.mult)
                    tt(c2, c2, t, ALU.subtract)
                    ts(s2, s2, 2.0, ALU.mult)

                e.wait_ge(mem_in, 16)
                mean_inv("mem", 8, D, 256)
                e.wait_ge(rstd_ready, 1)
                apply("mem", memT, rstd, G_MEM, 8, 256)
                square(v[V_L2RE], v[V_L2IM], v[V_LRE], v[V_LIM], v[V_T])
                tt(v[V_T], v[V_R], v[V_R], ALU.mult)
                tt(v[V_R4], v[V_T], v[V_T], ALU.mult)
                square(v[V_PC], v[V_PS], v[V_C1], v[V_S1], v[V_T])
                square(uph[:, 0, 0], uph[:, 0, 1], v[V_PC], v[V_PS], v[V_T])
                for m in range(5):
                    square(uph[:, m + 1, 0], uph[:, m + 1, 1], uph[:, m, 0], uph[:, m, 1], v[V_T])
                e.memset(elh[:, :, 0, :, 0:1], 1.0)
                link(e.memset(elh[:, :, 1, :, 0:1], 0.0))
                for k in range(3):
                    n = 1 << k
                    for h in range(2):
                        ec, es = elh[:, h, 0], elh[:, h, 1]
                        uc, us = (uph[:, 3 * h + k, z].rearrange("p (t o) -> p t o", o=1).broadcast_to([P, S_TILES, n])
                                  for z in range(2))
                        tt(ec[:, :, n:2 * n], ec[:, :, 0:n], uc, ALU.mult)
                        tt(e_t[:, 0, :, 0:n], es[:, :, 0:n], us, ALU.mult)
                        tt(es[:, :, n:2 * n], ec[:, :, 0:n], us, ALU.mult)
                        tt(e_t[:, 1, :, 0:n], es[:, :, 0:n], uc, ALU.mult)
                        tt(ec[:, :, n:2 * n], ec[:, :, n:2 * n], e_t[:, 0, :, 0:n], ALU.subtract)
                        tt(es[:, :, n:2 * n], es[:, :, n:2 * n], e_t[:, 1, :, 0:n], ALU.add)
                e.wait_ge(w_used, CH_MEM + 8)
                e.tensor_copy(mkT[:, :, 0:256], banks[:, 0:4, 0:256]).then_inc(half_free[0], 1)
                e.wait_ge(w_used, CH_MEM + 16)
                e.tensor_copy(mv[:, 0:2, :], banks[:, 4:6, :]).then_inc(half_free[1], 1)

                def add_down(half, w, scale, i=None, per=0):
                    for m in range(4):
                        ins = e.scalar_tensor_tensor(out=x[:, 4 * w + m], in0=banks[:, 4 * half + m, 0:N], scalar=scale,
                                                     in1=x[:, 4 * w + m], op0=ALU.mult, op1=ALU.add)
                    ins.then_inc(half_free[half], 1)

                def ffn(name, c0, gr, g):
                    if name == "ffn1":
                        e.wait_ge(x_in, 16)
                    else:
                        e.wait_ge(half_free[0], gr[0])
                        e.wait_ge(half_free[1], gr[1])
                    mean_inv(name, 8, D)
                    e.wait_ge(rstd_ready, NORM[name] + 1)
                    apply(name, x, rstd, g, 8)
                    base = 0 if name == "ffn1" else FFN_BLOCKS

                    def visit(c, kind, k, b, i, per, step):
                        body = step == "body"
                        if kind == "up" and k == 7:
                            wait(e, half_free[0], gr[0] + (2 if body else 1), i, 3)
                            wait(e, w_used, c + 1, i, per)
                            for m in range(4):
                                ins = e.tensor_tensor(prod[:, m], banks[:, 4 + m, 0:N], silu_g[:, m], ALU.mult)
                            ins.then_inc(half_free[1], 1)
                            wait(e, half_free[1], gr[1] + (4 if body else 1), i, 3)
                            e.tensor_copy(phi[:], prod[:]).then_inc(prod_hi, 1)
                            wait(e, prod_hi, base + (2 if body else 1), i, 1)
                            e.tensor_tensor(plo[:], prod[:], phi[:].bitcast(F32), ALU.subtract).then_inc(prod_lo, 1)
                        if kind == "down" and k % 2 == 1:
                            w = k // 2
                            half = (1, 0, 1, 0)[w] if body else (0, 1, 0, 1)[w]
                            wait(e, w_used, c + 1, i, per)
                            add_down(half, w, 0.5)
                    ffn_stream(e, c0, visit)

                ffn("ffn1", CH_FFN1, GR_FFN1, G_FFN1)
                e.wait_ge(half_free[0], GR_Z[0])
                e.wait_ge(half_free[1], GR_Z[1])
                mean_inv("mix", 8, D)
                e.wait_ge(rstd_ready, NORM["mix"] + 1)
                apply("mix", x, rstd_mix, G_MIX, 8)
                grow = lambda a, n: a.rearrange("p (i o) -> p i o", o=1).broadcast_to([P, S_IT, n])

                def powers(s):
                    own = slice(S_IT * s, S_IT * s + S_IT)
                    out = pq[s % 2]
                    e.wait_ge(s5_in[s % 2], 16 * (s // 2 + 1))
                    if s >= 2:
                        e.wait_ge(q_padded, s - 1)

                    def factor(row, step, n):
                        a = s5v[:, row:row + 2, own] if step else s5v[:, row:row + 1, own]
                        a = a.rearrange("p r (i o) -> p r i o", o=1)
                        return a.broadcast_to([P, n, S_IT, 16])

                    def four(dst, src_re, src_im, f_a, f_b, f_c, ops):
                        n = src_re.shape[1]
                        t0 = s_t[:].rearrange("p i c -> p (i c)")[:, 0:64 * n].rearrange("p (r i h) -> p r i h", i=S_IT, h=16)
                        t1 = s_t2[:].rearrange("p i c -> p (i c)")[:, 0:64 * n].rearrange("p (r i h) -> p r i h", i=S_IT, h=16)
                        e.tensor_tensor(dst[0], src_re, f_a, ALU.mult)
                        e.tensor_tensor(t0, src_im, f_b, ALU.mult)
                        e.tensor_tensor(dst[1], src_im, f_c, ALU.mult)
                        link(e.tensor_tensor(t1, src_re, f_b, ALU.mult))
                        e.tensor_tensor(dst[0], dst[0], t0, ops[0])
                        return e.tensor_tensor(dst[1], dst[1], t1, ops[1])

                    flat = lambda z, r0, r1: out[:, z, r0:r1].rearrange("p r a i h -> p (r a) i h")
                    link(four((flat(0, 0, 1), flat(1, 0, 1)), sw[s % 2][:, 0:2], sw[s % 2][:, 2:4],
                              factor(V_ZRE, 1, 2), factor(V_ZIM, 1, 2), factor(V_NZRE, 1, 2),
                              (ALU.subtract, ALU.subtract)))
                    link(four((flat(0, 1, 2), flat(1, 1, 2)), flat(0, 0, 1), flat(1, 0, 1), factor(V_LRE, 0, 2),
                              factor(V_LIM, 0, 2), factor(V_LRE, 0, 2), (ALU.add, ALU.subtract)))
                    four((flat(0, 2, 4), flat(1, 2, 4)), flat(0, 0, 2), flat(1, 0, 2), factor(V_L2RE, 0, 4),
                         factor(V_L2IM, 0, 4), factor(V_L2RE, 0, 4), (ALU.add, ALU.subtract)).then_inc(pq_ready, 1)
                    e.wait_ge(pq_ready, s + 1)

                def phases(s):
                    own = slice(S_IT * s, S_IT * s + S_IT)
                    lo = [elh[:, 0, z, own, :].rearrange("p i (o b) -> p i o b", o=1).broadcast_to([P, S_IT, 8, 8])
                          for z in range(2)]
                    hi = [elh[:, 1, z, own, :].rearrange("p i (a o) -> p i a o", o=1).broadcast_to([P, S_IT, 8, 8])
                          for z in range(2)]
                    view = lambda t: t[:, :, 0:B_P].rearrange("p i (a b) -> p i a b", a=8)
                    e.tensor_tensor(view(ee[:, 0]), lo[0], hi[0], ALU.mult)
                    e.tensor_tensor(view(s_t), lo[1], hi[1], ALU.mult)
                    e.tensor_tensor(view(ee[:, 1]), lo[0], hi[1], ALU.mult)
                    e.tensor_tensor(view(s_t2), lo[1], hi[0], ALU.mult)
                    link(e.tensor_copy(dec[:], grow(s5v[:, V_R4, own], BLKS)))
                    e.memset(dec[:, :, 0:1], 0.0)
                    e.memset(dec[:, :, B_P:B_P + 1], 0.0)
                    e.tensor_tensor(ee[:, 0, :, 0:B_P], ee[:, 0, :, 0:B_P], s_t[:, :, 0:B_P], ALU.subtract)
                    link(e.tensor_tensor(ee[:, 1, :, 0:B_P], ee[:, 1, :, 0:B_P], s_t2[:, :, 0:B_P], ALU.add))
                    for z in range(2):
                        ins = e.tensor_copy(ee[:, z, :, B_P:BLKS], ee[:, z, :, 0:B_S + 1])
                    link(ins)

                def recurrence(s):
                    own = slice(S_IT * s, S_IT * s + S_IT)
                    c, sn = ee[:, 0], ee[:, 1]
                    b_re, b_im = (banks[:, 6 + z, 0:S_IT * BLKS].rearrange("p (i n) -> p i n", i=S_IT) for z in range(2))
                    flat = lambda t: t.rearrange("p i n -> p (i n)")
                    wf = [flat(xs[:, z])[:, 0:S_IT * BLKS] for z in range(2)]
                    w_re, w_im = (a.rearrange("p (i n) -> p i n", i=S_IT) for a in wf)
                    g1 = lambda a: a.rearrange("p (i o) -> p i o", o=1)
                    e.wait_ge(bu_ready, s + 1)
                    e.tensor_tensor(w_re, b_re, c, ALU.mult)
                    e.tensor_tensor(s_t[:], b_im, sn, ALU.mult)
                    e.tensor_tensor(w_im, b_im, c, ALU.mult)
                    ins = e.tensor_tensor(s_t2[:], b_re, sn, ALU.mult)
                    ins.then_inc(bu_read, 1)
                    e.wait_ge(bu_read, s + 1)
                    e.tensor_tensor(w_re, w_re, s_t[:], ALU.subtract)
                    link(e.tensor_tensor(w_im, w_im, s_t2[:], ALU.add))
                    e.tensor_copy(w_re[:, :, B_P:B_P + 1], g1(s5p[:, S_H0RE, own]))
                    link(e.tensor_copy(w_im[:, :, B_P:B_P + 1], g1(s5p[:, S_H0IM, own])))
                    e.tensor_tensor_scan(flat(v_re), flat(dec), wf[0], 0.0, ALU.mult, ALU.add)
                    link(e.tensor_tensor_scan(flat(v_im), flat(dec), wf[1], 0.0, ALU.mult, ALU.add))
                    x_re, x_im = xs[:, 0, :, 1:BLKS + 1], xs[:, 1, :, 1:BLKS + 1]
                    e.memset(xs[:, :, :, 0:1], 0.0)
                    e.tensor_tensor(x_re, v_re[:], c, ALU.mult)
                    e.tensor_tensor(s_t[:], v_im[:], sn, ALU.mult)
                    e.tensor_tensor(x_im, v_re[:], sn, ALU.mult)
                    link(e.tensor_tensor(s_t2[:], v_im[:], c, ALU.mult))
                    e.tensor_tensor(x_re, x_re, s_t[:], ALU.add)
                    e.tensor_tensor(x_im, x_im, s_t2[:], ALU.subtract).then_inc(s5_x, 1)
                    e.wait_ge(s5_x, s + 1)
                    for k, last in enumerate((B_P, BLKS)):
                        for z in range(2):
                            e.tensor_copy(g1(states[:, 2 * k + z, own]), xs[:, z, :, last:last + 1])

                def outputs(s):
                    own = slice(S_IT * s, S_IT * s + S_IT)
                    if s >= 1:
                        e.wait_ge(gelu_ready, s)
                    link(e.tensor_tensor(s_t[:], u4[:, own, :], grow(gains[:, G_D + S_IT * s:G_D + S_IT * s + S_IT], BLKS),
                                         ALU.mult))
                    e.wait_ge(s5_y, s + 1)
                    e.tensor_tensor(ycur[:], banks[:, 4, 0:S_IT * BLKS].rearrange("p (i n) -> p i n", i=S_IT), s_t[:],
                                    ALU.add).then_inc(ycur_ready, 1)
                    e.wait_ge(ycur_ready, s + 1)

                e.wait_ge(hf_lo, AP["mix"] + 8)
                powers(0)
                powers(1)
                phases(0)
                for w in range(2):
                    e.wait_ge(w_used, CH_Z + 8 * (w + 1))
                    for a in range(S_IT):
                        for j in range(T_BLK):
                            dst = u4[32 * j:32 * j + 32, 16 * w + a:16 * w + a + 13:S_IT, :]
                            src = banks[32 * a:32 * a + 32, 4 * w:4 * w + 4, 0:N].rearrange("p m (c k) -> p m c k", k=T_BLK)
                            e.tensor_copy(dst[:, :, 0:B_P], src[:, :, 0:B_P, j])
                            ins = e.tensor_copy(dst[:, :, B_P + 1:BLKS], src[:, :, B_P:B_P + B_S, j])
                    ins.then_inc(half_free[w], 1)
                for s in range(S_STEPS):
                    recurrence(s)
                    if s + 1 < S_STEPS:
                        phases(s + 1)
                    if s + 2 < S_STEPS:
                        powers(s + 2)
                    outputs(s)

                def heads(att, h0_, p_sb, pT, out, i=None):
                    nt = 3

                    def biggest(h):
                        wait(e, scores, h0_ + h + 1, i, 4)
                        for t, (q0, nq, k0, nk, bank, col) in enumerate(att["tiles"]):
                            ins = e.reduce_max(stats[0:nq, 0, t:t + 1], banks[0:nq, bank, col:col + nk], AX_X)
                        link(ins)
                        e.tensor_scalar(stats[:, 1, 0:nt], stats[:, 0, 0:nt], -att["scale"], None,
                                        ALU.mult).then_inc(max_ready, 1)

                    biggest(0)
                    for h in range(4):
                        wait(e, exp_ready, h0_ + h + 1, i, 4)
                        link(e.reciprocal(stats[:, 3, 0:nt], stats[:, 2, 0:nt]))
                        for t, (q0, nq, k0, nk, bank, col) in enumerate(att["tiles"]):
                            a = p_sb[h % 2][0:nq, att["pcols"][t]:att["pcols"][t] + nk]
                            ins = e.tensor_scalar(a, a, stats[0:nq, 3, t:t + 1], None, ALU.mult)
                        ins.then_inc(p_ready, 1)
                        if h < 3:
                            biggest(h + 1)
                        wait(e, p_turned, h0_ + h + 1, i, 4)
                        sp_, last = att["split"], att["last_rows"]
                        e.tensor_copy(pT[:, 0:sp_], banks[:, 2, 0:sp_])
                        e.tensor_copy(pT[:, sp_:sp_ + 64], banks[:, 3, 0:64])
                        e.tensor_copy(pT[0:last, sp_ + 64:sp_ + 128], banks[0:last, 3, 64:128]).then_inc(pT_ready, 1)
                        wait(e, pv_done, h0_ + h + 1, i, 4)
                        o = out(h)
                        src = banks[:, 4, 0:N]
                        if len(o.shape) == 3:
                            src = src.rearrange("p (o n) -> p o n", o=1)
                        e.tensor_copy(o, src).then_inc(pv_out, 1)

                heads(MEM_ATT, AT_MEM, mem_p, mem_pT, lambda h: ymf[:, h, :])
                e.wait_ge(pv_out, MEM_HEADS)
                e.tensor_copy(ymhi[:], ymf[:]).then_inc(ym_split, 1)
                e.wait_ge(ym_split, 1)
                e.tensor_tensor(ymlo[:], ymf[:], ymhi[:].bitcast(F32), ALU.subtract).then_inc(ym_split, 1)
                cos, sin = const[:, C_COS:C_COS + N], const[:, C_SIN:C_SIN + N]
                tt(krot[:], krraw[:], cos, ALU.mult)
                e.wait_ge(kr_turned, 1)
                tt(mean[:], banks[:, 5, 0:N], sin, ALU.mult)
                e.tensor_tensor(krot[:], krot[:], mean[:], ALU.add).then_inc(kr_rotated, 1)
                e.wait_ge(kr_rotated, 1)
                e.memset(kr[64:128, 0, :], 0.0)
                e.memset(kr[0:64, 1, :], 0.0)
                for z in range(2):
                    r = slice(64 * z, 64 * z + 64)
                    e.tensor_copy(kr[r, z, 0:N_P], krot[r, 0:N_P])
                    ins = e.tensor_copy(kr[r, z, N_P + PAST:KEYS], krot[r, N_P:N])
                ins.then_inc(kr_rotated, 1)
                mean_inv("q", 3, Q_LORA)
                e.wait_ge(rstd_ready, NORM["q"] + 1)
                apply("q", cqT, rstd, G_Q, 3)
                mean_inv("kv", 2, KV_LORA)
                e.wait_ge(rstd_ready, NORM["kv"] + 1)
                for p in range(2):
                    for q in range(2):
                        t = 2 * p + q
                        ins = e.scalar_tensor_tensor(out=latf[:, t], in0=ckvT[:, t], scalar=gains[:, G_KV + t:G_KV + t + 1],
                                                     in1=rstd[:], op0=ALU.mult, op1=ALU.mult)
                    ins.then_inc(hf_ready, 1)
                e.wait_ge(gelu_ready, S_STEPS)
                e.wait_ge(hf_lo, AP["q"] + 3)
                e.wait_ge(sq_used, SQ["kv"] + 2)
                for a in range(S_IT):
                    for j in range(T_BLK):
                        dst = u[32 * a:32 * a + 32].rearrange("p m (c k) -> p m c k", k=T_BLK)
                        src = u4[32 * j:32 * j + 32, a:a + 29:S_IT, :]
                        e.tensor_copy(dst[:, :, 0:B_P, j], src[:, :, 0:B_P])
                        ins = e.tensor_copy(dst[:, :, B_P:B_P + B_S, j], src[:, :, B_P + 1:BLKS])
                link(ins)
                with loop(4, MLA_LINKS) as i:
                    for un in range(2):
                        wait(e, w_used, CH_MLA + 4 * un + 4, i, 12)
                        e.tensor_copy(qn[:, 2 * un:2 * un + 2, :], banks[:, 4 * un:4 * un + 2, 0:N])
                        e.tensor_copy(qraw[:, un], banks[:, 4 * un + 2, 0:N]).then_inc(half_free[un], 1)
                    wait(e, w_used, CH_MLA + 10, i, 12)
                    e.tensor_copy(kn[:], banks[:, 0:4, 0:KEYS]).then_inc(half_free[0], 1)
                    wait(e, w_used, CH_MLA + 12, i, 12)
                    e.tensor_copy(vv[:], banks[:, 4:8, :]).then_inc(half_free[1], 1)
                    for un in range(2):
                        tt(qrope[:, un], qraw[:, un], cos, ALU.mult)
                        wait(e, q_turned, un + 1, i, 2)
                        tt(mean[:], banks[:, 5 + un, 0:N], sin, ALU.mult)
                        e.tensor_tensor(qrope[:, un], qrope[:, un], mean[:], ALU.add).then_inc(q_rotated, 1)
                    at = e.snap(i * 4)
                    heads(MLA_ATT, AT_MLA, mla_p, mla_pT, lambda h: ymla[:, bass.ds(at + h, 1), :], i)
                e.wait_ge(pv_out, AT_MLA + 16)
                e.tensor_copy(gyhi[:], u[:]).then_inc(gy_split, 1)
                e.wait_ge(gy_split, 1)
                e.tensor_tensor(gylo[:], u[:], gyhi[:].bitcast(F32), ALU.subtract).then_inc(gy_split, 1)
                for w in range(2):
                    e.wait_ge(half_free[w], GR_GLU[w] + 1)
                    e.tensor_tensor(u[:, 4 * w:4 * w + 4], u[:, 4 * w:4 * w + 4], sgl[:], ALU.mult).then_inc(ys_half, 1)
                e.wait_ge(ys_half, 2)
                link(e.tensor_copy(yshi[:], u[:]))
                e.tensor_tensor(yslo[:], u[:], yshi[:].bitcast(F32), ALU.subtract).then_inc(ys_split, 1)
                e.wait_ge(ys_split, 1)
                apply("mix2", x, rstd_mix, G_MIX, 8)
                e.tensor_copy(yahi[:], ymla[:]).then_inc(ya_split, 1)
                e.wait_ge(ya_split, 1)
                e.tensor_tensor(yalo[:], ymla[:], yahi[:].bitcast(F32), ALU.subtract).then_inc(ya_split, 1)
                with loop(4, MERGE_LINKS) as i:
                    branch = -1
                    for j, (kind, b, k) in enumerate(merge_order()):
                        if kind == "branch" and k == BR[b][1] - 1:
                            wait(e, half_free[0], GR_MERGE[0] + b + 1, i, 5)
                            wait(e, w_used, CH_MERGE + j + 1, i, 48)
                            dst = merged if b == 0 else gate
                            for m in range(4):
                                ins = e.tensor_tensor(dst[:, m], banks[:, 4 + m, 0:N], gate[:, m], ALU.mult)
                            if b:
                                link(ins)
                                ins = e.tensor_tensor(merged[:], merged[:], gate[:], ALU.add)
                            ins.then_inc(half_free[1], 1)
                            wait(e, half_free[1], GR_MERGE[1] + b + 1, i, 5)
                            if b == 2:
                                link(e.tensor_copy(mhi[:], merged[:]))
                                e.tensor_tensor(mlo[:], merged[:], mhi[:].bitcast(F32), ALU.subtract).then_inc(m_split, 1)
                        if kind == "out" and k % 2 == 1:
                            wait(e, w_used, CH_MERGE + j + 1, i, 48)
                            add_down((k // 2) % 2, k // 2, 1.0)
                ffn("ffn2", CH_FFN2, GR_FFN2, G_FFN2)
                e.wait_ge(half_free[0], GR_END[0])
                e.wait_ge(half_free[1], GR_END[1])
                mean_inv("fin", 8, D)
                e.wait_ge(rstd_ready, NORM["fin"] + 1)
                apply("fin", x, rstd, G_FIN, 8)


_OUT = {"yT": (D, N), "latT": (KV_LORA, N), "krT": (ROPE, N), "mkT": (MEM_W, 256), "mv": (256, MEM_W),
        "states": (P, 4, S_TILES)}


def _constants():
    c = np.zeros((P, C_COLS), np.float32)
    c[:, C_ID:C_ID + P] = np.eye(P, dtype=np.float32)
    for b in (0, 64):
        for r in range(32):
            c[b + 32 + r, C_PERM + b + r] = -1.0
            c[b + r, C_PERM + b + 32 + r] = 1.0
    half = ROPE // 2
    inv = np.float32(10000.0) ** (-np.arange(half, dtype=np.float32) / np.float32(half))
    pos = np.concatenate([np.arange(N_P), PAST + np.arange(N_S)]).astype(np.float32)
    ang = (inv[:, None] * pos[None, :]).astype(np.float32)
    c[:, C_COS:C_COS + N] = np.tile(np.cos(ang), (4, 1))
    c[:, C_SIN:C_SIN + N] = np.tile(np.sin(ang), (4, 1))
    c[0, C_HALF:C_HALF + 64] = 1.0
    c[0, C_MASK + 192:C_MASK + 256] = -1e30
    return c


def kernel(**inp):
    import concourse.bacc as bacc
    from concourse.bass_utils import run_bass_kernel_spmd as run
    a = {k: np.asarray(v) for k, v in inp.items()}
    col = lambda v: v.reshape(-1, P)
    d4 = np.tile(a["ssm_d"].reshape(S_TILES, 32), (1, T_BLK))
    gains = np.concatenate([col(a["ffn1_norm"]), col(a["mix_norm"]), col(a["ffn2_norm"]), col(a["final_norm"]),
                            col(a["mem_norm"]), col(a["q_norm"]), col(a["kv_norm"]), col(a["ssm_b_glu"]),
                            d4]).T
    modes = lambda v: v.reshape(S_TILES, P).T
    ldt = np.repeat(a["ssm_log_dt"][0], 64)
    s5p = np.stack([modes(a["ssm_a_re"]), modes(a["ssm_a_im"]), modes(ldt), modes(a["state_ssm_re"]),
                    modes(a["state_ssm_im"])], axis=1)

    def steps(v):
        return v.reshape(S_TILES, P, 16).transpose(1, 0, 2).reshape(P, S_STEPS, S_IT, 16)

    def apart(v):
        out = np.zeros((2, 64, S_STEPS, S_IT, 2, 16), np.float32)
        w = v.reshape(S_STEPS, S_IT, 2, 64, 16)
        for g in range(2):
            out[g, :, :, :, g] = w[:, :, g].transpose(2, 0, 1, 3)
        return out.reshape(P, S_STEPS, 2, S_IT, 16)

    b_re, b_im = a["ssm_b_re"][0], a["ssm_b_im"][0]
    c_re, c_im = a["ssm_c_re"][0].transpose(0, 2, 1), a["ssm_c_im"][0].transpose(0, 2, 1)
    s5w = np.concatenate([np.stack([steps(v) for v in (b_re, c_re, b_im, c_im)], axis=2), apart(c_re), apart(c_im)],
                         axis=2)
    w_in = a["w_in"][0]
    arrays = {
        "const": _constants(), "gains": gains, "s5p": s5p,
        "xT": np.concatenate([a["x_prompt"][0], a["x_sample"][0]]).T,
        "memT": a["mem_prompt"][0].T,
        "cmkT": a["cache_mem_k"].reshape(256, MEM_W).T, "cmv": a["cache_mem_v"].reshape(256, MEM_W),
        "platT": a["cache_kv_latent"][0, 0].T, "pkrT": a["cache_k_rope"][0, 0].T,
        "s5w": s5w,
        "w_in": w_in, "w_kr2": np.concatenate([w_in[:, COL_KR:COL_QM]] * 2, axis=1),
    }
    arrays["w_post"] = np.concatenate([a[n][0] for n in ("w_out", "w_br_ssm", "w_br_mla", "w_br_mem")])
    uq = a["w_uq"][0].reshape(Q_LORA, HEADS // 2, 2, NOPE + ROPE)
    arrays["w_uq"] = np.concatenate([uq[..., :NOPE].reshape(Q_LORA, HEADS // 2, 2 * NOPE),
                                     uq[..., NOPE:].reshape(Q_LORA, HEADS // 2, 2 * ROPE)], axis=2).reshape(Q_LORA, -1)
    for name in ("w_mem_k", "w_mem_v", "ffn1_w_gate", "ffn1_w_up", "ffn1_w_down", "w_uk", "w_uv", "ssm_w_glu",
                 "ffn2_w_gate", "ffn2_w_up", "ffn2_w_down"):
        arrays[name] = a[name][0]
    nc = bacc.Bacc("TRN2", target_bir_lowering=False, num_devices=1)
    t_in, feed = {}, {}
    for name, v in arrays.items():
        feed["i_" + name] = np.ascontiguousarray(v)
        t_in[name] = nc.dram_tensor("i_" + name, v.shape, F32, kind="ExternalInput").ap()
    t_out = {n: nc.dram_tensor("o_" + n, s, F32, kind="ExternalOutput").ap() for n, s in _OUT.items()}
    build(nc, t_in, t_out)
    r = run(nc, [feed], core_ids=[0]).results[0]
    y, lat, kr = (np.asarray(r["o_" + n]).T for n in ("yT", "latT", "krT"))
    st = np.asarray(r["o_states"]).transpose(1, 2, 0).reshape(4, 1, 1, 64, 64)
    cut = lambda v: (v[None, :N_P], v[None, N_P:])
    (y_p, y_s), (l_p, l_s), (k_p, k_s) = cut(y), cut(lat), cut(kr)
    mk = np.asarray(r["o_mkT"]).T.reshape(1, 1, 256, MEM_HEADS, HD)
    mv = np.asarray(r["o_mv"]).reshape(1, 1, 256, MEM_HEADS, HD)
    return tuple(np.ascontiguousarray(v) for v in (
        y_p, y_s, l_p[None], k_p[None], mk, mv, st[0], st[1], l_s[None], k_s[None], st[2], st[3]))
```

```python
from contextlib import ExitStack, contextmanager

import numpy as np
import concourse.bass as bass
from concourse import mybir

F32 = mybir.dt.float32
F32R = mybir.dt.float32r
ACT = mybir.ActivationFunctionType
ALU = mybir.AluOpType
AX_X = mybir.AxisListType.X

P = 128
D = 2048
KD = D // P
N_P, N_S = 256, 64
N = N_P + N_S
PAST = 128
KEYS = N_P + PAST + N_S
D_FF = 5632
WIN = 512
FFN_BLOCKS = D_FF // WIN
SSM_W, Q_LORA, KV_LORA, ROPE, MEM_W = 1024, 768, 512, 64, 512
NOPE, HEADS, MEM_HEADS, HD = 128, 16, 4, 128
COL_Q = SSM_W
COL_KV = COL_Q + Q_LORA
COL_KR = COL_KV + KV_LORA
COL_QM = COL_KR + ROPE
COL_GATE = COL_QM + MEM_W
EPS = 1e-6
MLA_SCALE = (NOPE + ROPE) ** -0.5
MEM_SCALE = HD ** -0.5
S_TILES = 32
S_IT = 4
S_STEPS = S_TILES // S_IT
T_BLK = 4
B_P, B_S = N_P // T_BLK, N_S // T_BLK
BLKS = B_P + 1 + B_S
RAW, SPL = 3, 4

G_FFN1, G_MIX, G_FFN2, G_FIN, G_MEM, G_Q, G_KV, G_BGLU, G_D = 0, 16, 32, 48, 64, 80, 86, 90, 98
G_COLS = 98 + S_TILES
C_ID, C_PERM, C_COS, C_SIN, C_HALF, C_MASK = 0, 128, 256, 576, 896, 1024
C_COLS = 1280
S_ARE, S_AIM, S_LDT, S_H0RE, S_H0IM = range(5)
(V_ZRE, V_LRE, V_ZIM, V_LIM, V_NZRE, V_NLRE, V_L2RE, V_L2IM, V_R4, V_C1, V_S1, V_R, V_DT, V_AR, V_PH, V_PS, V_PC,
 V_K, V_INV, V_T, V_NR, V_T2) = range(22)

FFN_CH = 24 * FFN_BLOCKS
CH_MEM = 0
CH_FFN1 = CH_MEM + 16
CH_Z = CH_FFN1 + FFN_CH
CH_MLA = CH_Z + 56
CH_GLU = CH_MLA + 4 * 12
CH_MERGE = CH_GLU + 8
CH_FFN2 = CH_MERGE + 4 * 48
CH_END = CH_FFN2 + FFN_CH
GR_MEM = (0, 0)
GR_FFN1 = (1, 1)
GR_Z = (1 + 33, 1 + 33)
GR_MLA = (GR_Z[0] + 6, GR_Z[1] + 1)
GR_GLU = (GR_MLA[0] + 16, GR_MLA[1])
GR_MERGE = (GR_GLU[0] + 1, GR_GLU[1] + 1)
GR_FFN2 = (GR_MERGE[0] + 20, GR_MERGE[1] + 20)
GR_END = (GR_FFN2[0] + 33, GR_FFN2[1] + 33)
SQ = {"mem": 0, "ffn1": 8, "mix": 16, "q": 24, "kv": 27, "ffn2": 29, "fin": 37}
AP = {"mem": 0, "ffn1": 8, "mix": 16, "q": 24, "kv": 27, "mix2": 29, "ffn2": 37, "fin": 45}
NORM = {"mem": 0, "ffn1": 1, "mix": 2, "q": 3, "kv": 4, "ffn2": 5, "fin": 6}
MLA_LINKS, MERGE_LINKS = 12, 5
AT_MEM, AT_MLA = 0, MEM_HEADS

MLA_ATT = dict(
    tiles=[(0, 128, 0, 128, 4, 0), (128, 128, 0, 256, 4, 128), (256, 64, 256, 192, 5, 0)],
    pcols=[0, 128, 384],
    turns=[(0, 0, 128, 6, 0), (1, 0, 128, 6, 128), (1, 128, 128, 6, 256), (2, 0, 128, 6, 384), (2, 128, 64, 6, 448)],
    copies=[(128, 0, 448, 6, 0), (64, 448, 512, 6, 448)], pv_bank=7,
    pv=[(0, 128, 0, 256, 0, True, False), (1, 128, 256, 128, 128, False, True),
        (2, 128, 384, 64, 256, True, False), (3, 64, 448, 64, 256, False, True)],
    scale=MLA_SCALE)
MEM_ATT = dict(
    tiles=[(0, 128, 0, 256, 4, 0), (128, 128, 0, 256, 4, 256), (256, 64, 256, 256, 5, 0)],
    pcols=[0, 256, 512],
    turns=[(0, 0, 128, 6, 0), (1, 0, 128, 6, 128), (0, 128, 128, 6, 256), (1, 128, 128, 6, 384),
           (2, 0, 128, 7, 320), (2, 128, 128, 7, 384)],
    pv=[(0, 128, 0, 256, 0, True, False), (1, 128, 256, 256, 0, False, True),
        (2, 128, 512, 64, 256, True, False), (3, 128, 576, 64, 256, False, True)],
    copies=[(128, 0, 512, 6, 0), (128, 512, 640, 7, 320)], pv_bank=7, scale=MEM_SCALE)


def build(nc, t_in, t_out):
    with ExitStack() as ctx:
        def psum(name, shape):
            return ctx.enter_context(nc.psum_tensor(name, shape, F32))

        def sem(name):
            return ctx.enter_context(nc.semaphore(name))

        BASE = 16512
        END = nc.sbuf_usable_end

        class Region:

            def __init__(self, at):
                self.at = at

            def take(self, name, cols, dt=F32):
                shape = [P] + (list(cols) if isinstance(cols, (list, tuple)) else [cols])
                size = 4
                for c in shape[1:]:
                    size *= c
                t = nc.alloc_sbuf_tensor_at(name, shape, dt, offset=self.at)
                self.at += (size + 31) // 32 * 32
                assert self.at <= END, (name, self.at, END)
                return t

        R = Region(BASE)
        const = R.take("const", C_COLS)
        ones = R.take("ones", P)
        gains = R.take("gains", G_COLS)
        s5p = R.take("s5p", [5, S_TILES])
        s5v = R.take("s5v", [22, S_TILES])
        states = R.take("states", [4, S_TILES])
        stats = R.take("stats", [4, 4])
        rstd = R.take("rstd", N)
        rstd_mix = R.take("rstd_mix", N)
        mean = R.take("mean", N)
        x = R.take("x", [KD, N])
        raw = R.take("raw", [RAW, 2 * WIN])
        whi = R.take("whi", [SPL, 2 * WIN], F32R)
        wlo = R.take("wlo", [SPL, 2 * WIN], F32R)
        n0 = R.at
        sq = R.take("sq", [2, 2, N])
        hf = R.take("hf", [2, 2, N])
        sqs = [sq[:, 0], sq[:, 1], hf[:, 0], hf[:, 1]]
        M = Region(n0)
        gate = M.take("gate", [4, N])
        merged = M.take("merged", [4, N])
        assert M.at <= R.at
        u = Region(n0).take("u", [8, N])
        M = Region(n0)
        s_t = M.take("s_t", [S_IT, BLKS])
        s_t2 = M.take("s_t2", [S_IT, BLKS])
        v_re = M.take("v_re", [S_IT, BLKS])
        v_im = M.take("v_im", [S_IT, BLKS])
        dec = M.take("dec", [S_IT, BLKS])
        ycur = M.take("ycur", [S_IT, BLKS])
        assert M.at <= R.at
        h0 = R.at
        hhi = R.take("hhi", [KD, N], F32R)
        hlo = R.take("hlo", [KD, N], F32R)
        v0 = R.at

        V = Region(v0)
        mkT = V.take("mkT", [MEM_HEADS, 512])
        mv = V.take("mv", [4, MEM_W])
        v16 = V.at
        memT = Region(v16).take("memT", [KD, 256])
        B = Region(v16)
        silu_g = B.take("silu_g", [4, N])
        prod = B.take("prod", [4, N])
        phi = B.take("phi", [4, N], F32R)
        plo = B.take("plo", [4, N], F32R)
        Z = Region(v16)
        cqT = Z.take("cqT", [6, N])
        ckvT = Z.take("ckvT", [4, N])
        krraw = Z.take("krraw", N)
        qmT = Z.take("qmT", [MEM_HEADS, N])
        S = Region(Z.at)
        mem_p = [Z.take(f"mem_p{b}", 768) for b in range(2)]
        mem_pT = Z.take("mem_pT", 640)
        ymf = Z.take("ymf", [4, N])
        assert Z.at <= v0 + 61440
        T = Region(v0 + 61440)
        ymhi = T.take("ymhi", [4, N], F32R)
        ymlo = T.take("ymlo", [4, N], F32R)
        T = Region(v0 + 71680)
        u4 = T.take("u4", [S_TILES, BLKS])
        pq = [S.take(f"pq{b}", [2, T_BLK, 2, S_IT, 16]) for b in range(2)]
        sw = [S.take(f"sw{b}", [8, S_IT, 16]) for b in range(2)]
        elh = S.take("elh", [2, 2, S_TILES, 8])
        bp = S.take("bp", [2, S_IT, T_BLK, 32])
        qp = S.take("qp", [2, S_IT, T_BLK, 32])
        pT = S.take("pT", [2, S_IT, P])
        tz = S.take("tz", [S_IT, P])
        ee = S.take("ee", [2, S_IT, BLKS])
        xs = S.take("xs", [2, S_IT, BLKS + 1])
        assert S.at <= v0 + 71680
        S = Region(v0 + 39680)
        uph = S.take("uph", [6, 2, S_TILES])
        e_t = S.take("e_t", [2, S_TILES, 4])
        assert S.at <= v0 + 43776
        T = Region(v0 + 71680)
        mhi = T.take("mhi", [4, N], F32R)
        mlo = T.take("mlo", [4, N], F32R)
        L = Region(h0)
        cqhi = L.take("cqhi", [6, N], F32R)
        cqlo = L.take("cqlo", [6, N], F32R)
        lathi = L.take("lathi", [4, 512], F32R)
        latlo = L.take("latlo", [4, 512], F32R)
        kr = L.take("kr", [2, KEYS])
        krot = L.take("krot", N)
        assert L.at <= v0
        K1 = Region(v0 + 20480)
        qn = K1.take("qn", [4, N])
        qraw = K1.take("qraw", [2, N])
        qrope = K1.take("qrope", [2, N])
        kn = K1.take("kn", [4, KEYS])
        mla_p0 = K1.take("mla_p0", 576)
        assert K1.at <= v0 + 40960
        ymla = Region(v0).take("ymla", [HEADS, N])
        K2 = Region(v0 + 40960)
        vv = K2.take("vv", [4, WIN])
        mla_pT = K2.take("mla_pT", 512)
        mla_p = [mla_p0, K2.take("mla_p1", 576)]
        past = K2.take("past", [4, PAST])
        latf = K2.take("latf", [4, N])
        assert K2.at <= v0 + 61440
        rstd_kv = Region(v0 + 51200).take("rstd_kv", N)
        U = Region(v0 + 20480)
        yshi = U.take("yshi", [8, N], F32R)
        yslo = U.take("yslo", [8, N], F32R)
        gyhi = Region(v0 + 71680).take("gyhi", [8, N], F32R)
        gylo = Region(n0).take("gylo", [8, N], F32R)
        U = Region(v0 + 40960)
        sgl = U.take("sgl", [8, N])
        hf2 = U.take("hf2", [2, 2, N])
        yalo = Region(v0).take("yalo", [HEADS, N], F32R)
        y = Region(v0).take("y", [8, 2, N])
        yahi = Region(v0 + 40960).take("yahi", [HEADS, N], F32R)

        banks = psum("banks", [P, 8, 512])

        const_in = sem("const_in")
        x_in = sem("x_in")
        s5p_in = sem("s5p_in")
        mem_in = [sem(f"mem_in{q}") for q in range(4)]
        memkv_in = sem("memkv_in")
        past_in = sem("past_in")
        s5_in = [sem("s5_in0"), sem("s5_in1")]
        raw_in = [sem(f"raw_in{i}") for i in range(RAW)]
        w_hi = sem("w_hi")
        w_lo = sem("w_lo")
        w_used = sem("w_used")
        half_free = [sem("half0_free"), sem("half1_free")]
        ones_set = sem("ones_set")
        sq_ready = sem("sq_ready")
        sq_added = sem("sq_added")
        sq_used = sem("sq_used")
        mean_ready = sem("mean_ready")
        rstd_ready = sem("rstd_ready")
        hf_ready = sem("hf_ready")
        hf_hi = sem("hf_hi")
        hf_lo = sem("hf_lo")
        prod_set = sem("prod_set")
        prod_hi = sem("prod_hi")
        prod_lo = sem("prod_lo")
        past_hi = sem("past_hi")
        past_lo = sem("past_lo")
        lat_out = sem("lat_out")
        y_out = sem("y_out")
        kr_turned = sem("kr_turned")
        kr_rotated = sem("kr_rotated")
        q_turned = sem("q_turned")
        q_rotated = sem("q_rotated")
        scores = sem("scores")
        max_ready = sem("max_ready")
        exp_ready = sem("exp_ready")
        p_ready = sem("p_ready")
        p_turned = sem("p_turned")
        pT_ready = sem("pT_ready")
        pv_done = sem("pv_done")
        pv_out = sem("pv_out")
        ym_split = sem("ym_split")
        dve_link = sem("dve_link")
        s5_exp = sem("s5_exp")
        s5_arg = sem("s5_arg")
        s5_sin = sem("s5_sin")
        pads_set = sem("pads_set")
        pq_ready = sem("pq_ready")
        b_padded = sem("b_padded")
        q_padded = sem("q_padded")
        s5_turned = sem("s5_turned")
        own_ready = sem("own_ready")
        pT_set = sem("pT_set")
        tz_set = sem("tz_set")
        bu_ready = sem("bu_ready")
        bu_read = sem("bu_read")
        s5_x = sem("s5_x")
        s5_y = sem("s5_y")
        ycur_ready = sem("ycur_ready")
        gelu_ready = sem("gelu_ready")
        u_ready = sem("u_ready")
        gy_hi = sem("gy_hi")
        gy_lo = sem("gy_lo")
        ys_split = sem("ys_split")
        ya_split = sem("ya_split")
        m_split = sem("m_split")
        mkv_out = sem("mkv_out")
        states_out = sem("states_out")

        def wait(e, s, base, i=None, per=0):
            e.wait_ge(s, base if i is None else i * per + base)

        def rows(w, r0, n, c0, width):
            return w[bass.ds(r0, n * P), bass.ds(c0, width)].rearrange("(t p) c -> p t c", p=P)


        def load(e, c, src, n, width, i=None, per=0):
            slot = c % RAW
            if c >= RAW:
                wait(e, w_lo, c - RAW + 1, i, per)
            e.dma_start(raw[:, slot, 0:n * width].rearrange("p (t c) -> p t c", t=n), src).then_inc(raw_in[slot], 16)

        def round_w(e, c, size, i=None, per=0):
            slot = c % RAW
            wait(e, raw_in[slot], 16 * (c // RAW + 1), i, 16 * per // RAW)
            if c >= SPL:
                wait(e, w_used, c - SPL + 1, i, per)
            e.activation(whi[:, c % SPL, 0:size], raw[:, slot, 0:size], ACT.Copy).then_inc(w_hi, 1)

        def split_w(e, c, size, i=None, per=0):
            wait(e, w_hi, c + 1, i, per)
            e.tensor_tensor(wlo[:, c % SPL, 0:size], raw[:, c % RAW, 0:size],
                            whi[:, c % SPL, 0:size].bitcast(F32), ALU.subtract).then_inc(w_lo, 1)

        def three(e, out, hi_s, lo_s, hi_m, lo_m, start, stop):
            e.matmul(out, hi_s, hi_m, start=start, stop=False)
            e.matmul(out, hi_s, lo_m, start=False, stop=False)
            return e.matmul(out, lo_s, hi_m, start=False, stop=stop)

        def products(e, c, half, n, width, tiles, ahi, alo, k, first, last, cols=N, i=None, per=0):
            wait(e, w_lo, c + 1, i, per)
            s = c % SPL
            wh = whi[:, s, 0:n * width].rearrange("p (t c) -> p t c", t=n)
            wl = wlo[:, s, 0:n * width].rearrange("p (t c) -> p t c", t=n)
            for q in range(n):
                for m in range(tiles):
                    a, b = wh[:, q, m * P:(m + 1) * P], wl[:, q, m * P:(m + 1) * P]
                    ins = three(e, banks[:, 4 * half + m, 0:cols], a, b, ahi[:, k + q, 0:cols], alo[:, k + q, 0:cols],
                                first and q == 0, last and q == n - 1)
            ins.then_inc(w_used, 1)

        def token_products(e, c, half, n, tiles, ahi, alo, k, first, last, i=None, per=0):
            wait(e, w_lo, c + 1, i, per)
            s = c % SPL
            wh = whi[:, s, :].rearrange("p (t c) -> p t c", t=n)
            wl = wlo[:, s, :].rearrange("p (t c) -> p t c", t=n)
            for q in range(n):
                for m in range(tiles):
                    o = banks[:, 4 * half + m, :]
                    sl = slice(m * P, (m + 1) * P)
                    e.matmul(o, ahi[:, k + q, sl], wh[:, q, :], start=first and q == 0, stop=False)
                    e.matmul(o, alo[:, k + q, sl], wh[:, q, :], start=False, stop=False)
                    ins = e.matmul(o, ahi[:, k + q, sl], wl[:, q, :], start=False, stop=last and q == n - 1)
            ins.then_inc(w_used, 1)

        def ffn_order(first, last):
            g = [("gate", k) for k in range(8)]
            d = [("down", k) for k in range(8)]
            up = [("up", k) for k in range(8)]
            return g + up if first else d if last else g + d + up

        def ffn_stream(e, c0, visit):
            for j, (kind, k) in enumerate(ffn_order(True, False)):
                visit(c0 + j, kind, k, 0, None, 0, "head")
            with e.Fori(0, FFN_BLOCKS - 1) as i:
                for j, (kind, k) in enumerate(ffn_order(False, False)):
                    visit(c0 + 16 + j, kind, k, i, i, 24, "body")
            ce = c0 + 16 + 24 * (FFN_BLOCKS - 1)
            for j, (kind, k) in enumerate(ffn_order(False, True)):
                visit(ce + j, kind, k, FFN_BLOCKS - 1, None, 0, "tail")

        BR = [("ssm", 4, 2, D), ("mla", 8, 2, D + SSM_W), ("mem", 4, 1, D + SSM_W + HEADS * HD)]

        def merge_order(step):
            out, groups = [], [0, 0]

            def window(kind, b, chunks, first, half):
                out.extend((kind, b, first + k, half, groups[half]) for k in range(chunks))
                groups[half] += 1

            for b, (name, nch, n, row) in enumerate(BR):
                if step != "tail":
                    window("gate", b, 8, 0, 0)
                if b == 0 and step != "head":
                    for w in range(4):
                        window("out", 0, 2, 2 * w, 1 - w % 2)
                if step != "tail":
                    window("branch", b, nch, 0, 1)
            return out

        def merge_stream(e, visit, loop=None):
            c, g = CH_MERGE, GR_MERGE
            for j, item in enumerate(merge_order("head")):
                visit(c + j, item, None, "head", g)
            c, g = c + 40, (g[0] + 3, g[1] + 3)
            with (loop or (lambda: e.Fori(0, 3)))() as i:
                for j, item in enumerate(merge_order("body")):
                    visit(c + j, item, i, "body", g)
            c, g = c + 3 * 48, (g[0] + 15, g[1] + 15)
            for j, item in enumerate(merge_order("tail")):
                visit(c + j, item, None, "tail", g)

        Z_WIN = [(0, 512, 0), (512, 512, 1), (COL_Q + 512, 256, 0), (COL_KR, 128, 0), (COL_Q, 512, 0),
                 (COL_KV, 512, 0), (COL_QM, 512, 0)]

        z_cols = [width for _, width, _ in Z_WIN[2:] for _ in range(8)]
        S5_GAP = 3.4 * WIN

        def z_chunk(cols):
            n = 0
            while n < 40 and sum(z_cols[:n]) < cols:
                n += 1
            return 16 + n

        S5_B = [z_chunk(2.6 * WIN + S5_GAP * s) for s in range(S_STEPS)]
        S5_C = [z_chunk(2.6 * WIN + S5_GAP * s + 2.3 * WIN) for s in range(S_STEPS)]
        S5_A = [20] + [z_chunk(2.6 * WIN + S5_GAP * s - 2 * WIN) for s in range(1, S_STEPS)]

        def s5_slots(parts):
            at, rest = {}, []
            turn = dict(B=0, A=-9, C=2, pad_b=0, turned=1, own=2, pad_q=3, gelu=14, drain=0)
            for n, part, s in sorted(parts, key=lambda a: (a[0], 10 * a[2] + turn[a[1]])):
                if n < 56:
                    at.setdefault(n, []).append((part, s))
                else:
                    rest.append((part, s))
            return at, rest

        MLA_ORDER = ([("uq", un, k, n) for un in range(2) for k, n in ((0, 2), (2, 2), (4, 1), (5, 1))]
                     + [("uk", 0, 0, 2), ("uk", 0, 2, 2), ("uv", 0, 0, 2), ("uv", 0, 2, 2)])
        QW = 2 * (NOPE + ROPE)

        def size_of_mla(kind, n):
            return n * (QW if kind == "uq" else WIN)

        with nc.Block() as block:
            @block.sync
            def _(e):
                e.dma_start(s5p[:], t_in["s5p"]).then_inc(s5p_in, 16)
                for q in range(4):
                    e.dma_start(memT[:, 4 * q:4 * q + 4, :],
                                t_in["memT"][512 * q:512 * q + 512].rearrange("(t p) n -> p t n", p=P)).then_inc(mem_in[q], 16)
                e.dma_start(gains[:], t_in["gains"]).then_inc(const_in, 16)
                for k in range(3):
                    load(e, CH_MEM + k, rows(t_in["w_mem_k"], 256 * k, 2, 0, WIN), 2, WIN)
                e.dma_start(const[:], t_in["const"]).then_inc(const_in, 16)
                e.dma_start(x[:], t_in["xT"].rearrange("(t p) n -> p t n", p=P)).then_inc(x_in, 16)
                e.dma_start(mkT[:, :, 256:512], t_in["cmkT"].rearrange("(h p) n -> p h n", p=P)).then_inc(memkv_in, 16)
                e.dma_start(mv[:, 2:4, :], t_in["cmv"].rearrange("(t p) n -> p t n", p=P)).then_inc(memkv_in, 16)
                for w, name in enumerate(("w_mem_k", "w_mem_v")):
                    for k in range(3 if w == 0 else 0, 8):
                        load(e, CH_MEM + 8 * w + k, rows(t_in[name], 256 * k, 2, 0, WIN), 2, WIN)

                def ffn_loads(c0, name):
                    def visit(c, kind, k, b, i, per, step):
                        w = t_in[f"{name}_w_{kind}"]
                        if kind == "down":
                            r0 = b * WIN + (k % 2) * 256
                            c_at = (k // 2) * WIN
                        else:
                            r0 = k * 256
                            c_at = 0 if step == "head" else b * WIN + WIN
                        if step == "body":
                            if kind == "down":
                                r0 = e.snap(r0)
                            else:
                                c_at = e.snap(c_at)
                        load(e, c, rows(w, r0, 2, c_at, WIN), 2, WIN, i, per)
                    ffn_stream(e, c0, visit)

                ffn_loads(CH_FFN1, "ffn1")
                e.wait_ge(half_free[0], 1)
                e.wait_ge(half_free[1], 1)
                e.dma_start(t_out["mkT"].rearrange("(h p) n -> p h n", p=P), mkT[:, :, 0:256]).then_inc(mkv_out, 16)
                e.dma_start(t_out["mv"].rearrange("(t p) n -> p t n", p=P), mv[:, 0:2, :]).then_inc(mkv_out, 16)
                def s5_load(s):
                    if s >= 2:
                        e.wait_ge(own_ready, s - 1)
                    e.dma_start(sw[s % 2][:], t_in["s5w"][:, s]).then_inc(s5_in[s % 2], 16)

                s5_load(0)
                s5_load(1)
                c = CH_Z
                for c_at, width, half in Z_WIN:
                    for k in range(8):
                        n = c - CH_Z
                        for s in range(2, S_STEPS):
                            if n == min(S5_A[s - 2] + 6, S5_A[s]):
                                s5_load(s)
                        w, at = (t_in["w_kr2"], 0) if width == 128 else (t_in["w_in"], c_at)
                        load(e, c, rows(w, 256 * k, 2, at, width), 2, width)
                        c += 1
                def mla_load(j, i=None):
                    kind, un, k, n = MLA_ORDER[j]
                    width = QW if kind == "uq" else WIN
                    if i is None:
                        c, c_at = CH_MLA + j, un * QW if kind == "uq" else 0
                    else:
                        c = CH_MLA + 12 + j
                        c_at = e.snap(i * 2 * QW + (2 + un) * QW) if kind == "uq" else e.snap(i * WIN + WIN)
                    load(e, c, rows(t_in["w_" + kind], k * P, n, c_at, width), n, width, i, 12)

                for j in range(3):
                    mla_load(j)
                e.wait_ge(ycur_ready, S_STEPS)
                e.wait_ge(half_free[0], GR_MLA[0])
                e.dma_start(past[:], t_in["platT"].rearrange("(t p) n -> p t n", p=P)).then_inc(past_in, 16)
                e.dma_start(kr[0:64, 0, N_P:N_P + PAST], t_in["pkrT"]).then_inc(past_in, 16)
                e.dma_start(kr[64:128, 1, N_P:N_P + PAST], t_in["pkrT"]).then_inc(past_in, 16)
                e.dma_start(t_out["states"], states[:]).then_inc(states_out, 16)
                for j in range(3, 12):
                    mla_load(j)
                e.wait_ge(hf_ready, AP["kv"] + 2)
                e.dma_start(t_out["latT"].rearrange("(t p) n -> p t n", p=P), latf[:]).then_inc(lat_out, 16)
                e.wait_ge(kr_rotated, 1)
                e.dma_start(t_out["krT"], krot[0:64, :]).then_inc(lat_out, 16)
                with e.Fori(0, 3) as i:
                    for j in range(12):
                        mla_load(j, i)
                for w in range(2):
                    for k in range(4):
                        load(e, CH_GLU + 4 * w + k, rows(t_in["ssm_w_glu"], 256 * k, 2, w * WIN, WIN), 2, WIN)

                def merge_load(c, item, i, step, g):
                    kind, b, k, half, before = item
                    n = BR[b][2] if kind == "branch" else 2
                    if kind == "out":
                        r_at = (k % 2) * 256 + (i * WIN if step == "body" else 3 * WIN)
                        src = rows(t_in["w_post"], e.snap(r_at) if step == "body" else r_at, 2, (k // 2) * WIN, WIN)
                    elif kind == "gate":
                        c_at = e.snap(i * WIN + (COL_GATE + b * D + WIN)) if step == "body" else COL_GATE + b * D
                        src = rows(t_in["w_in"], 256 * k, 2, c_at, WIN)
                    else:
                        c_at = e.snap(i * WIN + WIN) if step == "body" else 0
                        src = rows(t_in["w_post"], BR[b][3] + n * P * k, n, c_at, WIN)
                    load(e, c, src, n, WIN, i, 48)
                merge_stream(e, merge_load)
                ffn_loads(CH_FFN2, "ffn2")
                out = t_out["yT"].rearrange("(t p) n -> p t n", p=P)
                for p in range(8):
                    e.wait_ge(hf_ready, AP["fin"] + p + 1)
                    e.dma_start(out[:, 2 * p:2 * p + 2, :], y[:, p]).then_inc(y_out, 16)
                e.wait_ge(y_out, 128)
                e.wait_ge(mkv_out, 32)
                e.wait_ge(states_out, 16)
                e.wait_ge(lat_out, 32)

            @block.scalar
            def _(e):
                def squares(name, src, pairs, cols=N, groups=None, first_half=0, first=0):
                    for p in range(first, pairs):
                        if name == "mem" and p % 2 == 0:
                            e.wait_ge(mem_in[p // 2], 16)
                        if groups and p % 2 == 0:
                            w = p // 2
                            h = (w + first_half) % 2
                            e.wait_ge(half_free[h], groups[h] - (1 if w < 2 else 0))
                        if p >= 4 or SQ[name]:
                            e.wait_ge(sq_used, SQ[name] + max(p - 3, 0))
                        e.activation(sqs[p % 4][:, :, 0:cols], src[:, 2 * p:2 * p + 2, :], ACT.Square).then_inc(sq_ready, 1)

                def squares_and_rounds(name, c0, groups, first_half):
                    round_w(e, c0, 2 * WIN)
                    round_w(e, c0 + 1, 2 * WIN)
                    squares(name, x, 4, groups=groups, first_half=first_half)
                    round_w(e, c0 + 2, 2 * WIN)
                    squares(name, x, 8, groups=groups, first_half=first_half, first=4)

                def root(name, out, cols=N):
                    e.wait_ge(mean_ready, 2 * NORM[name] + 2)
                    e.activation(out[:, 0:cols], mean[:, 0:cols], ACT.Sqrt).then_inc(rstd_ready, 1)

                def round_h(name, out, pairs, cols=N, first=0, src=hf):
                    for p in range(first, pairs):
                        e.wait_ge(hf_ready, AP[name] + p + 1)
                        e.activation(out[:, 2 * p:2 * p + 2, 0:cols], src[:, p % 2, :, 0:cols], ACT.Copy).then_inc(hf_hi, 1)

                e.wait_ge(s5p_in, 16)
                e.activation(s5v[:, V_DT], s5p[:, S_LDT], ACT.Exp).then_inc(s5_exp, 1)
                e.wait_ge(s5_arg, 1)
                e.activation(s5v[:, V_R], s5v[:, V_AR], ACT.Exp).then_inc(s5_exp, 1)
                e.wait_ge(s5_arg, 2)
                e.activation(s5v[:, V_S1], s5v[:, V_PS], ACT.Sin).then_inc(s5_sin, 1)
                e.activation(s5v[:, V_C1], s5v[:, V_PC], ACT.Sin).then_inc(s5_sin, 1)
                squares("mem", memT, 8, 256)
                for c in range(3):
                    round_w(e, CH_MEM + c, 2 * WIN)
                root("mem", rstd, 256)
                round_h("mem", hhi, 8, 256)
                for c in range(3, 12):
                    round_w(e, CH_MEM + c, 2 * WIN)
                e.wait_ge(x_in, 16)
                e.wait_ge(hf_lo, AP["mem"] + 8)
                squares("ffn1", x, 8)
                root("ffn1", rstd)
                for c in range(12, 20):
                    round_w(e, CH_MEM + c, 2 * WIN)
                    e.wait_ge(w_used, CH_MEM + 8 + c - 12 + 1)
                    round_h("ffn1", hhi, c - 11, first=c - 12)

                def ffn(name, c0, gr):
                    if name == "ffn2":
                        squares_and_rounds(name, c0, gr, 1)
                        root(name, rstd)
                        round_h(name, hhi, 8)

                    def silu(c_last, i, per, body):
                        wait(e, w_used, c_last + 1, i, per)
                        if body:
                            wait(e, half_free[1], gr[1] + 1, i, 3)
                        for m in range(4):
                            ins = e.activation(silu_g[:, m], banks[:, m, 0:N], ACT.Silu)
                        ins.then_inc(half_free[0], 1)

                    def visit(c, kind, k, b, i, per, step):
                        if c >= c0 + (4 if name == "ffn1" else 3):
                            round_w(e, c, 2 * WIN, i, per)
                        if step == "head" and kind == "up" and k == 2:
                            silu(c - 3, i, per, False)
                        if step == "body" and kind == "down" and k == 2:
                            silu(c - 3, i, per, True)
                    ffn_stream(e, c0, visit)

                ffn("ffn1", CH_FFN1, GR_FFN1)
                squares_and_rounds("mix", CH_Z, GR_Z, 0)
                root("mix", rstd_mix)
                round_h("mix", hhi, 8)
                def s5_act(part, s):
                    b = s % 2
                    if part == "pad_b":
                        e.wait_ge(pq_ready, s + 1)
                        if s == 0:
                            e.wait_ge(pads_set, 3)
                        else:
                            e.wait_ge(own_ready, s)
                        for g in range(2):
                            r = slice(64 * g, 64 * g + 64)
                            for k in range(T_BLK):
                                ins = e.activation(bp[r, :, :, k, 16 * g:16 * g + 16], pq[b][r, :, T_BLK - 1 - k, 0],
                                                   ACT.Copy)
                        ins.then_inc(b_padded, 1)
                    elif part == "pad_q":
                        if s >= 1:
                            e.wait_ge(s5_y, s)
                        for g in range(2):
                            r = slice(64 * g, 64 * g + 64)
                            for z in range(2):
                                ins = e.activation(qp[r, z, :, :, 16 * g:16 * g + 16].rearrange("p i j h -> p j i h"),
                                                   pq[b][r, z, :, 1], ACT.Copy)
                        ins.then_inc(q_padded, 1)
                    elif part == "turned":
                        e.wait_ge(s5_turned, s + 1)
                        if s >= 1:
                            e.wait_ge(bu_ready, s)
                        for z in range(2):
                            ins = e.activation(pT[:, z], banks[:, 4 + z, :].rearrange("p (i m) -> p i m", i=S_IT),
                                               ACT.Copy)
                        ins.then_inc(pT_set, 1)
                    elif part == "own":
                        e.wait_ge(own_ready, s + 1)
                        if s >= 1:
                            e.wait_ge(s5_y, s)
                        own = banks[:, 6, 384:512].rearrange("p (i h) -> p i h", i=S_IT)
                        for k in range(T_BLK):
                            for j in range(k, T_BLK):
                                r = 32 * (T_BLK - 1 - (j - k))
                                ins = e.activation(tz[32 * k:32 * k + 32, :, 32 * j:32 * j + 32], own[r:r + 32],
                                                   ACT.Copy)
                        ins.then_inc(tz_set, 1)
                    else:
                        e.wait_ge(ycur_ready, s + 1)
                        e.activation(u4[:, S_IT * s:S_IT * s + S_IT, :], ycur[:],
                                     ACT.Gelu_apprx_tanh).then_inc(gelu_ready, 1)

                parts = []
                for s in range(S_STEPS):
                    last = max(S5_A[s], S5_C[s - 1]) if s else S5_A[s]
                    parts += [(S5_A[s] + 2, "pad_b", s), (S5_A[s] + 3, "turned", s), (last + 3, "own", s),
                              (last + 4, "pad_q", s), (S5_C[s] + 6, "gelu", s)]
                parts.append((59, "drain", 6))
                s5_at, s5_rest = s5_slots(parts)

                def drain(w):
                    e.wait_ge(w_used, CH_Z + 8 * (w + 1))
                    n = Z_WIN[w][1] // P
                    src = banks[:, 0:n, 0:N] if n > 1 else banks[:, 0, 0:N]
                    e.activation(z_out[w - 2], src, ACT.Copy).then_inc(half_free[0], 1)

                z_out = [cqT[:, 4:6], krraw[:], cqT[:, 0:4], ckvT[:], qmT[:]]
                for n in range(56):
                    w = n // 8 - 1
                    if n % 8 == 3 and w >= 2:
                        drain(w)
                    for part, s in s5_at.get(n, []):
                        s5_act(part, s)
                    if n >= 3:
                        round_w(e, CH_Z + n, 2 * Z_WIN[n // 8][1])
                for part, s in s5_rest:
                    if part == "drain":
                        drain(s)
                    else:
                        s5_act(part, s)

                def softmax(att, p_sb, h, i=None):
                    wait(e, max_ready, h + 1, i, 4)
                    for t, (q0, nq, k0, nk, bank, col) in enumerate(att["tiles"]):
                        ins = e.activation(p_sb[0:nq, att["pcols"][t]:att["pcols"][t] + nk],
                                           banks[0:nq, bank, col:col + nk], ACT.Exp, scale=att["scale"],
                                           bias=stats[0:nq, 1, t:t + 1], accum_out=stats[0:nq, 2, t:t + 1])
                    ins.then_inc(exp_ready, 1)

                for j in range(3):
                    round_w(e, CH_MLA + j, size_of_mla(MLA_ORDER[j][0], MLA_ORDER[j][3]))
                e.wait_ge(gelu_ready, S_STEPS)
                squares("q", cqT, 3)
                squares("kv", ckvT, 2)
                root("q", rstd)
                root("kv", rstd_kv)
                round_h("q", cqhi, 3)
                for p in range(2):
                    e.wait_ge(hf_ready, AP["kv"] + p + 1)
                    for q in range(2):
                        ins = e.activation(lathi[:, 2 * p + q, 0:N_P], latf[:, 2 * p + q, 0:N_P], ACT.Copy)
                        ins = e.activation(lathi[:, 2 * p + q, N_P + PAST:KEYS], latf[:, 2 * p + q, N_P:N], ACT.Copy)
                    ins.then_inc(hf_hi, 1)
                e.wait_ge(past_in, 48)
                e.activation(lathi[:, :, N_P:N_P + PAST], past[:], ACT.Copy).then_inc(past_hi, 1)

                def mla_rounds(att, p_sb, base, c0, i=None):
                    for j, (kind, un, k, n) in enumerate(MLA_ORDER):
                        if j in (3, 5, 8, 10):
                            h = (3, 5, 8, 10).index(j)
                            softmax(att, p_sb[h % 2], base + h, i)
                        if c0 + j >= CH_MLA + 3:
                            round_w(e, c0 + j, size_of_mla(kind, n), i, 12)

                mla_rounds(MEM_ATT, mem_p, AT_MEM, CH_MLA)
                e.wait_ge(u_ready, 1)
                e.activation(gyhi[:], u[:], ACT.Copy).then_inc(gy_hi, 1)
                with e.Fori(0, 3) as i:
                    mla_rounds(MLA_ATT, mla_p, AT_MLA, CH_MLA + 12, i)
                for c in range(8):
                    if 3 <= c < 7:
                        softmax(MLA_ATT, mla_p[(c - 3) % 2], AT_MLA + 12 + c - 3)
                    round_w(e, CH_GLU + c, 2 * WIN)

                def glu_gate(w):
                    e.wait_ge(w_used, CH_GLU + 4 * w + 4)
                    for m in range(4):
                        ins = e.activation(sgl[:, 4 * w + m], banks[:, 4 * w + m, 0:N], ACT.Sigmoid,
                                           bias=gains[:, G_BGLU + 4 * w + m:G_BGLU + 4 * w + m + 1])
                    ins.then_inc(half_free[w], 1)

                e.wait_ge(pv_out, AT_MLA + 16)
                glu_gate(0)
                round_h("mix2", hhi, 8, src=hf2)
                for c in range(3):
                    round_w(e, CH_MERGE + c, 2 * WIN)
                glu_gate(1)

                def merge_act(c, item, i, step, g):
                    kind, b, k, half, before = item
                    n = BR[b][2] if kind == "branch" else 2
                    if c >= CH_MERGE + 3:
                        round_w(e, c, n * WIN, i, 48)
                    first = kind == "out" if b == 0 and step == "body" else kind == "branch"
                    if step != "tail" and first and k == 2:
                        wait(e, w_used, c - 2, i, 48)
                        if b == 0 and step == "head":
                            e.wait_ge(ys_split, 1)
                        wait(e, half_free[1], g[1] + (before if b else 0), i, 5)
                        for m in range(4):
                            ins = e.activation(gate[:, m], banks[:, m, 0:N], ACT.Sigmoid)
                        ins.then_inc(half_free[0], 1)
                merge_stream(e, merge_act)
                ffn("ffn2", CH_FFN2, GR_FFN2)
                squares("fin", x, 8, groups=GR_END)
                root("fin", rstd)

            @block.gpsimd
            def _(e):
                e.memset(ones[:], 1.0).then_inc(ones_set, 1)
                e.memset(bp[:], 0.0).then_inc(pads_set, 1)
                e.memset(qp[:], 0.0).then_inc(pads_set, 1)
                e.memset(tz[:], 0.0).then_inc(pads_set, 1)

                def split_h(name, out, hi, pairs, cols=N, first=0, src=hf):
                    for p in range(first, pairs):
                        e.wait_ge(hf_hi, AP[name] + p + 1)
                        e.tensor_tensor(out[:, 2 * p:2 * p + 2, 0:cols], src[:, p % 2, :, 0:cols],
                                        hi[:, 2 * p:2 * p + 2, 0:cols].bitcast(F32), ALU.subtract).then_inc(hf_lo, 1)

                def add_squares(name, pairs, cols=N, first=0):
                    for p in range(first, pairs):
                        e.wait_ge(sq_ready, SQ[name] + p + 1)
                        a = sqs[p % 4][:, :, 0:cols]
                        e.tensor_tensor(a[:, 0], a[:, 0], a[:, 1], ALU.add).then_inc(sq_added, 1)

                def squares_and_splits(name, c0):
                    split_w(e, c0, 2 * WIN)
                    split_w(e, c0 + 1, 2 * WIN)
                    add_squares(name, 4)
                    split_w(e, c0 + 2, 2 * WIN)
                    add_squares(name, 8, first=4)

                add_squares("mem", 8, 256)
                for c in range(3):
                    split_w(e, CH_MEM + c, 2 * WIN)
                split_h("mem", hlo, hhi, 8, 256)
                for c in range(3, 20):
                    if c == 12:
                        add_squares("ffn1", 8)
                    split_w(e, CH_MEM + c, 2 * WIN)
                    if c >= 12:
                        split_h("ffn1", hlo, hhi, c - 11, first=c - 12)

                def ffn_splits(c0, done):
                    def visit(c, kind, k, b, i, per, step):
                        if c >= c0 + done:
                            split_w(e, c, 2 * WIN, i, per)
                    ffn_stream(e, c0, visit)

                ffn_splits(CH_FFN1, 4)
                squares_and_splits("mix", CH_Z)
                split_h("mix", hlo, hhi, 8)
                c = CH_Z
                for c_at, width, half in Z_WIN:
                    for k in range(8):
                        if c >= CH_Z + 3:
                            split_w(e, c, 2 * width)
                        c += 1
                for j in range(3):
                    split_w(e, CH_MLA + j, size_of_mla(MLA_ORDER[j][0], MLA_ORDER[j][3]))
                add_squares("q", 3)
                add_squares("kv", 2)
                split_h("q", cqlo, cqhi, 3)
                for p in range(2):
                    e.wait_ge(hf_hi, AP["kv"] + p + 1)
                    for q in range(2):
                        ins = e.tensor_tensor(latlo[:, 2 * p + q, 0:N_P], latf[:, 2 * p + q, 0:N_P],
                                              lathi[:, 2 * p + q, 0:N_P].bitcast(F32), ALU.subtract)
                        ins = e.tensor_tensor(latlo[:, 2 * p + q, N_P + PAST:KEYS], latf[:, 2 * p + q, N_P:N],
                                              lathi[:, 2 * p + q, N_P + PAST:KEYS].bitcast(F32), ALU.subtract)
                    ins.then_inc(hf_lo, 1)
                e.wait_ge(past_hi, 1)
                e.tensor_tensor(latlo[:, :, N_P:N_P + PAST], past[:], lathi[:, :, N_P:N_P + PAST].bitcast(F32),
                                ALU.subtract).then_inc(past_lo, 1)
                e.memset(lathi[:, :, KEYS:512].bitcast(F32), 0.0)
                e.memset(latlo[:, :, KEYS:512].bitcast(F32), 0.0).then_inc(past_lo, 1)
                for j in range(3, 12):
                    split_w(e, CH_MLA + j, size_of_mla(MLA_ORDER[j][0], MLA_ORDER[j][3]))
                e.wait_ge(gy_hi, 1)
                e.tensor_tensor(gylo[:], u[:], gyhi[:].bitcast(F32), ALU.subtract).then_inc(gy_lo, 1)
                with e.Fori(0, 3) as i:
                    for j, (kind, un, k, n) in enumerate(MLA_ORDER):
                        split_w(e, CH_MLA + 12 + j, size_of_mla(kind, n), i, 12)
                for c in range(8):
                    split_w(e, CH_GLU + c, 2 * WIN)
                split_h("mix2", hlo, hhi, 8, src=hf2)
                merge_stream(e, lambda c, item, i, step, g: split_w(e, c, (BR[item[1]][2] if item[0] == "branch" else 2) * WIN,
                                                                    i, 48))
                squares_and_splits("ffn2", CH_FFN2)
                split_h("ffn2", hlo, hhi, 8)
                ffn_splits(CH_FFN2, 3)
                add_squares("fin", 8)

            @block.tensor
            def _(e):
                def sums(name, pairs, cols=N, bank=0, first=0, of=None):
                    for p in range(first, pairs):
                        e.wait_ge(sq_added, SQ[name] + p + 1)
                        e.matmul(banks[:, bank, 0:cols], ones[:], sqs[p % 4][:, 0, 0:cols], start=p == 0,
                                 stop=p == (of or pairs) - 1).then_inc(sq_used, 1)

                def window(half, c0, ahi, alo, tiles, width, kpairs, cols=N, norm=None):
                    for k in range(kpairs):
                        if norm is not None:
                            e.wait_ge(hf_lo, AP[norm] + k + 1)
                        products(e, c0 + k, half, 2, width, tiles, ahi, alo, 2 * k, k == 0, k == kpairs - 1, cols)

                e.wait_ge(ones_set, 1)
                sums("mem", 8, 256)
                e.wait_ge(mean_ready, 1)
                window(0, CH_MEM, hhi, hlo, 4, WIN, 8, cols=256, norm="mem")
                for k in range(8):
                    if k == 3:
                        sums("ffn1", 8, bank=7)
                    token_products(e, CH_MEM + 8 + k, 1, 2, 2, hhi, hlo, 2 * k, k == 0, k == 7)

                def ffn(name, c0, gr):
                    if name == "ffn2":
                        sums(name, 8, bank=4, first=4)
                    e.wait_ge(half_free[0], gr[0])
                    sbase = 0 if name == "ffn1" else FFN_BLOCKS

                    def visit(c, kind, k, b, i, per, step):
                        if kind in ("gate", "up"):
                            half = 0 if kind == "gate" else 1
                            if step == "head" and kind == "gate":
                                e.wait_ge(hf_lo, AP[name] + k + 1)
                            if step == "head" and kind == "up" and k == 0:
                                e.wait_ge(half_free[1], gr[1])
                                e.wait_ge(mean_ready, 2 * NORM[name] + 1)
                            if k == 0 and step == "body":
                                wait(e, half_free[half], gr[half] + (1 if kind == "gate" else 3), i, 3)
                            products(e, c, half, 2, WIN, 4, hhi, hlo, 2 * k, k == 0, k == 7, N, i, per)
                        else:
                            w = k // 2
                            half = (1, 0, 1, 0)[w] if step == "body" else (0, 1, 0, 1)[w]
                            if step == "tail" and k == 7:
                                e.wait_ge(half_free[0], gr[0] + 33)
                                sums("mix" if name == "ffn1" else "fin", 4, of=8)
                            if k < 2:
                                if step == "body":
                                    wait(e, prod_lo, 2 * sbase + k + 1, i, 2)
                                else:
                                    e.wait_ge(prod_lo, 2 * (sbase + FFN_BLOCKS - 1) + k + 1)
                            if k % 2 == 0:
                                if step == "body":
                                    wait(e, half_free[half], gr[half] + (1, 2, 2, 3)[w], i, 3)
                                else:
                                    e.wait_ge(half_free[half], gr[half] + 3 * (FFN_BLOCKS - 1) + 1 + w // 2)
                            products(e, c, half, 2, WIN, 4, phi, plo, 2 * (k % 2), k % 2 == 0, k % 2 == 1, N, i, per)
                    ffn_stream(e, c0, visit)

                ffn("ffn1", CH_FFN1, GR_FFN1)
                sums("mix", 8, first=4)
                e.wait_ge(mean_ready, 2 * NORM["mix"] + 1)
                seen = list(GR_Z)

                def s5_pe(part, s):
                    ident = const[:, C_ID:C_ID + P]
                    if part == "A":
                        e.wait_ge(b_padded, s + 1)
                        if s == 0:
                            e.wait_ge(half_free[1], GR_Z[1] + 1)
                        else:
                            e.wait_ge(pT_set, s)
                        if s >= 2:
                            e.wait_ge(ycur_ready, s - 1)
                        for z in range(2):
                            for i in range(S_IT):
                                ins = e.transpose(banks[:, 4 + z, i * P:(i + 1) * P],
                                                  bp[:, z, i].rearrange("p k h -> p (k h)"), ident)
                        ins.then_inc(s5_turned, 1)
                        if s >= 1:
                            e.wait_ge(bu_read, s)
                            e.wait_ge(tz_set, s)
                        for i in range(S_IT):
                            for z in range(2):
                                ins = e.matmul(banks[:, 6, 384 + 32 * i:384 + 32 * i + 32],
                                               bp[:, z, i].rearrange("p k h -> p (k h)"),
                                               sw[s % 2][:, 4 + 2 * z:6 + 2 * z].rearrange("p a i h -> p (a i h)")
                                               [:, 32 * i:32 * i + 32], start=z == 0, stop=z == 1)
                        ins.then_inc(own_ready, 1)
                    elif part == "B":
                        if s == 0:
                            e.wait_ge(half_free[0], GR_Z[0] + 1)
                        e.wait_ge(pT_set, s + 1)
                        e.wait_ge(tz_set, s + 1)
                        for z in range(2):
                            for i in range(S_IT):
                                ins = e.matmul(banks[:, 6 + z, BLKS * i:BLKS * i + BLKS], pT[:, z, i],
                                               u4[:, S_IT * s + i, :], start=True, stop=True)
                        ins.then_inc(bu_ready, 1)
                    else:
                        e.wait_ge(s5_x, s + 1)
                        e.wait_ge(q_padded, s + 1)
                        if s + 1 < S_STEPS:
                            e.wait_ge(pT_set, s + 2)
                        for i in range(S_IT):
                            o = banks[:, 4, BLKS * i:BLKS * i + BLKS]
                            for z in range(2):
                                e.matmul(o, qp[:, z, i].rearrange("p k h -> p (k h)"), xs[:, z, i, 0:BLKS],
                                         start=z == 0, stop=False)
                            ins = e.matmul(o, tz[:, i], u4[:, S_IT * s + i, :], start=False, stop=True)
                        ins.then_inc(s5_y, 1)

                parts = []
                for s in range(S_STEPS):
                    parts += [(S5_C[s], "C", s), (S5_A[s], "A", s), (S5_B[s], "B", s)]
                s5_at, s5_rest = s5_slots(parts)
                for w, (c_at, width, half) in enumerate(Z_WIN):
                    for k in range(8):
                        for part, s in s5_at.get(8 * w + k, []):
                            s5_pe(part, s)
                        if k == 0:
                            e.wait_ge(half_free[half], seen[half])
                            seen[half] += 1
                        if w == 0:
                            e.wait_ge(hf_lo, AP["mix"] + k + 1)
                        products(e, CH_Z + 8 * w + k, half, 2, width, width // P, hhi, hlo, 2 * k, k == 0, k == 7)
                for part, s in s5_rest:
                    s5_pe(part, s)

                def score(att, h0_, h, keys, queries, extra, i=None):
                    if h0_ + h >= 1:
                        wait(e, exp_ready, h0_ + h, i, 4)
                    for t, (q0, nq, k0, nk, bank, col) in enumerate(att["tiles"]):
                        ops = [(queries[:, h, q0:q0 + nq], keys[:, h, k0:k0 + nk])] + extra(h, t, q0, nq, k0, nk)
                        for n_, (a, b) in enumerate(ops):
                            ins = e.matmul(banks[0:nq, bank, col:col + nk], a, b, start=n_ == 0,
                                           stop=n_ == len(ops) - 1)
                    ins.then_inc(scores, 1)

                def turn(att, h0_, h, p_sb, i=None):
                    wait(e, p_ready, h0_ + h + 1, i, 4)
                    if att is MEM_ATT:
                        e.wait_ge(kr_rotated, 1)
                        if h >= 1:
                            e.wait_ge(pv_out, h0_ + h)
                    if h0_ + h >= 1:
                        wait(e, pT_ready, h0_ + h, i, 4)
                    for t, kk, nk, bank, col in att["turns"]:
                        nq = att["tiles"][t][1]
                        at = att["pcols"][t] + kk
                        ins = e.transpose(banks[0:nk, bank, col:col + nq], p_sb[h % 2][0:nq, at:at + nk],
                                          const[0:nq, C_ID:C_ID + nq])
                    ins.then_inc(p_turned, 1)

                def weigh(att, h0_, h, values, pT, i=None):
                    wait(e, pT_ready, h0_ + h + 1, i, 4)
                    if h0_ + h >= 1:
                        wait(e, pv_out, h0_ + h, i, 4)
                    for vt, nr, pc, nq, oc, st, sp_ in att["pv"]:
                        ins = e.matmul(banks[:, att["pv_bank"], oc:oc + nq], values[0:nr, vt, h * HD:(h + 1) * HD],
                                       pT[0:nr, pc:pc + nq], start=st, stop=sp_, skip_group_check=True)
                    ins.then_inc(pv_done, 1)

                e.wait_ge(half_free[0], GR_MLA[0])
                e.wait_ge(half_free[1], GR_MLA[1])
                e.wait_ge(ycur_ready, S_STEPS)
                sums("q", 3)
                sums("kv", 2, bank=1)
                e.matmul(banks[:, 7, 0:N], const[:, C_PERM:C_PERM + P], krraw[:], start=True, stop=True).then_inc(kr_turned, 1)
                e.wait_ge(mean_ready, 2 * NORM["kv"] + 1)
                e.wait_ge(memkv_in, 32)

                def extra(h, t, q0, nq, k0, nk):
                    ops = [(qrope[:, h // 2, q0:q0 + nq], kr[:, h % 2, k0:k0 + nk])]
                    if t < 2:
                        m0 = C_MASK + (128 if t == 0 else 0)
                        ops.append((const[0:1, C_HALF:C_HALF + nq], const[0:1, m0:m0 + nk]))
                    return ops

                def attend(part, h, base, i=None):
                    if part == "S":
                        if h == 0 and i is not None or h == 0 and base > AT_MLA:
                            wait(e, half_free[0], GR_MLA[0] + base - AT_MLA + 4, i, 4)
                            wait(e, q_rotated, (base - AT_MLA) // 2 + 2, i, 2)
                        score(MLA_ATT, base, h, kn, qn, extra, i)
                    elif part == "T":
                        turn(MLA_ATT, base, h, mla_p, i)
                    else:
                        weigh(MLA_ATT, base, h, vv, mla_pT, i)

                def remember(part, h):
                    if part == "S":
                        score(MEM_ATT, AT_MEM, h, mkT, qmT, lambda h, t, q0, nq, k0, nk: [])
                    elif part == "T":
                        turn(MEM_ATT, AT_MEM, h, mem_p)
                    else:
                        weigh(MEM_ATT, AT_MEM, h, mv, mem_pT)

                def mla_pass(first, i=None):
                    beside = {0: ["S0"], 2: ["S1", "T0"], 3: ["V0"], 5: ["S2", "T1"], 6: ["V1"],
                                               7: ["S3", "T2"], 8: ["V2"], 9: ["T3"], 10: ["V3"]}
                    n_pass = 0 if first else 1
                    for j, (kind, un, k, n) in enumerate(MLA_ORDER):
                        c = CH_MLA + 12 * n_pass + j
                        for part in beside.get(j, []):
                            if first:
                                remember(part[0], int(part[1]))
                            else:
                                attend(part[0], int(part[1]), AT_MLA, i)
                        if j == 10:
                            wait(e, exp_ready, AT_MLA + 4 if i is not None else MEM_HEADS, i, 4)
                            for r in range(2):
                                e.matmul(banks[:, 5 - r, 0:N], const[:, C_PERM:C_PERM + P], qraw[:, r], start=True,
                                         stop=True).then_inc(q_turned, 1)
                        if k == 0:
                            group = un if kind == "uq" else 2 if kind == "uk" else 3
                            wait(e, half_free[0], GR_MLA[0] + 4 * n_pass + group, i, 4)
                        if first and kind == "uq":
                            e.wait_ge(hf_lo, AP["q"] + k // 2 + 1)
                        if first and kind == "uk" and k == 0:
                            e.wait_ge(hf_lo, AP["kv"] + 2)
                            e.wait_ge(past_lo, 2)
                        if kind == "uq":
                            products(e, c, 0, n, QW, 3, cqhi, cqlo, k, k == 0, k == 5, N, i, 12)
                        elif kind == "uk":
                            products(e, c, 0, n, WIN, 4, lathi, latlo, k, k == 0, k == 2, KEYS, i, 12)
                        else:
                            token_products(e, c, 0, n, 4, lathi, latlo, k, k == 0, k == 2, i, 12)

                mla_pass(True)
                e.wait_ge(kr_rotated, 2)
                e.wait_ge(past_in, 48)
                with e.Fori(0, 3) as i:
                    mla_pass(False, i)
                e.wait_ge(gy_lo, 1)
                beside = [["S0"], ["S1", "T0"], ["V0", "S2", "T1"], ["V1", "S3", "T2"], ["V2", "T3", "V3"]]
                for c in range(8):
                    for part in beside[c] if c < 5 else []:
                        attend(part[0], int(part[1]), AT_MLA + 12)
                    if c == 4:
                        e.wait_ge(pv_out, AT_MLA + 16)
                    products(e, CH_GLU + c, c // 4, 2, WIN, 4, gyhi, gylo, 2 * (c % 4), c % 4 == 0, c % 4 == 3)
                e.wait_ge(hf_lo, AP["mix2"] + 8)
                acts = {"ssm": (yshi, yslo), "mla": (yahi, yalo), "mem": (ymhi, ymlo)}

                def merge_pe(c, item, i, step, g):
                    kind, b, k, half, before = item
                    if step == "tail" and k == 7:
                        e.wait_ge(half_free[1], GR_FFN2[1])
                        sums("ffn2", 4, bank=4, of=8)
                    if k == 0 or (kind == "out" and k % 2 == 0):
                        wait(e, half_free[half], g[half] + before, i, 5)
                    if kind == "gate":
                        products(e, c, half, 2, WIN, 4, hhi, hlo, 2 * k, k == 0, k == 7, N, i, 48)
                    elif kind == "branch":
                        name, nch, n, _ = BR[b]
                        if k == 0 and step == "head":
                            e.wait_ge({"ssm": ys_split, "mla": ya_split, "mem": ym_split}[name],
                                      {"ssm": 1, "mla": 2, "mem": 2}[name])
                        products(e, c, half, n, WIN, 4, *acts[name], n * k, k == 0, k == nch - 1, N, i, 48)
                    else:
                        if k < 2:
                            wait(e, m_split, k + 1 if step == "body" else 6 + k + 1, i, 2)
                        products(e, c, half, 2, WIN, 4, mhi, mlo, 2 * (k % 2), k % 2 == 0, k % 2 == 1, N, i, 48)
                merge_stream(e, merge_pe)
                ffn("ffn2", CH_FFN2, GR_FFN2)
                sums("fin", 8, first=4)

            @block.vector
            def _(e):
                links = [0, None, 0]

                def link(ins):
                    links[0] += 1
                    ins.then_inc(dve_link, 1)
                    wait(e, dve_link, links[0], links[1], links[2])

                @contextmanager
                def loop(trips, links_a_pass):
                    start = links[0]
                    with e.Fori(0, trips) as i:
                        links[1:] = [i, links_a_pass]
                        yield i
                    assert links[0] - start == links_a_pass, (links[0] - start, links_a_pass)
                    links[0] = start + trips * links_a_pass
                    links[1:] = [None, 0]

                def mean_inv(name, pairs, dim, cols=N, bank=0):
                    e.wait_ge(sq_used, SQ[name] + pairs)
                    e.tensor_scalar(mean[:, 0:cols], banks[:, bank, 0:cols], 1.0 / dim, EPS, ALU.mult,
                                    ALU.add).then_inc(mean_ready, 1)
                    e.wait_ge(mean_ready, 2 * NORM[name] + 1)
                    e.reciprocal(mean[:, 0:cols], mean[:, 0:cols]).then_inc(mean_ready, 1)

                def apply(name, src, rs, g, pairs, cols=N, out=hf):
                    for p in range(pairs):
                        if AP[name] + p >= 2 and name != "fin":
                            e.wait_ge(hf_lo, AP[name] + p - 1)
                        for q in range(2):
                            t = 2 * p + q
                            ins = e.scalar_tensor_tensor(out=out[:, p % out.shape[1], q, 0:cols], in0=src[:, t, 0:cols],
                                                         scalar=gains[:, g + t:g + t + 1], in1=rs[:, 0:cols],
                                                         op0=ALU.mult, op1=ALU.mult)
                        ins.then_inc(hf_ready, 1)

                def tt(out, a, b, op):
                    link(e.tensor_tensor(out, a, b, op))

                def ts(out, a, s1, op0, s2=None, op1=ALU.bypass):
                    link(e.tensor_scalar(out, a, s1, s2, op0, op1))

                link(e.memset(stats[:], 1.0))
                e.memset(u4[:, :, B_P:B_P + 1], 0.0)
                e.wait_ge(s5p_in, 16)
                v = [s5v[:, r] for r in range(22)]
                are, aim = s5p[:, S_ARE], s5p[:, S_AIM]
                e.wait_ge(s5_exp, 1)
                e.tensor_tensor(v[V_AR], are, v[V_DT], ALU.mult).then_inc(s5_arg, 1)
                tt(v[V_PH], aim, v[V_DT], ALU.mult)
                two_pi = 2 * np.pi
                c1 = 6.28125
                c2 = float(np.round((two_pi - c1) * 2 ** 20) / 2 ** 20)
                c3 = two_pi - c1 - c2
                for quarter, out in ((0.0, v[V_PS]), (0.25, v[V_PC])):
                    ts(v[V_K], v[V_PH], 1 / two_pi, ALU.mult, quarter, ALU.add)
                    ts(v[V_K], v[V_K], 12582912.0, ALU.add)
                    ts(v[V_K], v[V_K], 12582912.0, ALU.subtract)
                    src = v[V_PH]
                    for c in (c1, c2, c3):
                        link(e.scalar_tensor_tensor(out=out, in0=v[V_K], scalar=-c, in1=src, op0=ALU.mult, op1=ALU.add))
                        src = out
                    ts(out, out, two_pi * quarter, ALU.add)
                    ins = e.tensor_scalar(out, out, 3.1415925, -3.1415925, ALU.min, ALU.max)
                    if quarter:
                        ins.then_inc(s5_arg, 1)
                    else:
                        link(ins)
                e.wait_ge(const_in, 32)
                mean_inv("mem", 8, D, 256)
                e.wait_ge(rstd_ready, 1)
                apply("mem", memT, rstd, G_MEM, 8, 256)
                e.wait_ge(s5_sin, 2)
                tt(v[V_LRE], v[V_R], v[V_C1], ALU.mult)
                tt(v[V_LIM], v[V_R], v[V_S1], ALU.mult)
                tt(v[V_INV], are, are, ALU.mult)
                tt(v[V_T], aim, aim, ALU.mult)
                tt(v[V_INV], v[V_INV], v[V_T], ALU.add)
                link(e.reciprocal(v[V_INV], v[V_INV]))
                ts(v[V_NR], v[V_LRE], 1.0, ALU.subtract)
                for out, a, b, op in ((V_ZRE, (v[V_NR], are), (v[V_LIM], aim), ALU.add),
                                      (V_ZIM, (v[V_LIM], are), (v[V_NR], aim), ALU.subtract)):
                    tt(v[out], a[0], a[1], ALU.mult)
                    tt(v[V_T], b[0], b[1], ALU.mult)
                    tt(v[out], v[out], v[V_T], op)
                    tt(v[out], v[out], v[V_INV], ALU.mult)
                ts(v[V_NZRE], v[V_ZRE], -1.0, ALU.mult)
                ts(v[V_NLRE], v[V_LRE], -1.0, ALU.mult)
                ts(s5p[:, S_H0IM], s5p[:, S_H0IM], -1.0, ALU.mult)

                def square(c2, s2, c, s, t):
                    tt(c2, c, c, ALU.mult)
                    tt(t, s, s, ALU.mult)
                    tt(s2, c, s, ALU.mult)
                    tt(c2, c2, t, ALU.subtract)
                    ts(s2, s2, 2.0, ALU.mult)

                square(v[V_L2RE], v[V_L2IM], v[V_LRE], v[V_LIM], v[V_T])
                tt(v[V_T], v[V_R], v[V_R], ALU.mult)
                tt(v[V_R4], v[V_T], v[V_T], ALU.mult)
                square(v[V_PC], v[V_PS], v[V_C1], v[V_S1], v[V_T])
                square(uph[:, 0, 0], uph[:, 0, 1], v[V_PC], v[V_PS], v[V_T])
                for m in range(5):
                    square(uph[:, m + 1, 0], uph[:, m + 1, 1], uph[:, m, 0], uph[:, m, 1], v[V_T])
                e.memset(elh[:, :, 0, :, 0:1], 1.0)
                link(e.memset(elh[:, :, 1, :, 0:1], 0.0))
                for k in range(3):
                    n = 1 << k
                    for h in range(2):
                        ec, es = elh[:, h, 0], elh[:, h, 1]
                        uc, us = (uph[:, 3 * h + k, z].rearrange("p (t o) -> p t o", o=1).broadcast_to([P, S_TILES, n])
                                  for z in range(2))
                        tt(ec[:, :, n:2 * n], ec[:, :, 0:n], uc, ALU.mult)
                        tt(e_t[:, 0, :, 0:n], es[:, :, 0:n], us, ALU.mult)
                        tt(es[:, :, n:2 * n], ec[:, :, 0:n], us, ALU.mult)
                        tt(e_t[:, 1, :, 0:n], es[:, :, 0:n], uc, ALU.mult)
                        tt(ec[:, :, n:2 * n], ec[:, :, n:2 * n], e_t[:, 0, :, 0:n], ALU.subtract)
                        tt(es[:, :, n:2 * n], es[:, :, n:2 * n], e_t[:, 1, :, 0:n], ALU.add)
                e.wait_ge(w_used, CH_MEM + 8)
                e.tensor_copy(mkT[:, :, 0:256], banks[:, 0:4, 0:256]).then_inc(half_free[0], 1)
                e.wait_ge(x_in, 16)
                mean_inv("ffn1", 8, D, bank=7)
                e.wait_ge(rstd_ready, NORM["ffn1"] + 1)
                apply("ffn1", x, rstd, G_FFN1, 8)
                e.wait_ge(w_used, CH_MEM + 16)
                e.tensor_copy(mv[:, 0:2, :], banks[:, 4:6, :]).then_inc(half_free[1], 1)

                def add_down(half, w, scale, i=None, per=0):
                    for m in range(4):
                        ins = e.scalar_tensor_tensor(out=x[:, 4 * w + m], in0=banks[:, 4 * half + m, 0:N], scalar=scale,
                                                     in1=x[:, 4 * w + m], op0=ALU.mult, op1=ALU.add)
                    ins.then_inc(half_free[half], 1)

                def ffn(name, c0, gr, g):
                    if name == "ffn2":
                        e.wait_ge(half_free[0], gr[0])
                        e.wait_ge(half_free[1], gr[1])
                        mean_inv(name, 8, D, bank=4)
                        e.wait_ge(rstd_ready, NORM[name] + 1)
                        apply(name, x, rstd, g, 8)
                    base = 0 if name == "ffn1" else FFN_BLOCKS

                    def visit(c, kind, k, b, i, per, step):
                        body = step == "body"
                        if kind == "up" and k == 7:
                            wait(e, half_free[0], gr[0] + (2 if body else 1), i, 3)
                            wait(e, w_used, c + 1, i, per)
                            for m in range(4):
                                ins = e.tensor_tensor(prod[:, m], banks[:, 4 + m, 0:N], silu_g[:, m], ALU.mult)
                                if m == 1:
                                    ins.then_inc(prod_set, 1)
                            ins.then_inc(half_free[1], 1)
                            for r in range(2):
                                t = slice(2 * r, 2 * r + 2)
                                if r == 0:
                                    wait(e, prod_set, base + (2 if body else 1), i, 1)
                                else:
                                    wait(e, half_free[1], gr[1] + (4 if body else 1), i, 3)
                                e.tensor_copy(phi[:, t], prod[:, t]).then_inc(prod_hi, 1)
                                wait(e, prod_hi, 2 * base + (2 if body else 0) + r + 1, i, 2)
                                e.tensor_tensor(plo[:, t], prod[:, t], phi[:, t].bitcast(F32),
                                                ALU.subtract).then_inc(prod_lo, 1)
                        if kind == "down" and k % 2 == 1:
                            w = k // 2
                            half = (1, 0, 1, 0)[w] if body else (0, 1, 0, 1)[w]
                            wait(e, w_used, c + 1, i, per)
                            add_down(half, w, 0.5)
                    ffn_stream(e, c0, visit)

                ffn("ffn1", CH_FFN1, GR_FFN1, G_FFN1)
                e.wait_ge(half_free[0], GR_Z[0])
                e.wait_ge(half_free[1], GR_Z[1])
                mean_inv("mix", 8, D)
                e.wait_ge(rstd_ready, NORM["mix"] + 1)
                apply("mix", x, rstd_mix, G_MIX, 8)
                grow = lambda a, n: a.rearrange("p (i o) -> p i o", o=1).broadcast_to([P, S_IT, n])

                def powers(s):
                    own = slice(S_IT * s, S_IT * s + S_IT)
                    out = pq[s % 2]
                    e.wait_ge(s5_in[s % 2], 16 * (s // 2 + 1))
                    if s >= 2:
                        e.wait_ge(q_padded, s - 1)

                    def factor(row, step, n):
                        a = s5v[:, row:row + 2, own] if step else s5v[:, row:row + 1, own]
                        a = a.rearrange("p r (i o) -> p r i o", o=1)
                        return a.broadcast_to([P, n, S_IT, 16])

                    def four(dst, src_re, src_im, f_a, f_b, f_c, ops):
                        n = src_re.shape[1]
                        t0 = s_t[:].rearrange("p i c -> p (i c)")[:, 0:64 * n].rearrange("p (r i h) -> p r i h", i=S_IT, h=16)
                        t1 = s_t2[:].rearrange("p i c -> p (i c)")[:, 0:64 * n].rearrange("p (r i h) -> p r i h", i=S_IT, h=16)
                        e.tensor_tensor(dst[0], src_re, f_a, ALU.mult)
                        e.tensor_tensor(t0, src_im, f_b, ALU.mult)
                        e.tensor_tensor(dst[1], src_im, f_c, ALU.mult)
                        link(e.tensor_tensor(t1, src_re, f_b, ALU.mult))
                        e.tensor_tensor(dst[0], dst[0], t0, ops[0])
                        return e.tensor_tensor(dst[1], dst[1], t1, ops[1])

                    flat = lambda z, r0, r1: out[:, z, r0:r1].rearrange("p r a i h -> p (r a) i h")
                    link(four((flat(0, 0, 1), flat(1, 0, 1)), sw[s % 2][:, 0:2], sw[s % 2][:, 2:4],
                              factor(V_ZRE, 1, 2), factor(V_ZIM, 1, 2), factor(V_NZRE, 1, 2),
                              (ALU.subtract, ALU.subtract)))
                    link(four((flat(0, 1, 2), flat(1, 1, 2)), flat(0, 0, 1), flat(1, 0, 1), factor(V_LRE, 0, 2),
                              factor(V_LIM, 0, 2), factor(V_LRE, 0, 2), (ALU.add, ALU.subtract)))
                    four((flat(0, 2, 4), flat(1, 2, 4)), flat(0, 0, 2), flat(1, 0, 2), factor(V_L2RE, 0, 4),
                         factor(V_L2IM, 0, 4), factor(V_L2RE, 0, 4), (ALU.add, ALU.subtract)).then_inc(pq_ready, 1)
                    e.wait_ge(pq_ready, s + 1)

                def phases(s):
                    own = slice(S_IT * s, S_IT * s + S_IT)
                    lo = [elh[:, 0, z, own, :].rearrange("p i (o b) -> p i o b", o=1).broadcast_to([P, S_IT, 8, 8])
                          for z in range(2)]
                    hi = [elh[:, 1, z, own, :].rearrange("p i (a o) -> p i a o", o=1).broadcast_to([P, S_IT, 8, 8])
                          for z in range(2)]
                    view = lambda t: t[:, :, 0:B_P].rearrange("p i (a b) -> p i a b", a=8)
                    e.tensor_tensor(view(ee[:, 0]), lo[0], hi[0], ALU.mult)
                    e.tensor_tensor(view(s_t), lo[1], hi[1], ALU.mult)
                    e.tensor_tensor(view(ee[:, 1]), lo[0], hi[1], ALU.mult)
                    e.tensor_tensor(view(s_t2), lo[1], hi[0], ALU.mult)
                    link(e.tensor_copy(dec[:], grow(s5v[:, V_R4, own], BLKS)))
                    e.memset(dec[:, :, 0:1], 0.0)
                    e.memset(dec[:, :, B_P:B_P + 1], 0.0)
                    e.tensor_tensor(ee[:, 0, :, 0:B_P], ee[:, 0, :, 0:B_P], s_t[:, :, 0:B_P], ALU.subtract)
                    link(e.tensor_tensor(ee[:, 1, :, 0:B_P], ee[:, 1, :, 0:B_P], s_t2[:, :, 0:B_P], ALU.add))
                    for z in range(2):
                        ins = e.tensor_copy(ee[:, z, :, B_P:BLKS], ee[:, z, :, 0:B_S + 1])
                    link(ins)

                def recurrence(s):
                    own = slice(S_IT * s, S_IT * s + S_IT)
                    c, sn = ee[:, 0], ee[:, 1]
                    b_re, b_im = (banks[:, 6 + z, 0:S_IT * BLKS].rearrange("p (i n) -> p i n", i=S_IT) for z in range(2))
                    flat = lambda t: t.rearrange("p i n -> p (i n)")
                    wf = [flat(xs[:, z])[:, 0:S_IT * BLKS] for z in range(2)]
                    w_re, w_im = (a.rearrange("p (i n) -> p i n", i=S_IT) for a in wf)
                    g1 = lambda a: a.rearrange("p (i o) -> p i o", o=1)
                    e.wait_ge(bu_ready, s + 1)
                    e.tensor_tensor(w_re, b_re, c, ALU.mult)
                    e.tensor_tensor(s_t[:], b_im, sn, ALU.mult)
                    e.tensor_tensor(w_im, b_im, c, ALU.mult)
                    ins = e.tensor_tensor(s_t2[:], b_re, sn, ALU.mult)
                    ins.then_inc(bu_read, 1)
                    e.wait_ge(bu_read, s + 1)
                    e.tensor_tensor(w_re, w_re, s_t[:], ALU.subtract)
                    link(e.tensor_tensor(w_im, w_im, s_t2[:], ALU.add))
                    e.tensor_copy(w_re[:, :, B_P:B_P + 1], g1(s5p[:, S_H0RE, own]))
                    link(e.tensor_copy(w_im[:, :, B_P:B_P + 1], g1(s5p[:, S_H0IM, own])))
                    e.tensor_tensor_scan(flat(v_re), flat(dec), wf[0], 0.0, ALU.mult, ALU.add)
                    link(e.tensor_tensor_scan(flat(v_im), flat(dec), wf[1], 0.0, ALU.mult, ALU.add))
                    x_re, x_im = xs[:, 0, :, 1:BLKS + 1], xs[:, 1, :, 1:BLKS + 1]
                    e.memset(xs[:, :, :, 0:1], 0.0)
                    e.tensor_tensor(x_re, v_re[:], c, ALU.mult)
                    e.tensor_tensor(s_t[:], v_im[:], sn, ALU.mult)
                    e.tensor_tensor(x_im, v_re[:], sn, ALU.mult)
                    link(e.tensor_tensor(s_t2[:], v_im[:], c, ALU.mult))
                    e.tensor_tensor(x_re, x_re, s_t[:], ALU.add)
                    e.tensor_tensor(x_im, x_im, s_t2[:], ALU.subtract).then_inc(s5_x, 1)
                    e.wait_ge(s5_x, s + 1)
                    for k, last in enumerate((B_P, BLKS)):
                        for z in range(2):
                            e.tensor_copy(g1(states[:, 2 * k + z, own]), xs[:, z, :, last:last + 1])

                def outputs(s):
                    own = slice(S_IT * s, S_IT * s + S_IT)
                    if s >= 1:
                        e.wait_ge(gelu_ready, s)
                    link(e.tensor_tensor(s_t[:], u4[:, own, :], grow(gains[:, G_D + S_IT * s:G_D + S_IT * s + S_IT], BLKS),
                                         ALU.mult))
                    e.wait_ge(s5_y, s + 1)
                    e.tensor_tensor(ycur[:], banks[:, 4, 0:S_IT * BLKS].rearrange("p (i n) -> p i n", i=S_IT), s_t[:],
                                    ALU.add).then_inc(ycur_ready, 1)
                    e.wait_ge(ycur_ready, s + 1)

                e.wait_ge(hf_lo, AP["mix"] + 8)
                powers(0)
                powers(1)
                phases(0)
                for w in range(2):
                    e.wait_ge(w_used, CH_Z + 8 * (w + 1))
                    for a in range(S_IT):
                        for j in range(T_BLK):
                            dst = u4[32 * j:32 * j + 32, 16 * w + a:16 * w + a + 13:S_IT, :]
                            src = banks[32 * a:32 * a + 32, 4 * w:4 * w + 4, 0:N].rearrange("p m (c k) -> p m c k", k=T_BLK)
                            e.tensor_copy(dst[:, :, 0:B_P], src[:, :, 0:B_P, j])
                            ins = e.tensor_copy(dst[:, :, B_P + 1:BLKS], src[:, :, B_P:B_P + B_S, j])
                    ins.then_inc(half_free[w], 1)
                for s in range(S_STEPS):
                    recurrence(s)
                    if s + 1 < S_STEPS:
                        phases(s + 1)
                    if s + 2 < S_STEPS:
                        powers(s + 2)
                    outputs(s)

                def biggest(att, h0_, h, i=None):
                    wait(e, scores, h0_ + h + 1, i, 4)
                    for t, (q0, nq, k0, nk, bank, col) in enumerate(att["tiles"]):
                        ins = e.reduce_max(stats[0:nq, 0, t:t + 1], banks[0:nq, bank, col:col + nk], AX_X)
                    link(ins)
                    e.tensor_scalar(stats[:, 1, 0:3], stats[:, 0, 0:3], -att["scale"], None,
                                    ALU.mult).then_inc(max_ready, 1)

                def normalise(att, h0_, h, p_sb, i=None):
                    wait(e, exp_ready, h0_ + h + 1, i, 4)
                    link(e.reciprocal(stats[:, 3, 0:3], stats[:, 2, 0:3]))
                    for t, (q0, nq, k0, nk, bank, col) in enumerate(att["tiles"]):
                        a = p_sb[h % 2][0:nq, att["pcols"][t]:att["pcols"][t] + nk]
                        ins = e.tensor_scalar(a, a, stats[0:nq, 3, t:t + 1], None, ALU.mult)
                    ins.then_inc(p_ready, 1)

                def take_turned(att, h0_, h, pT, i=None):
                    wait(e, p_turned, h0_ + h + 1, i, 4)
                    for nr, a, b, bank, col in att["copies"]:
                        ins = e.tensor_copy(pT[0:nr, a:b], banks[0:nr, bank, col:col + b - a])
                    ins.then_inc(pT_ready, 1)

                def take_out(att, h0_, h, o, i=None):
                    wait(e, pv_done, h0_ + h + 1, i, 4)
                    src = banks[:, att["pv_bank"], 0:N]
                    if len(o.shape) == 3:
                        src = src.rearrange("p (o n) -> p o n", o=1)
                    e.tensor_copy(o, src).then_inc(pv_out, 1)

                def heads(att, h0_, p_sb, pT, out):
                    biggest(att, h0_, 0)
                    for h in range(4):
                        normalise(att, h0_, h, p_sb)
                        if h < 3:
                            biggest(att, h0_, h + 1)
                        take_turned(att, h0_, h, pT)
                        take_out(att, h0_, h, out(h))

                mean_inv("q", 3, Q_LORA)
                e.wait_ge(rstd_ready, NORM["q"] + 1)
                mean_inv("kv", 2, KV_LORA, bank=1)
                apply("q", cqT, rstd, G_Q, 3)
                e.wait_ge(rstd_ready, NORM["kv"] + 1)
                for p in range(2):
                    for q in range(2):
                        t = 2 * p + q
                        ins = e.scalar_tensor_tensor(out=latf[:, t], in0=ckvT[:, t], scalar=gains[:, G_KV + t:G_KV + t + 1],
                                                     in1=rstd_kv[:], op0=ALU.mult, op1=ALU.mult)
                    ins.then_inc(hf_ready, 1)
                cos, sin = const[:, C_COS:C_COS + N], const[:, C_SIN:C_SIN + N]
                tt(krot[:], krraw[:], cos, ALU.mult)
                e.wait_ge(kr_turned, 1)
                tt(mean[:], banks[:, 7, 0:N], sin, ALU.mult)
                e.tensor_tensor(krot[:], krot[:], mean[:], ALU.add).then_inc(kr_rotated, 1)
                e.wait_ge(kr_rotated, 1)
                e.memset(kr[64:128, 0, :], 0.0)
                e.memset(kr[0:64, 1, :], 0.0)
                for z in range(2):
                    r = slice(64 * z, 64 * z + 64)
                    e.tensor_copy(kr[r, z, 0:N_P], krot[r, 0:N_P])
                    ins = e.tensor_copy(kr[r, z, N_P + PAST:KEYS], krot[r, N_P:N])
                ins.then_inc(kr_rotated, 1)
                def token_order(a):
                    for j in range(T_BLK):
                        dst = u[32 * a:32 * a + 32].rearrange("p m (c k) -> p m c k", k=T_BLK)
                        src = u4[32 * j:32 * j + 32, a:a + 29:S_IT, :]
                        e.tensor_copy(dst[:, :, 0:B_P, j], src[:, :, 0:B_P])
                        ins = e.tensor_copy(dst[:, :, B_P:B_P + B_S, j], src[:, :, B_P + 1:BLKS])
                    return ins

                def take_window(group, base, i=None):
                    wait(e, w_used, CH_MLA + 12 * base + (4, 8, 10, 12)[group], i, 12)
                    if group < 2:
                        e.tensor_copy(qn[:, 2 * group:2 * group + 2, :], banks[:, 0:2, 0:N])
                        ins = e.tensor_copy(qraw[:, group], banks[:, 2, 0:N])
                    elif group == 2:
                        ins = e.tensor_copy(kn[:], banks[:, 0:4, 0:KEYS])
                    else:
                        ins = e.tensor_copy(vv[:], banks[:, 0:4, :])
                    ins.then_inc(half_free[0], 1)

                def rotate(un, base, i=None):
                    tt(qrope[:, un], qraw[:, un], cos, ALU.mult)
                    wait(e, q_turned, 2 * base + un + 1, i, 2)
                    tt(mean[:], banks[:, 5 - un, 0:N], sin, ALU.mult)
                    e.tensor_tensor(qrope[:, un], qrope[:, un], mean[:], ALU.add).then_inc(q_rotated, 1)
                    if un == 0:
                        wait(e, q_rotated, 2 * base + 1, i, 2)

                def attention_pass(att, A, p_sb, pT, out, base, i=None, between=lambda a: None):
                    biggest(att, A, 0, i)
                    normalise(att, A, 0, p_sb, i)
                    biggest(att, A, 1, i)
                    take_turned(att, A, 0, pT, i)
                    take_out(att, A, 0, out(0), i)
                    take_window(0, base, i)
                    normalise(att, A, 1, p_sb, i)
                    between(0)
                    biggest(att, A, 2, i)
                    take_turned(att, A, 1, pT, i)
                    take_out(att, A, 1, out(1), i)
                    normalise(att, A, 2, p_sb, i)
                    between(1)
                    biggest(att, A, 3, i)
                    take_turned(att, A, 2, pT, i)
                    take_window(1, base, i)
                    take_out(att, A, 2, out(2), i)
                    normalise(att, A, 3, p_sb, i)
                    between(2)
                    take_turned(att, A, 3, pT, i)
                    take_window(2, base, i)
                    take_out(att, A, 3, out(3), i)
                    between(3)
                    rotate(0, base, i)
                    rotate(1, base, i)
                    take_window(3, base, i)

                e.wait_ge(gelu_ready, S_STEPS)
                e.wait_ge(hf_lo, AP["q"] + 3)
                e.wait_ge(sq_used, SQ["kv"] + 2)

                def beside_memory(a):
                    ins = token_order(a)
                    if a == 3:
                        ins.then_inc(u_ready, 1)
                        e.wait_ge(pv_out, MEM_HEADS)
                        e.tensor_copy(ymhi[:], ymf[:]).then_inc(ym_split, 1)
                        e.wait_ge(ym_split, 1)
                        e.tensor_tensor(ymlo[:], ymf[:], ymhi[:].bitcast(F32), ALU.subtract).then_inc(ym_split, 1)
                        e.wait_ge(ym_split, 2)

                e.wait_ge(mkv_out, 32)
                attention_pass(MEM_ATT, AT_MEM, mem_p, mem_pT, lambda h: ymf[:, h, :], 0, between=beside_memory)
                with loop(3, MLA_LINKS) as i:
                    at = e.snap(i * 4)
                    attention_pass(MLA_ATT, AT_MLA, mla_p, mla_pT, lambda h: ymla[:, bass.ds(at + h, 1), :], 1, i)
                heads(MLA_ATT, AT_MLA + 12, mla_p, mla_pT, lambda h: ymla[:, 12 + h, :])
                e.wait_ge(pv_out, AT_MLA + 16)
                e.wait_ge(lat_out, 32)
                apply("mix2", x, rstd_mix, G_MIX, 8, out=hf2)
                e.wait_ge(w_used, CH_GLU + 8)
                tt(u[:], gyhi[:].bitcast(F32), gylo[:].bitcast(F32), ALU.add)
                e.wait_ge(half_free[0], GR_GLU[0] + 1)
                e.wait_ge(half_free[1], GR_GLU[1] + 1)
                tt(u[:], u[:], sgl[:], ALU.mult)
                link(e.tensor_copy(yshi[:], u[:]))
                e.tensor_tensor(yslo[:], u[:], yshi[:].bitcast(F32), ALU.subtract).then_inc(ys_split, 1)
                e.wait_ge(ys_split, 1)
                e.wait_ge(hf_lo, AP["mix2"] + 8)
                e.tensor_copy(yahi[:], ymla[:]).then_inc(ya_split, 1)
                e.wait_ge(ya_split, 1)
                e.tensor_tensor(yalo[:], ymla[:], yahi[:].bitcast(F32), ALU.subtract).then_inc(ya_split, 1)
                def merge_dve(c, item, i, step, g):
                    kind, b, k, half, before = item
                    if kind == "branch" and k == BR[b][1] - 1:
                        gates = [it[4] for it in merge_order(step) if it[0] == "gate" and it[1] == b][0] + 1
                        wait(e, half_free[0], g[0] + gates, i, 5)
                        wait(e, w_used, c + 1, i, 48)
                        dst = merged if b == 0 else gate
                        for m in range(4):
                            ins = e.tensor_tensor(dst[:, m], banks[:, 4 + m, 0:N], gate[:, m], ALU.mult)
                        if b:
                            link(ins)
                        if b == 1:
                            ins = e.tensor_tensor(merged[:], merged[:], gate[:], ALU.add)
                        two = [slice(0, 2), slice(2, 4)]
                        if b == 2:
                            link(e.tensor_tensor(merged[:, two[0]], merged[:, two[0]], gate[:, two[0]], ALU.add))
                            ins = e.tensor_tensor(merged[:, two[1]], merged[:, two[1]], gate[:, two[1]], ALU.add)
                        ins.then_inc(half_free[1], 1)
                        if b < 2:
                            wait(e, half_free[1], g[1] + before + 1, i, 5)
                        else:
                            for r, t in enumerate(two):
                                if r == 1:
                                    wait(e, half_free[1], g[1] + before + 1, i, 5)
                                link(e.tensor_copy(mhi[:, t], merged[:, t]))
                                e.tensor_tensor(mlo[:, t], merged[:, t], mhi[:, t].bitcast(F32),
                                                ALU.subtract).then_inc(m_split, 1)
                            wait(e, m_split, 4 if i is not None else 2, i, 2)
                    if kind == "out" and k % 2 == 1:
                        wait(e, w_used, c + 1, i, 48)
                        add_down(half, k // 2, 1.0)
                merge_stream(e, merge_dve, lambda: loop(3, MERGE_LINKS))
                ffn("ffn2", CH_FFN2, GR_FFN2, G_FFN2)
                e.wait_ge(half_free[0], GR_END[0])
                e.wait_ge(half_free[1], GR_END[1])
                mean_inv("fin", 8, D)
                e.wait_ge(rstd_ready, NORM["fin"] + 1)
                apply("fin", x, rstd, G_FIN, 8, out=y)


_OUT = {"yT": (D, N), "latT": (KV_LORA, N), "krT": (ROPE, N), "mkT": (MEM_W, 256), "mv": (256, MEM_W),
        "states": (P, 4, S_TILES)}


def _constants():
    c = np.zeros((P, C_COLS), np.float32)
    c[:, C_ID:C_ID + P] = np.eye(P, dtype=np.float32)
    for b in (0, 64):
        for r in range(32):
            c[b + 32 + r, C_PERM + b + r] = -1.0
            c[b + r, C_PERM + b + 32 + r] = 1.0
    half = ROPE // 2
    inv = np.float32(10000.0) ** (-np.arange(half, dtype=np.float32) / np.float32(half))
    pos = np.concatenate([np.arange(N_P), PAST + np.arange(N_S)]).astype(np.float32)
    ang = (inv[:, None] * pos[None, :]).astype(np.float32)
    c[:, C_COS:C_COS + N] = np.tile(np.cos(ang), (4, 1))
    c[:, C_SIN:C_SIN + N] = np.tile(np.sin(ang), (4, 1))
    c[0, C_HALF:C_HALF + 64] = 1.0
    c[0, C_MASK + 192:C_MASK + 256] = -1e30
    return c


def kernel(**inp):
    import concourse.bacc as bacc
    from concourse.bass_utils import run_bass_kernel_spmd as run
    a = {k: np.asarray(v) for k, v in inp.items()}
    col = lambda v: v.reshape(-1, P)
    d4 = np.tile(a["ssm_d"].reshape(S_TILES, 32), (1, T_BLK))
    gains = np.concatenate([col(a["ffn1_norm"]), col(a["mix_norm"]), col(a["ffn2_norm"]), col(a["final_norm"]),
                            col(a["mem_norm"]), col(a["q_norm"]), col(a["kv_norm"]), col(a["ssm_b_glu"]),
                            d4]).T
    modes = lambda v: v.reshape(S_TILES, P).T
    ldt = np.repeat(a["ssm_log_dt"][0], 64)
    s5p = np.stack([modes(a["ssm_a_re"]), modes(a["ssm_a_im"]), modes(ldt), modes(a["state_ssm_re"]),
                    modes(a["state_ssm_im"])], axis=1)

    def steps(v):
        return v.reshape(S_TILES, P, 16).transpose(1, 0, 2).reshape(P, S_STEPS, S_IT, 16)

    def apart(v):
        out = np.zeros((2, 64, S_STEPS, S_IT, 2, 16), np.float32)
        w = v.reshape(S_STEPS, S_IT, 2, 64, 16)
        for g in range(2):
            out[g, :, :, :, g] = w[:, :, g].transpose(2, 0, 1, 3)
        return out.reshape(P, S_STEPS, 2, S_IT, 16)

    b_re, b_im = a["ssm_b_re"][0], a["ssm_b_im"][0]
    c_re, c_im = a["ssm_c_re"][0].transpose(0, 2, 1), a["ssm_c_im"][0].transpose(0, 2, 1)
    s5w = np.concatenate([np.stack([steps(v) for v in (b_re, c_re, b_im, c_im)], axis=2), apart(c_re), apart(c_im)],
                         axis=2)
    w_in = a["w_in"][0]
    arrays = {
        "const": _constants(), "gains": gains, "s5p": s5p,
        "xT": np.concatenate([a["x_prompt"][0], a["x_sample"][0]]).T,
        "memT": a["mem_prompt"][0].T,
        "cmkT": a["cache_mem_k"].reshape(256, MEM_W).T, "cmv": a["cache_mem_v"].reshape(256, MEM_W),
        "platT": a["cache_kv_latent"][0, 0].T, "pkrT": a["cache_k_rope"][0, 0].T,
        "s5w": s5w,
        "w_in": w_in, "w_kr2": np.concatenate([w_in[:, COL_KR:COL_QM]] * 2, axis=1),
    }
    arrays["w_post"] = np.concatenate([a[n][0] for n in ("w_out", "w_br_ssm", "w_br_mla", "w_br_mem")])
    uq = a["w_uq"][0].reshape(Q_LORA, HEADS // 2, 2, NOPE + ROPE)
    arrays["w_uq"] = np.concatenate([uq[..., :NOPE].reshape(Q_LORA, HEADS // 2, 2 * NOPE),
                                     uq[..., NOPE:].reshape(Q_LORA, HEADS // 2, 2 * ROPE)], axis=2).reshape(Q_LORA, -1)
    for name in ("w_mem_k", "w_mem_v", "ffn1_w_gate", "ffn1_w_up", "ffn1_w_down", "w_uk", "w_uv", "ssm_w_glu",
                 "ffn2_w_gate", "ffn2_w_up", "ffn2_w_down"):
        arrays[name] = a[name][0]
    nc = bacc.Bacc("TRN2", target_bir_lowering=False, num_devices=1)
    t_in, feed = {}, {}
    for name, v in arrays.items():
        feed["i_" + name] = np.ascontiguousarray(v)
        t_in[name] = nc.dram_tensor("i_" + name, v.shape, F32, kind="ExternalInput").ap()
    t_out = {n: nc.dram_tensor("o_" + n, s, F32, kind="ExternalOutput").ap() for n, s in _OUT.items()}
    build(nc, t_in, t_out)
    r = run(nc, [feed], core_ids=[0]).results[0]
    y, lat, kr = (np.asarray(r["o_" + n]).T for n in ("yT", "latT", "krT"))
    st = np.asarray(r["o_states"]).transpose(1, 2, 0).reshape(4, 1, 1, 64, 64)
    cut = lambda v: (v[None, :N_P], v[None, N_P:])
    (y_p, y_s), (l_p, l_s), (k_p, k_s) = cut(y), cut(lat), cut(kr)
    mk = np.asarray(r["o_mkT"]).T.reshape(1, 1, 256, MEM_HEADS, HD)
    mv = np.asarray(r["o_mv"]).reshape(1, 1, 256, MEM_HEADS, HD)
    return tuple(np.ascontiguousarray(v) for v in (
        y_p, y_s, l_p[None], k_p[None], mk, mv, st[0], st[1], l_s[None], k_s[None], st[2], st[3]))
```
